# Optimizing a Trainium2 kernel written in Bass

```python
import math
import jax, jax.numpy as jnp
from jax import lax
import numpy as np

D_MODEL = 1024
BATCH = 1
SEQ = 1024
DEPTH = 1

MLA_HEADS = 8
Q_LORA_RANK = 256
KV_LORA_RANK = 128
QK_NOPE_DIM = 64
QK_ROPE_DIM = 32
V_HEAD_DIM = 64
ROPE_THETA = 10000.0
Q_BLOCK = 128
SSM_GROUP = 16
SSM_GROUPS = 32
SSM_WIDTH = SSM_GROUP * SSM_GROUPS
SSM_STATE = 64
DT_MIN = 0.001
DT_MAX = 0.1
D_FF = 2816
FFN_RES = 0.5
EPS = 1e-6
N_BRANCH = 2
MAX_POS_OFFSET = 4096

OFF_CQ = 0
OFF_CKV = OFF_CQ + Q_LORA_RANK
OFF_KR = OFF_CKV + KV_LORA_RANK
OFF_U = OFF_KR + QK_ROPE_DIM
OFF_GA = OFF_U + SSM_WIDTH
OFF_GS = OFF_GA + D_MODEL
IN_PROJ = OFF_GS + D_MODEL

kernel_name = "hybrid_mla_s5_macaron_encoder"

def _rmsnorm(x, g):
    x32 = x.astype(jnp.float32)
    y = x32 * lax.rsqrt(jnp.mean(x32 * x32, axis=-1, keepdims=True) + EPS)
    return (y * g.astype(jnp.float32)).astype(x.dtype)

def _swiglu(x, w_gate, w_up, w_down):
    return (jax.nn.silu(x @ w_gate) * (x @ w_up)) @ w_down

def _rope_tables(positions):
    inv_freq = ROPE_THETA ** (-jnp.arange(0, QK_ROPE_DIM, 2, dtype=jnp.float32) / QK_ROPE_DIM)
    ang = positions.astype(jnp.float32)[..., None] * inv_freq
    return jnp.cos(ang), jnp.sin(ang)

def _apply_rope(t, cos, sin):
    half = t.shape[-1] // 2
    cos = cos.astype(t.dtype)
    sin = sin.astype(t.dtype)
    t1, t2 = t[..., :half], t[..., half:]
    return jnp.concatenate([t1 * cos - t2 * sin, t2 * cos + t1 * sin], axis=-1)

def _mla_attention(q_nope, q_rope, k_nope, k_rope, v):
    b, s, h, _ = q_nope.shape
    dv = v.shape[-1]
    n_blk = s // Q_BLOCK
    scale = (QK_NOPE_DIM + QK_ROPE_DIM) ** -0.5

    def blocks(t):
        return t.reshape((b, n_blk, Q_BLOCK) + t.shape[2:]).swapaxes(0, 1)

    def attend(qs):
        qn, qr = qs
        sc = (jnp.einsum('bqhd,bkhd->bhqk', qn, k_nope)
              + jnp.einsum('bqhr,bkr->bhqk', qr, k_rope))
        p = jax.nn.softmax(sc.astype(jnp.float32) * scale, axis=-1).astype(v.dtype)
        return jnp.einsum('bhqk,bkhd->bqhd', p, v)

    o = lax.map(attend, (blocks(q_nope), blocks(q_rope)))
    return o.swapaxes(0, 1).reshape(b, s, h * dv)

def _ssm_direction(u, lam_re, lam_im, log_dt, b_re, b_im, c_re, c_im, reverse):
    dt = jnp.exp(log_dt)[:, None]
    mag = jnp.exp(lam_re * dt)
    lb_re = mag * jnp.cos(lam_im * dt)
    lb_im = mag * jnp.sin(lam_im * dt)
    den = lam_re * lam_re + lam_im * lam_im
    nr = lb_re - 1.0
    k_re = (nr * lam_re + lb_im * lam_im) / den
    k_im = (lb_im * lam_re - nr * lam_im) / den
    bb_re = k_re[..., None] * b_re - k_im[..., None] * b_im
    bb_im = k_re[..., None] * b_im + k_im[..., None] * b_re
    x_re = jnp.einsum('sbgi,gpi->sbgp', u, bb_re)
    x_im = jnp.einsum('sbgi,gpi->sbgp', u, bb_im)
    seq = u.shape[0]
    a_re = jnp.broadcast_to(lb_re, (seq, 1) + lb_re.shape)
    a_im = jnp.broadcast_to(lb_im, (seq, 1) + lb_im.shape)

    def combine(e1, e2):
        ar1, ai1, xr1, xi1 = e1
        ar2, ai2, xr2, xi2 = e2
        ar = ar2 * ar1 - ai2 * ai1
        ai = ar2 * ai1 + ai2 * ar1
        xr = ar2 * xr1 - ai2 * xi1 + xr2
        xi = ar2 * xi1 + ai2 * xr1 + xi2
        return (ar, ai, xr, xi)

    _, _, h_re, h_im = lax.associative_scan(combine, (a_re, a_im, x_re, x_im),
                                            reverse=reverse, axis=0)
    return (jnp.einsum('sbgp,gip->sbgi', h_re, c_re)
            - jnp.einsum('sbgp,gip->sbgi', h_im, c_im))

def setup_inputs(seed: int = 0) -> dict:
    key = jax.random.key(seed)
    ks = iter(jax.random.split(key, 48))
    f32 = jnp.float32

    def nrm(shape, fan_in):
        return jax.random.normal(next(ks), shape, f32) * (fan_in ** -0.5)

    def gain(shape):
        return 1.0 + 0.02 * jax.random.normal(next(ks), shape, f32)

    L, D, G, P, I = DEPTH, D_MODEL, SSM_GROUPS, SSM_STATE, SSM_GROUP
    x = jax.random.normal(next(ks), (BATCH, SEQ, D), f32)
    offset = jax.random.randint(next(ks), (BATCH, 1), 0, MAX_POS_OFFSET, dtype=jnp.int32)
    positions = (jnp.arange(SEQ, dtype=jnp.int32)[None, :] + offset).astype(jnp.int32)

    n_idx = jnp.arange(P, dtype=f32)
    lam_re = -0.5 + 0.01 * jax.random.normal(next(ks), (L, 2, G, P), f32)
    lam_im = jnp.pi * n_idx + 0.01 * jax.random.normal(next(ks), (L, 2, G, P), f32)
    log_dt = jax.random.uniform(next(ks), (L, 2, G), f32,
                                minval=math.log(DT_MIN), maxval=math.log(DT_MAX))

    return {
        "x": x,
        "positions": positions,
        "ffn1_norm": gain((L, D)),
        "ffn1_w_gate": nrm((L, D, D_FF), D),
        "ffn1_w_up": nrm((L, D, D_FF), D),
        "ffn1_w_down": nrm((L, D_FF, D), D_FF),
        "mix_norm": gain((L, D)),
        "w_in": nrm((L, D, IN_PROJ), D),
        "q_norm": gain((L, Q_LORA_RANK)),
        "w_uq": nrm((L, Q_LORA_RANK, MLA_HEADS * (QK_NOPE_DIM + QK_ROPE_DIM)), Q_LORA_RANK),
        "kv_norm": gain((L, KV_LORA_RANK)),
        "w_ukv": nrm((L, KV_LORA_RANK, MLA_HEADS * (QK_NOPE_DIM + V_HEAD_DIM)), KV_LORA_RANK),
        "w_o_attn": nrm((L, MLA_HEADS * V_HEAD_DIM, D), MLA_HEADS * V_HEAD_DIM),
        "ssm_lambda_re": lam_re,
        "ssm_lambda_im": lam_im,
        "ssm_log_dt": log_dt,
        "ssm_b_re": nrm((L, 2, G, P, I), 2 * I),
        "ssm_b_im": nrm((L, 2, G, P, I), 2 * I),
        "ssm_c_re": nrm((L, 2, G, I, P), 2 * P),
        "ssm_c_im": nrm((L, 2, G, I, P), 2 * P),
        "ssm_d": jax.random.normal(next(ks), (L, SSM_WIDTH), f32),
        "w_glu": nrm((L, SSM_WIDTH, 2 * SSM_WIDTH), SSM_WIDTH),
        "b_glu": 0.01 * jax.random.normal(next(ks), (L, 2 * SSM_WIDTH), f32),
        "w_o_ssm": nrm((L, SSM_WIDTH, D), SSM_WIDTH),
        "w_out": nrm((L, D, D), D),
        "ffn2_norm": gain((L, D)),
        "ffn2_w_gate": nrm((L, D, D_FF), D),
        "ffn2_w_up": nrm((L, D, D_FF), D),
        "ffn2_w_down": nrm((L, D_FF, D), D_FF),
        "final_norm": gain((D,)),
    }

def reference(x, positions, ffn1_norm, ffn1_w_gate, ffn1_w_up, ffn1_w_down, mix_norm, w_in,
              q_norm, w_uq, kv_norm, w_ukv, w_o_attn, ssm_lambda_re, ssm_lambda_im,
              ssm_log_dt, ssm_b_re, ssm_b_im, ssm_c_re, ssm_c_im, ssm_d, w_glu, b_glu,
              w_o_ssm, w_out, ffn2_norm, ffn2_w_gate, ffn2_w_up, ffn2_w_down, final_norm):
    b, s, _ = x.shape
    f32 = jnp.float32
    cos, sin = _rope_tables(positions)
    h = x
    for l in range(DEPTH):
        h = h + FFN_RES * _swiglu(_rmsnorm(h, ffn1_norm[l]), ffn1_w_gate[l], ffn1_w_up[l], ffn1_w_down[l])

        n = _rmsnorm(h, mix_norm[l])
        z = n @ w_in[l]
        c_q = z[..., OFF_CQ:OFF_CKV]
        c_kv = z[..., OFF_CKV:OFF_KR]
        k_r = z[..., OFF_KR:OFF_U]
        u = z[..., OFF_U:OFF_GA]
        g_attn = z[..., OFF_GA:OFF_GS]
        g_ssm = z[..., OFF_GS:IN_PROJ]

        q = (_rmsnorm(c_q, q_norm[l]) @ w_uq[l]).reshape(b, s, MLA_HEADS, QK_NOPE_DIM + QK_ROPE_DIM)
        q_nope = q[..., :QK_NOPE_DIM]
        q_rope = _apply_rope(q[..., QK_NOPE_DIM:], cos[:, :, None, :], sin[:, :, None, :])
        kv = (_rmsnorm(c_kv, kv_norm[l]) @ w_ukv[l]).reshape(b, s, MLA_HEADS, QK_NOPE_DIM + V_HEAD_DIM)
        k_nope = kv[..., :QK_NOPE_DIM]
        v = kv[..., QK_NOPE_DIM:]
        k_rope = _apply_rope(k_r, cos, sin)
        attn = _mla_attention(q_nope, q_rope, k_nope, k_rope, v)

        u32 = u.astype(f32)
        ug = u32.reshape(b, s, SSM_GROUPS, SSM_GROUP).swapaxes(0, 1)
        y_dirs = []
        for direction, rev in ((0, False), (1, True)):
            y_dirs.append(_ssm_direction(
                ug,
                ssm_lambda_re[l, direction].astype(f32), ssm_lambda_im[l, direction].astype(f32),
                ssm_log_dt[l, direction].astype(f32),
                ssm_b_re[l, direction].astype(f32), ssm_b_im[l, direction].astype(f32),
                ssm_c_re[l, direction].astype(f32), ssm_c_im[l, direction].astype(f32),
                rev))
        y_ssm = (y_dirs[0] + y_dirs[1]).swapaxes(0, 1).reshape(b, s, SSM_WIDTH)
        y_ssm = (y_ssm + ssm_d[l].astype(f32) * u32).astype(x.dtype)
        glu = jax.nn.gelu(y_ssm) @ w_glu[l] + b_glu[l]
        ssm_out = glu[..., :SSM_WIDTH] * jax.nn.sigmoid(glu[..., SSM_WIDTH:])

        merged = (jax.nn.sigmoid(g_attn) * (attn @ w_o_attn[l])
                  + jax.nn.sigmoid(g_ssm) * (ssm_out @ w_o_ssm[l]))
        h = h + merged @ w_out[l]

        h = h + FFN_RES * _swiglu(_rmsnorm(h, ffn2_norm[l]), ffn2_w_gate[l], ffn2_w_up[l], ffn2_w_down[l])
    return _rmsnorm(h, final_norm)


_drawn_inputs = setup_inputs


def setup_inputs(seed=0):
    import zlib

    import numpy as np

    out = dict(_drawn_inputs(seed))
    spreads = {}
    factors = {'ffn1_norm': 6.291,
     'mix_norm': 8.0,
     'q_norm': 8.0,
     'kv_norm': 8.0,
     'ssm_lambda_re': 64.0,
     'ssm_lambda_im': 29.856,
     'ssm_log_dt': 31.008,
     'ssm_b_re': 42.208,
     'ssm_b_im': 42.56,
     'ssm_c_re': 42.592,
     'ssm_c_im': 42.304,
     'b_glu': 64.0,
     'ffn2_norm': 7.173,
     'final_norm': 8.581}
    for name, (base, spread) in spreads.items():
        noise = np.random.default_rng([zlib.crc32(name.encode()), seed]).standard_normal(out[name].shape)
        drawn = base * np.exp(spread * noise) if base else spread * noise
        out[name] = __import__('jax').numpy.asarray(drawn.astype(out[name].dtype))
    for name, factor in factors.items():
        out[name] = (out[name] * factor).astype(out[name].dtype)
    return out
```

```python
import math
from contextlib import ExitStack

import numpy as np
import concourse.bass as bass
from concourse import mybir

F32 = mybir.dt.float32
F32R = mybir.dt.float32r
I32 = mybir.dt.int32
ALU = mybir.AluOpType
ACT = mybir.ActivationFunctionType
AX = mybir.AxisListType


def two_pi_parts():
    rest, parts = 2 * math.pi, []
    for _ in range(3):
        unit = 2.0 ** (math.floor(math.log2(rest)) - 7)
        parts.append(math.floor(rest / unit) * unit)
        rest -= parts[-1]
    return parts + [float(np.float32(rest))]


P = 128
SEQ = 1024
D = 1024
F = 2816
ST = SEQ // P
KT = D // P
HALF = 512
EPS = 1e-6
ROUND = 1.5 * 2.0 ** 23
TWO_PI_PARTS = two_pi_parts()
PI_DOWN = 3.1415925


def three_passes(pe, out, lhs_hi, lhs_lo, rhs_hi, rhs_lo, first, last):
    pe.matmul(out, lhs_hi, rhs_hi, start=first, stop=False)
    pe.matmul(out, lhs_hi, rhs_lo, start=False, stop=False)
    return pe.matmul(out, lhs_lo, rhs_hi, start=False, stop=last)


class Phase(ExitStack):

    def __init__(self, nc):
        super().__init__()
        self.taken = []

        def clear():
            if self.taken:
                nc.clear_and_free_semaphores(self.taken)
                nc.all_engine_barrier()
        self.callback(clear)


def semaphores(nc, ctx, tag):
    def sem(name):
        ctx.taken.append(nc.alloc_semaphore(f"{tag}_{name}"))
        return ctx.taken[-1]
    return sem


class Chain:

    def __init__(self, eng, s, n=0):
        self.eng, self.s, self.n = eng, s, n

    def __call__(self, ins):
        self.n += 1
        ins.then_inc(self.s, 1)
        self.eng.wait_ge(self.s, self.n)


def newton(link, var, root, out, tmp):
    dve = link.eng
    link(dve.reciprocal(out, root))
    link(dve.tensor_tensor(tmp, out, out, ALU.mult))
    link(dve.tensor_tensor(tmp, tmp, var, ALU.mult))
    link(dve.tensor_scalar(tmp, tmp, -0.5, 1.5, ALU.mult, ALU.add))
    link(dve.tensor_tensor(out, out, tmp, ALU.mult))


def reduce_angle(link, ang, turns, tmp, quarter):
    dve = link.eng
    link(dve.tensor_scalar(turns, ang, 1.0 / (2 * math.pi), quarter, ALU.mult, ALU.add))
    link(dve.tensor_scalar(turns, turns, ROUND, None, ALU.add))
    link(dve.tensor_scalar(turns, turns, ROUND, None, ALU.subtract))
    for part in TWO_PI_PARTS:
        link(dve.scalar_tensor_tensor(out=ang, in0=turns, scalar=-part, in1=ang, op0=ALU.mult, op1=ALU.add))
    if quarter:
        link(dve.tensor_scalar(ang, ang, math.pi / 2, None, ALU.add))
    link(dve.tensor_scalar(ang, ang, PI_DOWN, -PI_DOWN, ALU.min, ALU.max))


class ColumnProduct:

    def __init__(self, nc, ctx, tag, w, tiles, rhs_hi, rhs_lo, psum, slot0=0):
        sb = lambda n, s, d=F32: ctx.enter_context(nc.sbuf_tensor(f"{tag}_{n}", s, d))
        sem = semaphores(nc, ctx, tag)
        self.K = w.shape[0] // P
        self.w, self.tiles, self.N = w.rearrange("(k p) f -> p k f", p=P), tiles, len(tiles)
        self.rhs_hi, self.rhs_lo = rhs_hi, rhs_lo
        self.raw = [sb(f"raw{i}", [P, self.K, P]) for i in range(2)]
        self.hi = sb("hi", [P, 2, self.K, P], F32R)
        self.lo = sb("lo", [P, 2, self.K, P], F32R)
        self.ps = [psum[:, slot0 + 2 * i:slot0 + 2 * i + 2, :] for i in range(2)]
        self.raw_in = [sem(f"raw_in{i}") for i in range(2)]
        self.hi_done, self.lo_done, self.mm_done = sem("hi_done"), sem("lo_done"), sem("mm_done")
        self.read = [sem(f"read{i}") for i in range(2)]

    def load(self, sp, n):
        if n >= 2:
            sp.wait_ge(self.lo_done, n - 1)
        sp.dma_start(self.raw[n % 2][:], self.w[:, :, self.tiles[n]:self.tiles[n] + P]).then_inc(self.raw_in[n % 2], 16)

    def high(self, act, n):
        if n >= self.N:
            return
        act.wait_ge(self.raw_in[n % 2], 16 * (n // 2 + 1))
        if n >= 2:
            act.wait_ge(self.mm_done, n - 1)
        act.copy(self.hi[:, n % 2], self.raw[n % 2][:]).then_inc(self.hi_done, 1)

    def low(self, dve, n):
        if n >= self.N:
            return
        dve.wait_ge(self.hi_done, n + 1)
        if n >= 2:
            dve.wait_ge(self.mm_done, n - 1)
        dve.tensor_tensor(self.lo[:, n % 2], self.raw[n % 2][:], self.hi[:, n % 2].bitcast(F32), ALU.subtract).then_inc(self.lo_done, 1)

    def product(self, pe, n):
        pe.wait_ge(self.lo_done, n + 1)
        if n >= 2:
            pe.wait_ge(self.read[n % 2], n // 2)
        for half in range(2):
            sl = slice(half * HALF, (half + 1) * HALF)
            for k in range(self.K):
                mm = three_passes(pe, self.ps[n % 2][:, half, :], self.hi[:, n % 2, k, :], self.lo[:, n % 2, k, :],
                                  self.rhs_hi[:, k, sl], self.rhs_lo[:, k, sl], k == 0, k == self.K - 1)
        mm.then_inc(self.mm_done, 1)


class RowProduct:

    def __init__(self, nc, ctx, tag, jobs, lhs, psum):
        sb = lambda n, s, d=F32: ctx.enter_context(nc.sbuf_tensor(f"{tag}_{n}", s, d))
        sem = semaphores(nc, ctx, tag)
        self.jobs, self.lhs, self.psum = jobs, lhs, psum
        self.raw = [sb(f"raw{i}", [P, HALF]) for i in range(2)]
        self.hi = sb("hi", [P, 2, HALF], F32R)
        self.lo = sb("lo", [P, 2, HALF], F32R)
        self.raw_in = [sem(f"raw_in{i}") for i in range(2)]
        self.hi_done, self.lo_done, self.k_done, self.mm_done, self.read = (sem(n) for n in ("hi_done", "lo_done", "k_done", "mm_done", "read"))

    def units(self):
        return [(j, k) for j in range(len(self.jobs)) for k in range(self.jobs[j][0].shape[0] // P)]

    def load(self, sp, n):
        units = self.units()
        w, parts, width = self.jobs[units[n][0]]
        k = units[n][1]
        if n >= 2:
            sp.wait_ge(self.lo_done, n - 1)
        for at, cols in parts:
            sp.dma_start(self.raw[n % 2][:, at:at + cols.stop - cols.start], w[k * P:(k + 1) * P, cols]).then_inc(self.raw_in[n % 2], 16)

    def arrived(self, n):
        units = self.units()
        return sum(16 * len(self.jobs[units[i][0]][1]) for i in range(n % 2, n + 1, 2))

    def high(self, act, n):
        units = self.units()
        if n >= len(units):
            return
        width = self.jobs[units[n][0]][2]
        act.wait_ge(self.raw_in[n % 2], self.arrived(n))
        if n >= 2:
            act.wait_ge(self.k_done, n - 1)
        act.copy(self.hi[:, n % 2, 0:width], self.raw[n % 2][:, 0:width]).then_inc(self.hi_done, 1)

    def low(self, eng, n):
        units = self.units()
        if n >= len(units):
            return
        width = self.jobs[units[n][0]][2]
        eng.wait_ge(self.hi_done, n + 1)
        if n >= 2:
            eng.wait_ge(self.k_done, n - 1)
        eng.tensor_tensor(self.lo[:, n % 2, 0:width], self.raw[n % 2][:, 0:width], self.hi[:, n % 2, 0:width].bitcast(F32), ALU.subtract).then_inc(self.lo_done, 1)

    def products(self, pe, only=None):
        units = self.units()
        for n, (j, k) in enumerate(units):
            if only is not None and j != only:
                continue
            w, parts, width = self.jobs[j]
            last = k == w.shape[0] // P - 1
            pe.wait_ge(self.lo_done, n + 1)
            for m in range(ST):
                if k == 0 and j:
                    pe.wait_ge(self.read, (j - 1) * ST + m + 1)
                hi, lo = self.lhs(j, k, m)
                mm = three_passes(pe, self.psum[:, m, 0:width], hi, lo, self.hi[:, n % 2, 0:width], self.lo[:, n % 2, 0:width], k == 0, last)
                if m == ST - 1:
                    mm.then_inc(self.k_done, 1)
                elif last:
                    mm.then_inc(self.mm_done, 1)

    def wait_bank(self, eng, j, m):
        if m < ST - 1:
            eng.wait_ge(self.mm_done, j * (ST - 1) + m + 1)
        else:
            eng.wait_ge(self.k_done, sum(1 for u in self.units() if u[0] <= j))


class Norm:

    def __init__(self, nc, ctx, tag, gain, rows, ident, nT_hi, nT_lo, psum):
        sb = lambda n, s, d=F32: ctx.enter_context(nc.sbuf_tensor(f"{tag}_{n}", s, d))
        sem = semaphores(nc, ctx, tag)
        self.gain, self.rows, self.ident = gain, rows, ident
        self.hi, self.lo, self.psum = nT_hi, nT_lo, psum
        self.gb = sb("gb", [P, D])
        self.xn = sb("xn", [P, 2, D])
        self.stat = sb("stat", [P, 5, ST])
        self.s_gain, self.s_sq, self.s_var, self.s_sqrt, self.s_rstd = map(sem, ("gain", "sq", "var", "sqrt", "rstd"))
        self.s_xn, self.s_tr, self.s_hi, self.s_lo = map(sem, ("xn", "tr", "nhi", "nlo"))

    def load(self, sp):
        sp.dma_start(self.gb[:], self.gain.rearrange("(a d) -> a d", a=1).broadcast_to([P, D])).then_inc(self.s_gain, 16)

    def act_squares(self, act, rows_ready):
        for m in range(ST):
            rows_ready(act, m)
            if m >= 4:
                act.wait_ge(self.s_sq, m - 3)
            act.activation(self.psum[:, 2 * (m % 4):2 * (m % 4) + 2, :], self.rows[:, m, :].rearrange("p (a b) -> p a b", a=2), ACT.Square,
                           accum_out=self.stat[:, 0, m:m + 1]).then_inc(self.s_sq, 1)
        act.wait_ge(self.s_var, 1)
        act.activation(self.stat[:, 2, :], self.stat[:, 1, :], ACT.Sqrt).then_inc(self.s_sqrt, 1)

    def dve_rstd(self, dve):
        st, s = self.stat, self.s_rstd
        dve.wait_ge(self.s_sq, ST)
        dve.tensor_scalar(st[:, 1, :], st[:, 0, :], 1.0 / D, EPS, ALU.mult, ALU.add).then_inc(self.s_var, 1)
        dve.wait_ge(self.s_sqrt, 1)
        newton(Chain(dve, s), st[:, 1, :], st[:, 2, :], st[:, 3, :], st[:, 4, :])

    def dve_rows(self, dve, m):
        if m == 0:
            dve.wait_ge(self.s_gain, 16)
        if m >= 2:
            dve.wait_ge(self.s_tr, m - 1)
        dve.scalar_tensor_tensor(out=self.xn[:, m % 2, :], in0=self.rows[:, m, :], scalar=self.stat[:, 3, m:m + 1],
                                 in1=self.gb[:], op0=ALU.mult, op1=ALU.mult).then_inc(self.s_xn, 1)

    def dve_low(self, dve, m):
        sl = slice(m * P, (m + 1) * P)
        dve.wait_ge(self.s_hi, m + 1)
        ps = self.psum[:, 2 * (m % 4):2 * (m % 4) + 2, :].rearrange("p a (k s) -> p (a k) s", s=P)
        dve.tensor_tensor(self.lo[:, :, sl], ps, self.hi[:, :, sl].bitcast(F32), ALU.subtract).then_inc(self.s_lo, 1)

    def dve(self, dve):
        self.dve_rstd(dve)
        self.dve_rows(dve, 0)
        for m in range(ST):
            if m + 1 < ST:
                self.dve_rows(dve, m + 1)
            self.dve_low(dve, m)

    def act_high(self, act):
        for m in range(ST):
            act.wait_ge(self.s_tr, m + 1)
            ps = self.psum[:, 2 * (m % 4):2 * (m % 4) + 2, :].rearrange("p a (k s) -> p (a k) s", s=P)
            act.copy(self.hi[:, :, m * P:(m + 1) * P], ps).then_inc(self.s_hi, 1)

    def pe(self, pe):
        pe.wait_ge(self.s_sqrt, 1)
        for m in range(ST):
            pe.wait_ge(self.s_xn, m + 1)
            if m >= 4:
                pe.wait_ge(self.s_lo, m - 3)
            for k in range(KT):
                t = pe.transpose(self.psum[:, 2 * (m % 4) + k // 4, (k % 4) * P:(k % 4 + 1) * P],
                                 self.xn[:, m % 2, k * P:(k + 1) * P], self.ident[:])
            t.then_inc(self.s_tr, 1)


def ffn_phase(nc, tag, gain, w_gate, w_up, w_down, rows, ident, psum, x=None, finish=None):
    NP = F // (2 * P)
    with Phase(nc) as ctx:
        sb = lambda n, s, d=F32: ctx.enter_context(nc.sbuf_tensor(f"{tag}_{n}", s, d))
        sem = semaphores(nc, ctx, tag)
        nT_hi = sb("nT_hi", [P, KT, SEQ], F32R)
        nT_lo = sb("nT_lo", [P, KT, SEQ], F32R)
        norm = Norm(nc, ctx, tag, gain, rows, ident, nT_hi, nT_lo, psum)
        raw = [sb(f"raw{i}", [P, D]) for i in range(3)]
        w_hi = sb("w_hi", [P, 2, 2, D], F32R)
        w_lo = sb("w_lo", [P, 2, 2, D], F32R)
        d_hi = sb("d_hi", [P, 2, D], F32R)
        d_lo = sb("d_lo", [P, 2, D], F32R)
        h = norm.xn
        hT_hi = sb("hT_hi", [P, 2, 2, SEQ], F32R)
        hT_lo = sb("hT_lo", [P, 2, 2, SEQ], F32R)
        x_in = [sem(f"x_in{m}") for m in range(ST if x is not None else 0)]
        raw_in = [sem(f"raw_in{i}") for i in range(3)]
        w_hi_done, w_lo_done = sem("w_hi_done"), sem("w_lo_done")
        gu_done, silu_done, mult_done = sem("gu_done"), sem("silu_done"), sem("mult_done")
        h_hi_done, h_lo_done = sem("h_hi_done"), sem("h_lo_done")
        down_tile, added = sem("down_tile"), sem("added")

        gate_v = w_gate.rearrange("(k p) f -> p k f", p=P)
        up_v = w_up.rearrange("(k p) f -> p k f", p=P)
        ps = lambda slot, half: psum[:, 2 * slot + half, :]
        ps2 = lambda slot: psum[:, 2 * slot:2 * slot + 2, :]
        two = lambda ap: ap.rearrange("p (a b) -> p a b", a=2)

        def gu_units(p):
            return 4 + 6 * (p - 1)

        def down_unit(p):
            return 4 + 6 * p + 4

        block = ctx.enter_context(nc.Block())

        @block.sync
        def _(sp):
            if x is not None:
                for m in range(ST):
                    sp.dma_start(rows[:, m, :], x[m * P:(m + 1) * P, :]).then_inc(x_in[m], 16)
            norm.load(sp)

            def unit(n, slot, src, third):
                if not isinstance(n, int) or n >= 3:
                    sp.wait_ge(w_lo_done, n - 2)
                sp.dma_start(raw[slot][:] if len(src.shape) == 2 else raw[slot][:].rearrange("p (k f) -> p k f", k=KT), src).then_inc(raw_in[slot], 16)

            def gu(p, t, base):
                for j, v in enumerate((gate_v, up_v)):
                    n = base + 2 * t + j
                    unit(n, (slot0 + 2 * t + j) % 3, v[:, :, bass.ds((2 * p + t) * P, P)], None)

            def down(p, base, only=False):
                for j in range(2):
                    n = base + j
                    unit(n, (slotd + j) % 3, w_down[bass.ds((2 * p + j) * P, P), :], None)

            slot0 = 0
            for t in range(2):
                gu(0, t, 0)
            slot0, slotd = 4 % 3, (4 + 4) % 3
            with sp.Fori(0, NP - 1) as p:
                for t in range(2):
                    gu(p + 1, t, p * 6 + 4)
                down(p, p * 6 + 8)
            slotd = (4 + 6 * (NP - 1)) % 3
            down(NP - 1, 4 + 6 * (NP - 1))

        def split_high(act, slot, n3, dst):
            act.wait_ge(raw_in[slot], n3 * 16)
            act.copy(dst, raw[slot][:]).then_inc(w_hi_done, 1)

        def split_low(dve, slot, n, dst, hi):
            dve.wait_ge(w_hi_done, n + 1)
            dve.tensor_tensor(dst, raw[slot][:], hi.bitcast(F32), ALU.subtract).then_inc(w_lo_done, 1)

        @block.scalar
        def _(act):
            norm.act_squares(act, (lambda e, m: e.wait_ge(x_in[m], 16)) if x is not None else (lambda e, m: None))
            norm.act_high(act)
            for t in range(2):
                for j in range(2):
                    n = 2 * t + j
                    split_high(act, n % 3, n // 3 + 1, w_hi[:, t, j, :])

            def pair(p, par, first=False, last=False):
                for t in range(2):
                    tile = p * 2 + t
                    act.wait_ge(gu_done, p * 4 + 2 * t + 1)
                    if not first:
                        act.wait_ge(h_lo_done, p * 2 + t - 1)
                    else:
                        act.wait_ge(norm.s_tr, ST)
                    act.activation(two(h[:, t, :]), ps2(2 * t), ACT.Silu).then_inc(silu_done, 1)
                    if not last:
                        for j in range(2):
                            act.wait_ge(gu_done, p * 4 + 2 * t + 1 + j)
                            u = 2 * t + j + 4
                            split_high(act, u % 3, p * 2 + u // 3 + 1, w_hi[:, t, j, :])
                    act.wait_ge(mult_done, p * 2 + t + 1)
                    if isinstance(p, int) and p < 2:
                        pass
                    else:
                        act.wait_ge(down_tile, p * 8 - 8)
                    act.copy(hT_hi[:, par, t, :], h[:, t, :]).then_inc(h_hi_done, 1)
                if not first:
                    act.wait_ge(down_tile, p * 8)
                for j in range(2):
                    u = 8 + j if not last else 4 + j
                    split_high(act, u % 3, p * 2 + u // 3 + 1, d_hi[:, j, :])

            pair(0, 0, first=True)
            pair(1, 1)
            with act.Fori(1, NP // 2) as q:
                pair(q * 2, 0)
                pair(q * 2 + 1, 1)
            pair(NP - 1, (NP - 1) % 2, last=True)

        @block.vector
        def _(dve):
            norm.dve(dve)
            for t in range(2):
                for j in range(2):
                    n = 2 * t + j
                    split_low(dve, n % 3, n, w_lo[:, t, j, :], w_hi[:, t, j, :])

            def add(q, m):
                dve.wait_ge(down_tile, q * 8 + m + 1)
                dve.scalar_tensor_tensor(out=two(rows[:, m, :]), in0=ps2(m % 4), scalar=0.5, in1=two(rows[:, m, :]),
                                         op0=ALU.mult, op1=ALU.add).then_inc(added, 1)

            def pair(p, par, first=False, last=False):
                base = p * 6 + 4
                for t in range(2):
                    def low(j):
                        if not last:
                            dve.wait_ge(gu_done, p * 4 + 2 * t + 1 + j)
                            u = 2 * t + j
                            split_low(dve, (u + 4) % 3, base + u, w_lo[:, t, j, :], w_hi[:, t, j, :])
                    low(0)
                    dve.wait_ge(silu_done, p * 2 + t + 1)
                    dve.wait_ge(gu_done, p * 4 + 2 * t + 2)
                    dve.tensor_tensor(two(h[:, t, :]), ps2(2 * t + 1), two(h[:, t, :]), ALU.mult).then_inc(mult_done, 1)
                    low(1)
                    dve.wait_ge(h_hi_done, p * 2 + t + 1)
                    dve.tensor_tensor(hT_lo[:, par, t, :], h[:, t, :], hT_hi[:, par, t, :].bitcast(F32), ALU.subtract).then_inc(h_lo_done, 1)
                if not first:
                    for m in range(ST):
                        add(p - 1, m)
                for j in range(2):
                    u = 4 + j if not last else j
                    split_low(dve, (u + 4) % 3, base + u, d_lo[:, j, :], d_hi[:, j, :])

            pair(0, 0, first=True)
            pair(1, 1)
            with dve.Fori(1, NP // 2) as q:
                pair(q * 2, 0)
                pair(q * 2 + 1, 1)
            pair(NP - 1, (NP - 1) % 2, last=True)
            for m in range(ST):
                add(NP - 1, m)

        @block.tensor
        def _(pe):
            norm.pe(pe)
            pe.wait_ge(norm.s_lo, ST)

            def gate_up(p):
                for t in range(2):
                    for j in range(2):
                        if isinstance(p, int) and p == 0:
                            pe.wait_ge(w_lo_done, 2 * t + j + 1)
                        else:
                            pe.wait_ge(w_lo_done, p * 6 + 2 * t + j - 1)
                            pe.wait_ge(mult_done, p * 2 + t - 1)
                            if not isinstance(p, int) or p >= 2:
                                pe.wait_ge(added, p * 8 - 8)
                        for half in range(2):
                            for k in range(KT):
                                mm = three_passes(pe, ps(2 * t + j, half), w_hi[:, t, j, k * P:(k + 1) * P], w_lo[:, t, j, k * P:(k + 1) * P],
                                                  nT_hi[:, k, half * HALF:(half + 1) * HALF], nT_lo[:, k, half * HALF:(half + 1) * HALF],
                                                  k == 0, k == KT - 1)
                        mm.then_inc(gu_done, 1)

            def down(q, par, last=False):
                pe.wait_ge(h_lo_done, q * 2 + 2)
                pe.wait_ge(w_lo_done, q * 6 + 10 if not last else 4 + 6 * (NP - 1) + 2)
                for m in range(ST):
                    if m >= 4:
                        pe.wait_ge(added, q * 8 + m - 3)
                    elif last:
                        pe.wait_ge(added, 8 * (NP - 1) - 4 + m + 1)
                    else:
                        pe.wait_ge(mult_done, q * 2 + 2 + m // 2 + 1)
                    for half in range(2):
                        for t in range(2):
                            mm = three_passes(pe, ps(m % 4, half), hT_hi[:, par, t, m * P:(m + 1) * P], hT_lo[:, par, t, m * P:(m + 1) * P],
                                              d_hi[:, t, half * HALF:(half + 1) * HALF], d_lo[:, t, half * HALF:(half + 1) * HALF],
                                              t == 0, t == 1)
                    mm.then_inc(down_tile, 1)

            gate_up(0)
            gate_up(1)
            down(0, 0)
            with pe.Fori(1, NP // 2) as q:
                gate_up(q * 2)
                down(q * 2 - 1, 1)
                gate_up(q * 2 + 1)
                down(q * 2, 0)
            gate_up(NP - 1)
            down(NP - 2, 1)
            down(NP - 1, 0, last=True)


def make_ident(nc, ident, s_id):
    with nc.Block() as block:
        @block.gpsimd
        def _(pool):
            pool.memset(ident[:], 0.0).then_inc(s_id, 1)
            pool.wait_ge(s_id, 1)
            pool.affine_select(out=ident[:], in_=ident[:], compare_op=ALU.not_equal, fill=1.0, base=0,
                               pattern=[[-1, P]], channel_multiplier=1).then_inc(s_id, 1)


GROUPS, STATE, SG = 32, 64, 16
T = P // SG
CH = SEQ // T
WIDTH = GROUPS * SG
SLOTS = 2 * T - 1
QR, KVR, NOPE, ROPE, VH, HEADS = 256, 128, 64, 32, 64, 8
OFF_CKV = QR
OFF_KR = OFF_CKV + KVR
OFF_U = OFF_KR + ROPE
OFF_GA = OFF_U + WIDTH
OFF_GS = OFF_GA + D
ZW = OFF_KR + 2 * ROPE
SCALE = (NOPE + ROPE) ** -0.5


def tools(nc, ctx, tag):
    sb = lambda n, s, d=F32: ctx.enter_context(nc.sbuf_tensor(f"{tag}_{n}", s, d))
    return sb, semaphores(nc, ctx, tag)


def project_phase(nc, w, rows, ident, psum, zrow, u, gates):
    with Phase(nc) as ctx:
        sb, sem = tools(nc, ctx, "pj")
        nT_hi, nT_lo = sb("nT_hi", [P, KT, SEQ], F32R), sb("nT_lo", [P, KT, SEQ], F32R)
        norm = Norm(nc, ctx, "pjn", w["mix_norm"][0], rows, ident, nT_hi, nT_lo, psum)
        w_in = w["w_in"][0]
        half = ROPE // 2
        latent = [(0, slice(0, OFF_U)), (OFF_U, slice(OFF_KR + half, OFF_U)), (OFF_U + half, slice(OFF_KR, OFF_KR + half))]

        def lhs(j, k, m):
            sl = slice(m * P, (m + 1) * P) if j == 0 else slice(m, SEQ, T)
            return nT_hi[:, k, sl], nT_lo[:, k, sl]

        rp = RowProduct(nc, ctx, "rp", [(w_in, latent, ZW), (w_in, [(0, slice(OFF_U, OFF_GA))], WIDTH)], lhs, psum)
        NG = 2 * D // P
        gp = ColumnProduct(nc, ctx, "gp", w_in, [OFF_GA + n * P for n in range(NG)], nT_hi, nT_lo, psum)
        sig = sb("sig", [P, 2, SEQ])
        s_out = [sem("s_out0"), sem("s_out1")]
        NU = len(rp.units())
        block = ctx.enter_context(nc.Block())

        @block.sync
        def _(sp):
            norm.load(sp)
            for n in range(NU):
                rp.load(sp, n)
            gp.load(sp, 0)
            gp.load(sp, 1)
            for n in range(NG):
                if n + 2 < NG:
                    gp.load(sp, n + 2)
                sp.wait_ge(gp.read[n % 2], n // 2 + 1)
                sp.dma_start(gates[n * P:(n + 1) * P, :], sig[:, n % 2, :]).then_inc(s_out[n % 2], 16)
            for i in range(2):
                sp.wait_ge(s_out[i], 16 * NG // 2)

        @block.scalar
        def _(act):
            norm.act_squares(act, lambda e, m: None)
            norm.act_high(act)
            for j in range(2):
                for k in range(KT):
                    rp.high(act, j * KT + k)
                    if j == 1 and k == 1:
                        for m in range(ST):
                            rp.wait_bank(act, 0, m)
                            act.copy(zrow[:, m, :], psum[:, m, 0:ZW]).then_inc(rp.read, 1)
            gp.high(act, 0)
            gp.high(act, 1)
            for m in range(ST):
                rp.wait_bank(act, 1, m)
                act.copy(u[:, :, m, :], psum[:, m, :].rearrange("p (g i) -> p g i", i=SG)).then_inc(rp.read, 1)
            for n in range(NG):
                act.wait_ge(gp.mm_done, n + 1)
                if n >= 2:
                    act.wait_ge(s_out[n % 2], 16 * (n // 2))
                act.activation(sig[:, n % 2, :].rearrange("p (a b) -> p a b", a=2), gp.ps[n % 2], ACT.Sigmoid).then_inc(gp.read[n % 2], 1)
                gp.high(act, n + 2)

        @block.vector
        def _(dve):
            norm.dve(dve)
            for n in range(NU):
                rp.low(dve, n)
            gp.low(dve, 0)
            gp.low(dve, 1)
            for n in range(NG):
                gp.low(dve, n + 2)

        @block.tensor
        def _(pe):
            norm.pe(pe)
            pe.wait_ge(norm.s_lo, ST)
            rp.products(pe)
            for n in range(NG):
                if n < 2:
                    pe.wait_ge(rp.read, ST + 4 * (n + 1))
                gp.product(pe, n)


def ssm_phase(nc, w, ident, psum, u, outer):
    sb, sem = tools(nc, outer, "ss")
    E_mat = [sb(f"EM{c}", [P, GROUPS, P]) for c in range(2)]
    C_mat = [sb(f"CM{c}", [P, GROUPS, T, SG]) for c in range(2)]
    lam8 = sb("lam8", [P, 2, 2, GROUPS])
    Bb = sb("Bb", [P, 2, GROUPS, SG])
    C0 = sb("C0", [P, 2, GROUPS, SG])
    with Phase(nc) as ctx:
        sb, sem = tools(nc, ctx, "sa")
        lam_raw = sb("lam_raw", [GROUPS, 2, P])
        ldt = sb("ldt", [P, GROUPS])
        b_raw = sb("b_raw", [P, 2, GROUPS, SG])
        c_raw = sb("c_raw", [P, 2, 4, P])
        lam = sb("lam", [P, 2, GROUPS])
        sc = sb("sc", [P, 12, GROUPS])
        pw = sb("pw", [P, T + 1, 2, GROUPS])
        PB = sb("PB", [P, 2, T, GROUPS])
        PC = sb("PC", [P, 3, T, GROUPS])
        X = [sb(f"X{c}", [P, GROUPS, T, SG]) for c in range(2)]
        tmp = sb("tmp", [P, GROUPS, T, SG])
        names = "lam b c tr mag ang sin dve pool pw evac xt xe".split()
        s = {n: sem(n) for n in names}
        s_ldt, s_cf, s_negc = sem("ldt_in"), sem("cf"), sem("negc")
        block = ctx.enter_context(nc.Block())

        @block.sync
        def _(sp):
            for c, a in enumerate((w["ssm_lambda_re"], w["ssm_lambda_im"])):
                sp.dma_start(lam_raw[:, c, :].rearrange("g (d p) -> g d p", d=2), a[0].rearrange("d g p -> g d p")).then_inc(s["lam"], 16)
            for d in range(2):
                h = slice(64 * d, 64 * d + 64)
                sp.dma_start(ldt[h, :], w["ssm_log_dt"][0, d:d + 1, :].broadcast_to([64, GROUPS])).then_inc(s_ldt, 16)
                for c, a in enumerate((w["ssm_b_re"], w["ssm_b_im"])):
                    sp.dma_start(b_raw[h, c], a[0, d].rearrange("g p i -> p g i")).then_inc(s["b"], 16)
                for c, a in enumerate((w["ssm_c_re"], w["ssm_c_im"])):
                    sp.dma_start(c_raw[:, c, :, h], a[0, d].rearrange("(b r) i p -> (r i) b p", b=4)).then_inc(s["c"], 16)

        @block.tensor
        def _(pe):
            pe.wait_ge(s["lam"], 32)
            for c in range(2):
                mm = pe.transpose(psum[:, 0, c * GROUPS:(c + 1) * GROUPS], lam_raw[:, c, :], ident[0:GROUPS, 0:GROUPS])
            mm.then_inc(s["tr"], 1)
            pe.wait_ge(s["c"], 64)
            for c in range(2):
                for b in range(4):
                    mm = pe.transpose(psum[:, 1 + c, b * P:(b + 1) * P], c_raw[:, c, b, :], ident[:])
                mm.then_inc(s["tr"], 1)
            for q in range(2 * GROUPS // 4):
                c, g0 = q // 8, q % 8 * 4
                if g0 == 0:
                    pe.wait_ge(s_cf, c + 1)
                if q >= 4:
                    pe.wait_ge(s["xe"], q - 3)
                for g in range(4):
                    mm = pe.transpose(psum[:, 4 + q % 4, g * P:(g + 1) * P], X[c][:, g0 + g, :, :].rearrange("p t i -> p (t i)"), ident[:])
                mm.then_inc(s["xt"], 1)

        @block.scalar
        def _(act):
            act.wait_ge(s["tr"], 1)
            act.copy(lam[:], psum[:, 0, 0:2 * GROUPS].rearrange("p (c g) -> p c g", c=2)).then_inc(s["mag"], 1)
            act.wait_ge(s_ldt, 32)
            act.activation(sc[:, 0, :], ldt[:], ACT.Exp).then_inc(s["mag"], 1)
            act.wait_ge(s["dve"], 2)
            act.activation(sc[:, 3, :], sc[:, 1, :], ACT.Exp).then_inc(s["mag"], 1)
            act.wait_ge(s["tr"], 3)
            act.copy(C0[:, 0].rearrange("p g i -> p (g i)"), psum[:, 1, :]).then_inc(s_negc, 1)
            act.mul(C0[:, 1].rearrange("p g i -> p (g i)"), psum[:, 2, :], -1.0).then_inc(s_negc, 1)
            act.wait_ge(s["ang"], 1)
            act.activation(sc[:, 4:6, :], sc[:, 4:6, :], ACT.Sin).then_inc(s["sin"], 1)
            for q in range(2 * GROUPS // 4):
                c, g0 = q // 8, q % 8 * 4
                act.wait_ge(s["xt"], q + 1)
                act.copy(E_mat[c][:, g0:g0 + 4, :], psum[:, 4 + q % 4, :].rearrange("p (g s) -> p g s", g=4)).then_inc(s["xe"], 1)

        @block.vector
        def _(dve):
            link = Chain(dve, s["dve"])
            mul = lambda o, a, b: link(dve.tensor_tensor(o, a, b, ALU.mult))
            add = lambda o, a, b: link(dve.tensor_tensor(o, a, b, ALU.add))
            sub = lambda o, a, b: link(dve.tensor_tensor(o, a, b, ALU.subtract))
            dve.wait_ge(s["mag"], 2)
            row = lambda i: sc[:, i, :]
            mul(row(1), lam[:, 0], row(0))
            mul(row(2), lam[:, 1], row(0))
            link(dve.tensor_copy(row(4), row(2)))
            link(dve.tensor_copy(row(5), row(2)))
            reduce_angle(link, row(4), row(6), row(7), 0.0)
            reduce_angle(link, row(5), row(6), row(7), 0.25)
            dve.sem_inc(s["ang"], 1)
            dve.wait_ge(s["mag"], 3)
            dve.wait_ge(s["sin"], 1)
            link(dve.memset(pw[:, 0, 0], 1.0))
            link(dve.memset(pw[:, 0, 1], 0.0))
            mul(pw[:, 1, 0], row(3), row(5))
            mul(pw[:, 1, 1], row(3), row(4))
            lre, lim, bre, bim = lam[:, 0], lam[:, 1], pw[:, 1, 0], pw[:, 1, 1]
            mul(row(0), lre, lre)
            mul(row(1), lim, lim)
            add(row(0), row(0), row(1))
            link(dve.reciprocal(row(2), row(0)))
            link(dve.tensor_scalar(row(6), bre, -1.0, None, ALU.add))
            mul(row(7), row(6), lre)
            mul(row(8), bim, lim)
            add(row(7), row(7), row(8))
            mul(row(7), row(7), row(2))
            mul(row(8), bim, lre)
            mul(row(9), row(6), lim)
            sub(row(8), row(8), row(9))
            mul(row(8), row(8), row(2))
            dve.wait_ge(s["b"], 64)
            wide = lambda a: a.unsqueeze(2).broadcast_to([P, GROUPS, SG])
            t0, t1 = tmp[:, :, 0, :], tmp[:, :, 1, :]
            kre, kim = wide(row(7)), wide(row(8))
            mul(t0, b_raw[:, 0], kre)
            mul(t1, b_raw[:, 1], kim)
            sub(Bb[:, 0], t0, t1)
            mul(t0, b_raw[:, 1], kre)
            mul(t1, b_raw[:, 0], kim)
            add(Bb[:, 1], t0, t1)

            def complex_mul(o, a, b, n):
                br, bi = (b[:, i:i + 1, :].broadcast_to([P, n, GROUPS]) for i in range(2))
                x, y = tmp[:, 0:n, 2, :], tmp[:, 0:n, 3, :]
                x, y = (tmp[:].rearrange("p g t i -> p (g t i)")[:, 2048 + z * n * GROUPS:2048 + (z + 1) * n * GROUPS].rearrange("p (n g) -> p n g", n=n) for z in range(2))
                mul(x, a[:, :, 0], br)
                mul(y, a[:, :, 1], bi)
                sub(o[:, :, 0], x, y)
                mul(x, a[:, :, 0], bi)
                mul(y, a[:, :, 1], br)
                add(o[:, :, 1], x, y)
            complex_mul(pw[:, 2:3], pw[:, 1:2], pw[:, 1], 1)
            complex_mul(pw[:, 3:5], pw[:, 1:3], pw[:, 2], 2)
            complex_mul(pw[:, 5:9], pw[:, 1:5], pw[:, 4], 4)
            for ri in range(2):
                link(dve.tensor_copy(lam8[:, 0, ri], pw[:, T, 0]))
            link(dve.tensor_copy(lam8[:, 1, 0], pw[:, T, 1]))
            link(dve.tensor_scalar(lam8[:, 1, 1], pw[:, T, 1], -1.0, None, ALU.mult))
            F_, B_ = slice(0, 64), slice(64, 128)
            for ri in range(2):
                link(dve.tensor_copy(PB[F_, ri], pw[F_, T - 1::-1, ri]))
                link(dve.tensor_copy(PB[B_, ri], pw[B_, 0:T, ri]))
                link(dve.tensor_copy(PC[F_, ri], pw[F_, 1:T + 1, ri]))
                link(dve.tensor_copy(PC[B_, ri], pw[B_, T:0:-1, ri]))
            link(dve.tensor_scalar(PC[:, 2], PC[:, 0], -1.0, None, ALU.mult))
            power = lambda a: a.rearrange("p t g -> p g t").unsqueeze(3).broadcast_to([P, GROUPS, T, SG])
            chan = lambda a: a.unsqueeze(2).broadcast_to([P, GROUPS, T, SG])

            def outer_product(o, p0, v0, p1, v1, op):
                for half in range(2):
                    g = slice(half * 16, half * 16 + 16)
                    mul(o[:, g], power(p0)[:, g], chan(v0)[:, g])
                    mul(tmp[:, g], power(p1)[:, g], chan(v1)[:, g])
                link(dve.tensor_tensor(o[:], o[:], tmp[:], op))
            outer_product(X[0], PB[:, 0], Bb[:, 0], PB[:, 1], Bb[:, 1], ALU.subtract)
            dve.sem_inc(s_cf, 1)
            outer_product(X[1], PB[:, 0], Bb[:, 1], PB[:, 1], Bb[:, 0], ALU.add)
            dve.sem_inc(s_cf, 1)
            dve.wait_ge(s_negc, 2)
            outer_product(C_mat[0], PC[:, 0], C0[:, 0], PC[:, 1], C0[:, 1], ALU.add)
            outer_product(C_mat[1], PC[:, 0], C0[:, 1], PC[:, 1], C0[:, 0], ALU.subtract)

    with Phase(nc) as ctx:
        sb, sem = tools(nc, ctx, "sb")
        M = sb("M", [P, GROUPS, P])
        UT = sb("UT", [P, GROUPS, CH])
        with Phase(nc) as inner:
            chunk_matrices(nc, inner, ident, psum, u, M, UT, C_mat, Bb, C0)
        with Phase(nc) as inner:
            scan_chunks(nc, inner, psum, E_mat, UT, lam8)
        chunk_outputs(nc, ctx, w, psum, u, M, UT, E_mat, C_mat)


def chunk_matrices(nc, ctx, ident, psum, u, M, UT, C_mat, Bb, C0):
    sb, sem = tools(nc, ctx, "sc")
    kern = sb("kern", [SG, GROUPS, SLOTS * SG])
    Bz = sb("Bz", [P, 2, 2, GROUPS, SG])
    s_mm, s_cp, s_m, s_ut, s_utc, s_z, s_bz = map(sem, ("kern_mm", "kern_cp", "m_in", "ut", "ut_cp", "z", "bz"))
    with nc.Block() as block:
        @block.tensor
        def _(pe):
            cm = lambda c, g, t0, t1: C_mat[c][:, g, t0:t1, :].rearrange("p t i -> p (t i)")
            pe.wait_ge(s_bz, 2)
            for g in range(GROUPS):
                q = g // 2
                if g % 2 == 0 and q >= 4:
                    pe.wait_ge(s_cp, q - 3)
                out = psum[0:SG, q % 4, g % 2 * 256:g % 2 * 256 + SLOTS * SG]
                for a, b, lhs, rhs in ((0, T - 1, lambda c: Bz[:, 1, c, g, :], lambda c: cm(c, g, 1, T)),
                                       (T - 1, T, lambda c: Bb[:, c, g, :], lambda c: C0[:, c, g, :]),
                                       (T, SLOTS, lambda c: Bz[:, 0, c, g, :], lambda c: cm(c, g, 0, T - 1))):
                    for c in range(2):
                        mm = pe.matmul(out[:, a * SG:b * SG], lhs(c), rhs(c), start=c == 0, stop=c == 1)
                if g % 2:
                    mm.then_inc(s_mm, 1)
            for q in range(GROUPS // 4):
                if q >= 4:
                    pe.wait_ge(s_utc, q - 3)
                for g in range(4):
                    mm = pe.transpose(psum[:, 4 + q % 4, g * P:(g + 1) * P], u[:, 4 * q + g, :, :].rearrange("p t i -> p (t i)"), ident[:])
                mm.then_inc(s_ut, 1)

        @block.scalar
        def _(act):
            for q in range(GROUPS // 2):
                act.wait_ge(s_mm, q + 1)
                act.copy(kern[:, 2 * q:2 * q + 2, :], psum[0:SG, q % 4, :].rearrange("p (g x) -> p g x", g=2)[:, :, 0:SLOTS * SG]).then_inc(s_cp, 1)

        @block.vector
        def _(dve):
            dve.memset(Bz[:], 0.0).then_inc(s_z, 1)
            dve.wait_ge(s_z, 1)
            for d, h in enumerate((slice(0, 64), slice(64, 128))):
                dve.tensor_copy(Bz[h, d], Bb[h]).then_inc(s_bz, 1)
            for q in range(GROUPS // 4):
                dve.wait_ge(s_ut, q + 1)
                dve.tensor_copy(UT[:, 4 * q:4 * q + 4, :], psum[:, 4 + q % 4, :].rearrange("p (g c) -> p g c", g=4)).then_inc(s_utc, 1)

        @block.sync
        def _(sp):
            for b in range(4):
                sp.wait_ge(s_cp, 4 * (b + 1))
                for t in range(T):
                    at = (T - 1 - t) * SG
                    sp.dma_start(M[t * SG:(t + 1) * SG, 8 * b:8 * b + 8, :], kern[:, 8 * b:8 * b + 8, at:at + P]).then_inc(s_m, 16)
            sp.wait_ge(s_m, 16 * 4 * T)


def scan_chunks(nc, ctx, psum, E_mat, UT, lam8):
    sb, sem = tools(nc, ctx, "sd")
    H = sb("H", [P, CH + 1, 2, GROUPS])
    prod = sb("prod", [P, 2, 2, GROUPS])
    s_e, s_ec, s_mul, s_sum, s_scan = map(sem, ("e", "e_cp", "mul", "sum", "scan"))
    with nc.Block() as block:
        @block.tensor
        def _(pe):
            for q in range(2 * GROUPS // 4):
                c, g0 = q // 8, q % 8 * 4
                if q >= 4:
                    pe.wait_ge(s_ec, 2 * (q - 3))
                for g in range(4):
                    mm = pe.matmul(psum[:, q % 4, g * P:(g + 1) * P], E_mat[c][:, g0 + g, :], UT[:, g0 + g, :], start=True, stop=True)
                mm.then_inc(s_e, 1)

        @block.scalar
        def _(act):
            for q in range(2 * GROUPS // 4):
                c, g0 = q // 8, q % 8 * 4
                act.wait_ge(s_e, q + 1)
                ps = psum[:, q % 4, :].rearrange("p (g c) -> p c g", g=4)
                act.copy(H[0:64, 1:CH + 1, c, g0:g0 + 4], ps[0:64]).then_inc(s_ec, 1)
                act.copy(H[64:128, CH:0:-1, c, g0:g0 + 4], ps[64:128]).then_inc(s_ec, 1)
            act.wait_ge(s_scan, CH)
            for c in range(2):
                act.copy(E_mat[c][0:64].rearrange("p g c -> p c g"), H[0:64, 0:CH, c, :])

        @block.vector
        def _(dve):
            dve.memset(H[:, 0], 0.0).then_inc(s_scan, 1)
            dve.wait_ge(s_ec, 4 * GROUPS // 4)
            flat = lambda ap: ap.rearrange("p a r g -> p (a r) g")

            def step(n):
                now = H[:, bass.ds(n, 1)].rearrange("p a r g -> p a (r g)").broadcast_to([P, 2, 2 * GROUPS])
                nxt = flat(H[:, bass.ds(n + 1, 1)])
                dve.wait_ge(s_scan, n + 1)
                dve.tensor_tensor(prod[:].rearrange("p c r g -> p c (r g)"), now, lam8[:].rearrange("p c r g -> p c (r g)"), ALU.mult).then_inc(s_mul, 1)
                dve.wait_ge(s_mul, n + 1)
                dve.tensor_tensor(nxt, nxt, prod[:, 0], ALU.add).then_inc(s_sum, 1)
                dve.wait_ge(s_sum, n + 1)
                dve.tensor_tensor(nxt, nxt, prod[:, 1, ::-1], ALU.add).then_inc(s_scan, 1)
            with dve.Fori(0, (CH - 4) // 4) as q:
                for i in range(4):
                    step(q * 4 + i)
            for n in range(CH - 4, CH - 1):
                step(n)
            dve.wait_ge(s_scan, CH)
            for c in range(2):
                dve.tensor_copy(E_mat[c][64:128].rearrange("p g c -> p c g"), H[64:128, CH - 1::-1, c, :])


def chunk_outputs(nc, ctx, w, psum, u, M, UT, H, C_mat):
    sb, sem = tools(nc, ctx, "se")
    Db = sb("Db", [P, GROUPS, SG])
    s_d, s_du, s_y, s_sum = map(sem, ("d_in", "du", "y", "y_sum"))
    with nc.Block() as block:
        @block.sync
        def _(sp):
            sp.dma_start(Db[:].rearrange("p g i -> p (g i)"), w["ssm_d"][0:1, :].broadcast_to([P, WIDTH])).then_inc(s_d, 16)

        @block.tensor
        def _(pe):
            for q in range(GROUPS // 4):
                if q >= 4:
                    pe.wait_ge(s_sum, q - 3)
                for g in range(4 * q, 4 * q + 4):
                    out = psum[:, q % 4, g % 4 * P:(g % 4 + 1) * P]
                    pe.matmul(out, UT[:, g, :], M[:, g, :], start=True, stop=False)
                    for c in range(2):
                        mm = pe.matmul(out, H[c][:, g, :], C_mat[c][:, g].rearrange("p t i -> p (t i)"), start=False, stop=c == 1)
                mm.then_inc(s_y, 1)

        @block.vector
        def _(dve):
            dve.wait_ge(s_d, 16)
            for q in range(GROUPS // 4):
                g = slice(4 * q, 4 * q + 4)
                dve.tensor_tensor(u[:, g], u[:, g], Db[:, g].unsqueeze(2).broadcast_to([P, 4, T, SG]), ALU.mult).then_inc(s_du, 1)
                dve.wait_ge(s_du, q + 1)
                dve.wait_ge(s_y, q // 2 * 2 + 2)
                block_y = UT[:, 8 * (q // 2):8 * (q // 2) + 8, :].rearrange("p a b -> p (a b)").rearrange("p (t g i) -> p g t i", t=T, i=SG)
                dve.tensor_tensor(block_y[:, q % 2 * 4:q % 2 * 4 + 4], psum[:, q % 4, :].rearrange("p (g t i) -> p g t i", g=4, i=SG),
                                  u[:, g], ALU.add).then_inc(s_sum, 1)

        @block.scalar
        def _(act):
            for b in range(GROUPS // 8):
                g = slice(8 * b, 8 * b + 8)
                act.wait_ge(s_sum, 2 * b + 2)
                act.activation(u[:, g].rearrange("p g t i -> p (g t i)"), UT[:, g, :].rearrange("p a b -> p (a b)"), ACT.Gelu_apprx_tanh)


def glu_phase(nc, w, ident, psum, y, gates, partial):
    with Phase(nc) as ctx:
        sb, sem = tools(nc, ctx, "gl")
        NB = WIDTH // P
        yT_hi, yT_lo = sb("yT_hi", [P, NB, SEQ], F32R), sb("yT_lo", [P, NB, SEQ], F32R)
        sT_hi, sT_lo = sb("sT_hi", [P, NB, SEQ], F32R), sb("sT_lo", [P, NB, SEQ], F32R)
        bias = sb("bias", [P, 2 * NB])
        sig, val = sb("sig", [P, SEQ]), sb("val", [P, 2, SEQ])
        gate, out = sb("gate", [P, 2, SEQ]), sb("out", [P, 2, SEQ])
        order = [c for b in range(NB) for c in (WIDTH + b * P, b * P)]
        glu = ColumnProduct(nc, ctx, "glu", w["w_glu"][0], order, yT_hi, yT_lo, psum)
        wos = ColumnProduct(nc, ctx, "wos", w["w_o_ssm"][0], [n * P for n in range(KT)], sT_hi, sT_lo, psum, 4)
        s_b, s_t, s_hi, s_lo, s_sig, s_vhi, s_vlo = map(sem, ("b", "t", "yhi", "ylo", "sig", "vhi", "vlo"))
        s_g, s_o = [sem("g0"), sem("g1")], [sem("o0"), sem("o1")]
        block = ctx.enter_context(nc.Block())
        two = lambda ap: ap.rearrange("p (a b) -> p a b", a=2)
        NT = 2 * NB
        yb = y[:].rearrange("p g t i -> p (g t i)").rearrange("p (b t c) -> p b t c", b=NB, t=T)
        dest = lambda a, b, tq: a[:, b, :].rearrange("p (c t) -> p t c", t=T)[:, 4 * tq:4 * tq + 4, :]
        bank = lambda n: psum[:, 4 + n % 4, :].rearrange("p (t c) -> p t c", t=4)

        @block.sync
        def _(sp):
            sp.dma_start(bias[:], w["b_glu"][0].rearrange("(n p) -> p n", p=P), allow_slow_non_contiguous=True).then_inc(s_b, 16)
            for n in range(glu.N):
                glu.load(sp, n)
            for n in range(2):
                wos.load(sp, n)
                sp.dma_start(gate[:, n, :], gates[D + n * P:D + (n + 1) * P, :]).then_inc(s_g[n], 16)
            for n in range(KT):
                if n + 2 < KT:
                    wos.load(sp, n + 2)
                sp.wait_ge(wos.read[n % 2], n // 2 + 1)
                if n + 2 < KT:
                    sp.dma_start(gate[:, n % 2, :], gates[D + (n + 2) * P:D + (n + 3) * P, :]).then_inc(s_g[n % 2], 16)
                sp.dma_start(partial[n * P:(n + 1) * P, :], out[:, n % 2, :]).then_inc(s_o[n % 2], 16)
            for i in range(2):
                sp.wait_ge(s_o[i], 16 * KT // 2)

        @block.tensor
        def _(pe):
            for n in range(NT):
                b, tq = n // 2, n % 2
                if n >= 4:
                    pe.wait_ge(s_lo, n - 3)
                for t in range(4):
                    mm = pe.transpose(psum[:, 4 + n % 4, t * P:(t + 1) * P], yb[:, b, 4 * tq + t, :], ident[:])
                mm.then_inc(s_t, 1)
            pe.wait_ge(s_lo, NT)
            for n in range(glu.N):
                glu.product(pe, n)
            pe.wait_ge(s_vlo, NB)
            for n in range(KT):
                wos.product(pe, n)

        @block.scalar
        def _(act):
            glu.high(act, 0)
            glu.high(act, 1)
            for n in range(NT):
                act.wait_ge(s_t, n + 1)
                act.copy(dest(yT_hi, n // 2, n % 2), bank(n)).then_inc(s_hi, 1)
            act.wait_ge(s_b, 16)
            for b in range(NB):
                act.wait_ge(glu.mm_done, 2 * b + 1)
                if b:
                    act.wait_ge(glu.read[1], b)
                act.activation(two(sig[:]), glu.ps[0], ACT.Sigmoid, bias=bias[:, NB + b:NB + b + 1]).then_inc(glu.read[0], 1)
                glu.high(act, 2 * b + 2)
                act.wait_ge(glu.read[1], b + 1)
                act.copy(sT_hi[:, b, :], val[:, b % 2, :]).then_inc(s_vhi, 1)
                glu.high(act, 2 * b + 3)
            wos.high(act, 0)
            wos.high(act, 1)
            for n in range(KT):
                wos.high(act, n + 2)

        @block.vector
        def _(dve):
            glu.low(dve, 0)
            glu.low(dve, 1)
            for n in range(NT):
                dve.wait_ge(s_hi, n + 1)
                dve.tensor_tensor(dest(yT_lo, n // 2, n % 2), bank(n), dest(yT_hi, n // 2, n % 2).bitcast(F32), ALU.subtract).then_inc(s_lo, 1)
            dve.wait_ge(s_b, 16)
            for b in range(NB):
                dve.wait_ge(glu.mm_done, 2 * b + 2)
                dve.wait_ge(glu.read[0], b + 1)
                if b >= 2:
                    dve.wait_ge(s_vlo, b - 1)
                dve.scalar_tensor_tensor(out=two(val[:, b % 2, :]), in0=glu.ps[1], scalar=bias[:, b:b + 1], in1=two(sig[:]),
                                         op0=ALU.add, op1=ALU.mult).then_inc(glu.read[1], 1)
                glu.low(dve, 2 * b + 2)
                dve.wait_ge(s_vhi, b + 1)
                dve.tensor_tensor(sT_lo[:, b, :], val[:, b % 2, :], sT_hi[:, b, :].bitcast(F32), ALU.subtract).then_inc(s_vlo, 1)
                glu.low(dve, 2 * b + 3)
            wos.low(dve, 0)
            wos.low(dve, 1)
            for n in range(KT):
                dve.wait_ge(wos.mm_done, n + 1)
                dve.wait_ge(s_g[n % 2], 16 * (n // 2 + 1))
                if n >= 2:
                    dve.wait_ge(s_o[n % 2], 16 * (n // 2))
                dve.tensor_tensor(two(out[:, n % 2, :]), wos.ps[n % 2], two(gate[:, n % 2, :]), ALU.mult).then_inc(wos.read[n % 2], 1)
                wos.low(dve, n + 2)


def attention_phase(nc, w, ident, psum, zrow, aT_hi, aT_lo):
    with Phase(nc) as ctx:
        sb, sem = tools(nc, ctx, "at")
        NL = 3
        lT_hi, lT_lo = sb("lT_hi", [P, NL, SEQ], F32R), sb("lT_lo", [P, NL, SEQ], F32R)
        krT = sb("krT", [P, SEQ])
        trig = sb("trig", [P, SEQ])
        with Phase(nc) as inner:
            latents(nc, inner, w, ident, psum, zrow, lT_hi, lT_lo, krT, trig)
        head_loop(nc, ctx, w, ident, psum, lT_hi, lT_lo, krT, trig, aT_hi, aT_lo)


def latents(nc, ctx, w, ident, psum, zrow, lT_hi, lT_lo, krT, trig):
    sb, sem = tools(nc, ctx, "la")
    gb = sb("gb", [P, QR + KVR])
    zn = sb("zn", [P, 2, QR + KVR])
    stat = sb("stat", [P, 5, 2, ST])
    pos, ang, turns = sb("pos", [P, SEQ], I32), sb("ang", [P, SEQ]), sb("turns", [P, SEQ])
    cst = sb("cst", [P, 2])
    s_gb, s_pos, s_cst, s_sq, s_var, s_sqrt, s_link, s_zn, s_tr, s_hi, s_lo, s_ang, s_kr, s_sgn = map(
        sem, ("gb", "pos", "cst", "sq", "var", "sqrt", "link", "zn", "tr", "hi", "lo", "ang", "kr", "sgn"))
    Rp = slice(64, 128)
    bank = lambda m: psum[:, m, 0:3 * P].rearrange("p (k s) -> p k s", k=3)
    with nc.Block() as block:
        @block.sync
        def _(sp):
            sp.dma_start(pos[Rp, :], w["positions"][0:1, :].broadcast_to([64, SEQ])).then_inc(s_pos, 16)
            sp.dma_start(cst[:], w["rope_const"]).then_inc(s_cst, 16)
            sp.dma_start(gb[:, 0:QR], w["q_norm"][0:1, :].broadcast_to([P, QR])).then_inc(s_gb, 16)
            sp.dma_start(gb[:, QR:], w["kv_norm"][0:1, :].broadcast_to([P, KVR])).then_inc(s_gb, 16)

        @block.scalar
        def _(act):
            for m in range(ST):
                act.activation(psum[:, m, 0:QR], zrow[:, m, 0:QR], ACT.Square, accum_out=stat[:, 0, 0, m:m + 1]).then_inc(s_sq, 1)
                act.activation(psum[:, m, QR:QR + KVR], zrow[:, m, QR:QR + KVR], ACT.Square, accum_out=stat[:, 0, 1, m:m + 1]).then_inc(s_sq, 1)
            act.wait_ge(s_var, 1)
            act.activation(stat[:, 2], stat[:, 1], ACT.Sqrt).then_inc(s_sqrt, 1)
            act.wait_ge(s_ang, 1)
            act.activation(trig[Rp, :], ang[Rp, :], ACT.Sin).then_inc(s_sgn, 1)
            for m in range(ST):
                act.wait_ge(s_tr, m + 1)
                act.copy(krT[Rp, m * P:(m + 1) * P], psum[Rp, m, 3 * P:4 * P])
                act.copy(lT_hi[:, :, m * P:(m + 1) * P], bank(m)).then_inc(s_hi, 1)

        @block.vector
        def _(dve):
            link = Chain(dve, s_link)

            def low(m):
                sl = slice(m * P, (m + 1) * P)
                dve.wait_ge(s_hi, m + 1)
                dve.tensor_tensor(lT_lo[:, :, sl], bank(m), lT_hi[:, :, sl].bitcast(F32), ALU.subtract)
            dve.wait_ge(s_sq, 2 * ST)
            for j, n in enumerate((QR, KVR)):
                link(dve.tensor_scalar(stat[:, 1, j], stat[:, 0, j], 1.0 / n, EPS, ALU.mult, ALU.add))
            dve.sem_inc(s_var, 1)
            dve.wait_ge(s_sqrt, 1)
            newton(link, stat[:, 1], stat[:, 2], stat[:, 3], stat[:, 4])
            dve.wait_ge(s_gb, 32)

            def row(m):
                if m >= 2:
                    dve.wait_ge(s_tr, m - 1)
                for j, sl in enumerate((slice(0, QR), slice(QR, QR + KVR))):
                    dve.scalar_tensor_tensor(out=zn[:, m % 2, sl], in0=zrow[:, m, sl], scalar=stat[:, 3, j, m:m + 1], in1=gb[:, sl],
                                             op0=ALU.mult, op1=ALU.mult).then_inc(s_zn, 1)
            dve.wait_ge(s_pos, 16)
            dve.wait_ge(s_cst, 16)
            link(dve.tensor_copy(ang[Rp], pos[Rp]))
            link(dve.tensor_scalar(ang[Rp], ang[Rp], cst[Rp, 0:1], None, ALU.mult))
            C, S = slice(64, 96), slice(96, 128)
            reduce_angle(link, ang[C], turns[C], None, 0.25)
            reduce_angle(link, ang[S], turns[S], None, 0.0)
            dve.sem_inc(s_ang, 1)
            for m in range(ST):
                row(m)
                if m:
                    low(m - 1)
            low(ST - 1)
            dve.wait_ge(s_sgn, 1)
            dve.tensor_scalar(trig[S], trig[S], cst[S, 1:2], None, ALU.mult)

        @block.tensor
        def _(pe):
            pe.wait_ge(s_sqrt, 1)
            for m in range(ST):
                pe.wait_ge(s_zn, 2 * m + 2)
                for k in range(3):
                    pe.transpose(psum[:, m, k * P:(k + 1) * P], zn[:, m % 2, k * P:(k + 1) * P], ident[:])
                pe.transpose(psum[:, m, 3 * P:4 * P], zrow[:, m, ZW - P:ZW], ident[:]).then_inc(s_tr, 1)


def head_loop(nc, ctx, w, ident, psum, lT_hi, lT_lo, krT, trig, aT_hi, aT_lo):
    sb, sem = tools(nc, ctx, "hd")
    KD = NOPE + ROPE
    raw = sb("raw", [P, 3, P])
    w_hi, w_lo = sb("w_hi", [P, 3, P], F32R), sb("w_lo", [P, 3, P], F32R)
    QT_hi, QT_lo = sb("QT_hi", [P, 2, SEQ], F32R), sb("QT_lo", [P, 2, SEQ], F32R)
    KT_hi, KT_lo = sb("KT_hi", [P, 2, SEQ], F32R), sb("KT_lo", [P, 2, SEQ], F32R)
    V_hi, V_lo = sb("V_hi", [P, 2, ST, VH], F32R), sb("V_lo", [P, 2, ST, VH], F32R)
    qf, rot = sb("qf", [P, 2, HALF]), sb("rot", [P, 2, HALF])
    prob = sb("prob", [P, 2, SEQ])
    PT_hi, PT_lo = sb("PT_hi", [P, 2, ST, 2 * P], F32R), sb("PT_lo", [P, 2, ST, 2 * P], F32R)
    mx, nmx, tot, inv = (sb(n, [P, 2]) for n in ("mx", "nmx", "tot", "inv"))
    names = "kr_rot raw_in w_hi w_lo proj proj_act proj_dve rot q_sum q_hi q_lo kr kr_hi kr_lo scores mx nmx exp inv norm tr tr_hi tr_lo pv av_hi av_lo".split()
    s = {n: sem(n) for n in names}
    w_uq, w_ukv = w["w_uq"][0].rearrange("(k p) f -> p k f", p=P), w["w_ukv"][0]
    half_r = ROPE // 2
    C, S = slice(64, 96), slice(96, 128)
    hs = lambda x: slice(x * HALF, (x + 1) * HALF)
    bank = psum[:, 7, :]
    two = lambda ap: ap.rearrange("p (a b) -> p a b", a=2)
    tbank = lambda b: psum[:, 4 + b, :].rearrange("p (k q) -> p k q", k=4)
    pt = lambda a, qt, b: a[:, qt // 2 % 2, 4 * b:4 * b + 4, qt % 2 * P:(qt % 2 + 1) * P]
    pv_out = lambda j: psum[0:VH, 6, j % 2 * 256:j % 2 * 256 + 256]
    block = ctx.enter_context(nc.Block())

    def heads(step_of_head):
        def run(eng):
            for h in (0, 1):
                step_of_head(h, h // 2, h % 2)
            with eng.Fori(1, HEADS // 2 - 1) as q:
                for par in (0, 1):
                    step_of_head(q * 2 + par, q, par)
            for h in (HEADS - 2, HEADS - 1):
                step_of_head(h, h // 2, h % 2)
        return run

    def is_first(h):
        return isinstance(h, int) and h == 0

    def is_last(h):
        return isinstance(h, int) and h == HEADS - 1

    @block.sync
    def _(sp):
        def load(n):
            if not isinstance(n, int) or n > 0:
                sp.wait_ge(s["w_lo"], n)
            nq = n * KD
            sp.dma_start(raw[:, 0:2, 0:KD], w_uq[:, :, bass.ds(nq, KD)]).then_inc(s["raw_in"], 16)
            sp.dma_start(raw[:, 0:2, KD:KD + half_r], w_uq[:, :, bass.ds(nq + NOPE + half_r, half_r)]).then_inc(s["raw_in"], 16)
            sp.dma_start(raw[:, 0:2, KD + half_r:P], w_uq[:, :, bass.ds(nq + NOPE, half_r)]).then_inc(s["raw_in"], 16)
            sp.dma_start(raw[:, 2, :], w_ukv[:, bass.ds(n * P, P)]).then_inc(s["raw_in"], 16)
        load(0)
        with sp.Fori(1, HEADS) as n:
            load(n)

    def proj_mm(pe, n, x, par):
        job = n * 5 + x
        if not (isinstance(n, int) and n == 0 and x == 0):
            pe.wait_ge(s["proj_act"], job)
            pe.wait_ge(s["proj_dve"], job)
        if x == 0:
            pe.wait_ge(s["w_lo"], n + 1)
        if x < 2:
            for k in range(2):
                mm = three_passes(pe, bank, w_hi[:, k, :], w_lo[:, k, :], lT_hi[:, k, hs(x)], lT_lo[:, k, hs(x)], k == 0, k == 1)
        elif x < 4:
            mm = three_passes(pe, bank[0:NOPE], w_hi[:, 2, 0:NOPE], w_lo[:, 2, 0:NOPE], lT_hi[:, 2, hs(x - 2)], lT_lo[:, 2, hs(x - 2)], True, True)
        else:
            for m in range(ST):
                sl = slice(m * P, (m + 1) * P)
                mm = three_passes(pe, bank[:, m * VH:(m + 1) * VH], lT_hi[:, 2, sl], lT_lo[:, 2, sl],
                                  w_hi[:, 2, NOPE:], w_lo[:, 2, NOPE:], True, True)
        mm.then_inc(s["proj"], 1)

    def scores(pe, h, qt, par):
        g = h * 8 + qt
        if qt == 0:
            pe.wait_ge(s["q_lo"], h * 2 + 2)
            pe.wait_ge(s["proj_dve"], h * 5 + 5)
        if not (isinstance(h, int) and g < 2):
            pe.wait_ge(s["exp"], g - 1)
        for half in range(2):
            mm = three_passes(pe, psum[:, 2 * (qt % 2) + half, :], QT_hi[0:KD, par, qt * P:(qt + 1) * P], QT_lo[0:KD, par, qt * P:(qt + 1) * P],
                              KT_hi[0:KD, par, hs(half)], KT_lo[0:KD, par, hs(half)], True, True)
        mm.then_inc(s["scores"], 1)

    def turn(pe, g, qt):
        pe.wait_ge(s["norm"], g + 1)
        for b in range(2):
            if not (isinstance(g, int) and g == 0):
                pe.wait_ge(s["tr_lo"], g * 2 - 1 + b)
            for k in range(4):
                t = pe.transpose(psum[:, 4 + b, k * P:(k + 1) * P], prob[:, qt % 2, (4 * b + k) * P:(4 * b + k + 1) * P], ident[:])
            t.then_inc(s["tr"], 1)

    def values(pe, jj, j, par):
        pe.wait_ge(s["tr_lo"], jj * 4 + 4)
        if not (isinstance(jj, int) and jj < 2):
            pe.wait_ge(s["av_lo"], jj - 1)
        for k in range(ST):
            mm = three_passes(pe, pv_out(j), V_hi[:, par, k, :], V_lo[:, par, k, :], PT_hi[:, j % 2, k, :], PT_lo[:, j % 2, k, :], k == 0, k == ST - 1)
        mm.then_inc(s["pv"], 1)

    @block.tensor
    def _(pe):
        for x in range(5):
            proj_mm(pe, 0, x, 0)
        pe.wait_ge(s["kr_lo"], 2)

        def head(h, q, par):
            for qt in range(ST):
                scores(pe, h, qt, par)
                if qt >= 2 or not is_first(h):
                    turn(pe, h * 8 + qt - 2, (qt - 2) % ST)
                if qt % 2 == 0 and (qt >= 4 or not is_first(h)):
                    values(pe, h * 4 + qt // 2 - 2, (qt // 2 - 2) % 4, par if qt >= 4 else 1 - par)
                if not is_last(h) and 1 <= qt <= 5:
                    proj_mm(pe, h + 1, qt - 1, 1 - par)
        heads(head)(pe)
        N = HEADS * ST
        turn(pe, N - 2, ST - 2)
        values(pe, N // 2 - 2, 2, 1)
        turn(pe, N - 1, ST - 1)
        values(pe, N // 2 - 1, 3, 1)

    @block.scalar
    def _(act):
        def split(n):
            act.wait_ge(s["raw_in"], n * 64 + 64)
            if not isinstance(n, int) or n > 0:
                act.wait_ge(s["proj"], n * 5)
            act.copy(w_hi[:], raw[:]).then_inc(s["w_hi"], 1)

        def project(n, x, par):
            act.wait_ge(s["proj"], n * 5 + x + 1)
            if x < 2:
                if not (isinstance(n, int) and n == 0):
                    act.wait_ge(s["q_lo"], n * 2 + x - 1)
                act.copy(qf[0:NOPE, x, :], bank[0:NOPE]).then_inc(s["proj_act"], 1)
            elif x < 4:
                if not (isinstance(n, int) and n < 2):
                    act.wait_ge(s["scores"], n * 8 - 8)
                act.copy(KT_hi[0:NOPE, par, hs(x - 2)], bank[0:NOPE]).then_inc(s["proj_act"], 1)
            else:
                if not (isinstance(n, int) and n < 2):
                    act.wait_ge(s["pv"], n * 4 - 4)
                act.copy(V_hi[:, par], bank.rearrange("p (m v) -> p m v", m=ST)).then_inc(s["proj_act"], 1)

        def queries(n, x, par):
            act.wait_ge(s["q_sum"], n * 2 + x + 1)
            act.wait_ge(s["proj_act"], n * 5 + x + 1)
            if not (isinstance(n, int) and n < 2):
                act.wait_ge(s["scores"], n * 8 - 8)
            act.copy(QT_hi[0:KD, par, hs(x)], qf[0:KD, x, :]).then_inc(s["q_hi"], 1)

        def turned(g, qt, jj):
            if qt % 2 == 0 and not (isinstance(jj, int) and jj < 2):
                act.wait_ge(s["pv"], jj - 1)
            for b in range(2):
                act.wait_ge(s["tr"], g * 2 + b + 1)
                act.copy(pt(PT_hi, qt, b), tbank(b)).then_inc(s["tr_hi"], 1)

        def exponential(g, qt):
            act.wait_ge(s["nmx"], g + 1)
            if not (isinstance(g, int) and g < 2):
                act.wait_ge(s["tr"], g * 2 - 2)
                act.wait_ge(s["inv"], g - 1)
            sl = qt % 2
            act.activation(two(prob[:, sl, :]), psum[:, 2 * sl:2 * sl + 2, :], ACT.Exp, bias=nmx[:, sl:sl + 1], scale=SCALE,
                           accum_out=tot[:, sl:sl + 1]).then_inc(s["exp"], 1)

        def attended(jj, j, hpar, hq):
            act.wait_ge(s["pv"], jj + 1)
            act.copy(aT_hi[hpar * VH:(hpar + 1) * VH, bass.ds(hq, 1), j * 256:(j + 1) * 256].rearrange("p a q -> p (a q)"), pv_out(j)).then_inc(s["av_hi"], 1)

        split(0)
        act.wait_ge(s["kr"], 1)
        for par in range(2):
            act.copy(KT_hi[C, par, :], krT[C, :]).then_inc(s["kr_hi"], 1)
        for x in range(5):
            project(0, x, 0)
            if x < 2:
                queries(0, x, 0)
        split(1)

        def head(h, q, par):
            for qt in range(ST):
                if qt % 2 == 1 and (qt >= 5 or not is_first(h)):
                    j = (qt // 2 - 2) % 4
                    same = qt >= 5
                    attended(h * 4 + qt // 2 - 2, j, par if same else 1 - par, q if same or par else q - 1)
                if not is_last(h) and 2 <= qt <= 6:
                    project(h + 1, qt - 2, 1 - par)
                if not is_last(h) and 3 <= qt <= 4:
                    queries(h + 1, qt - 3, 1 - par)
                if qt >= 2 or not is_first(h):
                    turned(h * 8 + qt - 2, (qt - 2) % ST, h * 4 + (qt - 2) // 2)
                exponential(h * 8 + qt, qt)
                if qt == 7 and not (isinstance(h, int) and h >= HEADS - 2):
                    split(h + 2)
        heads(head)(act)
        N = HEADS * ST
        turned(N - 2, ST - 2, N // 2 - 1)
        attended(N // 2 - 2, 2, 1, HEADS // 2 - 1)
        turned(N - 1, ST - 1, N // 2 - 1)
        attended(N // 2 - 1, 3, 1, HEADS // 2 - 1)

    @block.vector
    def _(dve):
        def split(n):
            dve.wait_ge(s["w_hi"], n + 1)
            dve.tensor_tensor(w_lo[:], raw[:], w_hi[:].bitcast(F32), ALU.subtract).then_inc(s["w_lo"], 1)

        def project(n, x, par):
            dve.wait_ge(s["proj"], n * 5 + x + 1)
            if x < 2:
                if not (isinstance(n, int) and n == 0):
                    dve.wait_ge(s["q_lo"], n * 2 + x - 1)
                dve.wait_ge(s["proj_act"], n * 5 + x + 1)
                dve.tensor_tensor(rot[C, x, :], bank[S], trig[S, hs(x)], ALU.mult).then_inc(s["rot"], 1)
                dve.tensor_tensor(qf[C, x, :], bank[C], trig[C, hs(x)], ALU.mult).then_inc(s["proj_dve"], 1)
            else:
                dve.wait_ge(s["proj_act"], n * 5 + x + 1)
                if x < 4:
                    dve.tensor_tensor(KT_lo[0:NOPE, par, hs(x - 2)], bank[0:NOPE], KT_hi[0:NOPE, par, hs(x - 2)].bitcast(F32), ALU.subtract).then_inc(s["proj_dve"], 1)
                else:
                    dve.tensor_tensor(V_lo[:, par].rearrange("p m v -> p (m v)"), bank, V_hi[:, par].rearrange("p m v -> p (m v)").bitcast(F32), ALU.subtract).then_inc(s["proj_dve"], 1)

        def maximum(g, qt):
            sl = qt % 2
            dve.wait_ge(s["scores"], g + 1)
            if not (isinstance(g, int) and g < 2):
                dve.wait_ge(s["nmx"], g - 1)
            dve.tensor_reduce(mx[:, sl:sl + 1], psum[:, 2 * sl:2 * sl + 2, :], AX.XY, ALU.max).then_inc(s["mx"], 1)
            dve.wait_ge(s["mx"], g + 1)
            dve.tensor_scalar(nmx[:, sl:sl + 1], mx[:, sl:sl + 1], -SCALE, None, ALU.mult).then_inc(s["nmx"], 1)

        def turned(g, qt):
            for b in range(2):
                dve.wait_ge(s["tr_hi"], g * 2 + b + 1)
                dve.tensor_tensor(pt(PT_lo, qt, b), tbank(b), pt(PT_hi, qt, b).bitcast(F32), ALU.subtract).then_inc(s["tr_lo"], 1)

        def inverse(g, qt):
            sl = qt % 2
            dve.wait_ge(s["exp"], g + 1)
            if not (isinstance(g, int) and g < 2):
                dve.wait_ge(s["norm"], g - 1)
            dve.reciprocal(inv[:, sl:sl + 1], tot[:, sl:sl + 1]).then_inc(s["inv"], 1)

        def attended(jj, j, hpar, hq):
            dst = lambda a: a[hpar * VH:(hpar + 1) * VH, bass.ds(hq, 1), j * 256:(j + 1) * 256].rearrange("p a q -> p (a q)")
            dve.wait_ge(s["av_hi"], jj + 1)
            dve.tensor_tensor(dst(aT_lo), pv_out(j), dst(aT_hi).bitcast(F32), ALU.subtract).then_inc(s["av_lo"], 1)

        dve.tensor_tensor(rot[C].rearrange("p a b -> p (a b)"), krT[S], trig[S], ALU.mult).then_inc(s["kr_rot"], 1)
        dve.tensor_tensor(krT[C], krT[C], trig[C], ALU.mult).then_inc(s["kr_rot"], 1)
        dve.wait_ge(s["kr_rot"], 2)
        dve.tensor_tensor(krT[C], krT[C], rot[C].rearrange("p a b -> p (a b)"), ALU.add).then_inc(s["kr"], 1)
        for par in range(2):
            dve.wait_ge(s["kr_hi"], par + 1)
            dve.tensor_tensor(KT_lo[C, par, :], krT[C, :], KT_hi[C, par, :].bitcast(F32), ALU.subtract).then_inc(s["kr_lo"], 1)
        split(0)
        for x in range(5):
            project(0, x, 0)
        split(1)

        def head(h, q, par):
            for qt in range(ST):
                if qt % 2 == 1 and (qt >= 5 or not is_first(h)):
                    j = (qt // 2 - 2) % 4
                    same = qt >= 5
                    attended(h * 4 + qt // 2 - 2, j, par if same else 1 - par, q if same or par else q - 1)
                if not is_last(h) and 2 <= qt <= 6:
                    project(h + 1, qt - 2, 1 - par)
                maximum(h * 8 + qt, qt)
                if qt >= 2 or not is_first(h):
                    turned(h * 8 + qt - 2, (qt - 2) % ST)
                inverse(h * 8 + qt, qt)
                if qt == 7 and not (isinstance(h, int) and h >= HEADS - 2):
                    split(h + 2)
        heads(head)(dve)
        N = HEADS * ST
        turned(N - 2, ST - 2)
        attended(N // 2 - 2, 2, 1, HEADS // 2 - 1)
        turned(N - 1, ST - 1)
        attended(N // 2 - 1, 3, 1, HEADS // 2 - 1)

    @block.gpsimd
    def _(pool):
        def queries(n, x, par):
            if not (isinstance(n, int) and n == 0 and x == 0):
                pool.wait_ge(s["q_lo"], n * 2 + x)
            if not (isinstance(n, int) and n == 0):
                pool.wait_ge(s["norm"], n * 8 + x - 5)
            pool.wait_ge(s["rot"], n * 2 + x + 1)
            pool.wait_ge(s["proj_dve"], n * 5 + x + 1)
            pool.tensor_tensor(qf[C, x, :], qf[C, x, :], rot[C, x, :], ALU.add).then_inc(s["q_sum"], 1)
            pool.wait_ge(s["q_hi"], n * 2 + x + 1)
            pool.tensor_tensor(QT_lo[0:KD, par, hs(x)], qf[0:KD, x, :], QT_hi[0:KD, par, hs(x)].bitcast(F32), ALU.subtract).then_inc(s["q_lo"], 1)

        def normalise(g, qt):
            pool.wait_ge(s["inv"], g + 1)
            pool.tensor_tensor(prob[:, qt % 2, :], prob[:, qt % 2, :], inv[:, qt % 2:qt % 2 + 1].broadcast_to([P, SEQ]), ALU.mult).then_inc(s["norm"], 1)

        for x in range(2):
            queries(0, x, 0)

        def head(h, q, par):
            for qt in range(ST):
                if not is_last(h) and 3 <= qt <= 4:
                    queries(h + 1, qt - 3, 1 - par)
                normalise(h * 8 + qt, qt)
        heads(head)(pool)


def merge_phase(nc, w, psum, rows, aT_hi, aT_lo, gates, partial):
    with Phase(nc) as ctx:
        sb, sem = tools(nc, ctx, "mg")
        mT_hi, mT_lo = sb("mT_hi", [P, KT, SEQ], F32R), sb("mT_lo", [P, KT, SEQ], F32R)
        gate, part, val = sb("gate", [P, 2, SEQ]), sb("part", [P, 2, SEQ]), sb("val", [P, 2, SEQ])
        woa = ColumnProduct(nc, ctx, "woa", w["w_o_attn"][0], [n * P for n in range(KT)], aT_hi, aT_lo, psum)
        lhs = lambda j, k, m: (mT_hi[:, k, m * P:(m + 1) * P], mT_lo[:, k, m * P:(m + 1) * P])
        w_out = w["w_out"][0]
        rp = RowProduct(nc, ctx, "wo", [(w_out, [(0, slice(j * HALF, (j + 1) * HALF))], HALF) for j in range(2)], lhs, psum)
        s_g, s_p = [sem("g0"), sem("g1")], [sem("p0"), sem("p1")]
        s_sum, s_hi, s_lo = sem("sum"), sem("hi"), sem("lo")
        NU = len(rp.units())
        two = lambda ap: ap.rearrange("p (a b) -> p a b", a=2)
        block = ctx.enter_context(nc.Block())

        def add(dve, j, m):
            rp.wait_bank(dve, j, m)
            sl = slice(j * HALF, (j + 1) * HALF)
            dve.tensor_tensor(rows[:, m, sl], psum[:, m, :], rows[:, m, sl], ALU.add).then_inc(rp.read, 1)

        @block.sync
        def _(sp):
            for n in range(KT):
                woa.load(sp, n)
                if n >= 2:
                    sp.wait_ge(s_sum, n - 1)
                sp.dma_start(gate[:, n % 2, :], gates[n * P:(n + 1) * P, :]).then_inc(s_g[n % 2], 16)
                sp.dma_start(part[:, n % 2, :], partial[n * P:(n + 1) * P, :]).then_inc(s_p[n % 2], 16)
            for n in range(NU):
                rp.load(sp, n)

        @block.scalar
        def _(act):
            woa.high(act, 0)
            woa.high(act, 1)
            for n in range(KT):
                woa.high(act, n + 2)
                act.wait_ge(s_sum, n + 1)
                act.copy(mT_hi[:, n, :], val[:, n % 2, :]).then_inc(s_hi, 1)
            for n in range(NU):
                rp.high(act, n)

        @block.vector
        def _(dve):
            woa.low(dve, 0)
            woa.low(dve, 1)
            for n in range(KT):
                dve.wait_ge(woa.mm_done, n + 1)
                dve.wait_ge(s_g[n % 2], 16 * (n // 2 + 1))
                if n >= 2:
                    dve.wait_ge(s_lo, n - 1)
                dve.tensor_tensor(two(val[:, n % 2, :]), woa.ps[n % 2], two(gate[:, n % 2, :]), ALU.mult).then_inc(woa.read[n % 2], 1)
                woa.low(dve, n + 2)
                dve.wait_ge(woa.read[n % 2], n // 2 + 1)
                dve.wait_ge(s_p[n % 2], 16 * (n // 2 + 1))
                dve.tensor_tensor(val[:, n % 2, :], val[:, n % 2, :], part[:, n % 2, :], ALU.add).then_inc(s_sum, 1)
                dve.wait_ge(s_hi, n + 1)
                dve.tensor_tensor(mT_lo[:, n, :], val[:, n % 2, :], mT_hi[:, n, :].bitcast(F32), ALU.subtract).then_inc(s_lo, 1)
            for j in range(2):
                for k in range(KT):
                    rp.low(dve, j * KT + k)
                    if j and k == 1:
                        for m in range(ST):
                            add(dve, 0, m)
            for m in range(ST):
                add(dve, 1, m)

        @block.tensor
        def _(pe):
            for n in range(KT):
                woa.product(pe, n)
            pe.wait_ge(s_lo, KT)
            rp.products(pe)


def final_phase(nc, w, psum, rows, out):
    with Phase(nc) as ctx:
        sb, sem = tools(nc, ctx, "fi")
        gb, stat, o = sb("gb", [P, D]), sb("stat", [P, 5, ST]), sb("o", [P, ST, D])
        s_g, s_sq, s_var, s_sqrt, s_link, s_o, s_out = map(sem, ("g", "sq", "var", "sqrt", "link", "o", "out"))
        block = ctx.enter_context(nc.Block())

        @block.sync
        def _(sp):
            sp.dma_start(gb[:], w["final_norm"].rearrange("(a d) -> a d", a=1).broadcast_to([P, D])).then_inc(s_g, 16)
            for m in range(ST):
                sp.wait_ge(s_o, m + 1)
                sp.dma_start(out[0, m * P:(m + 1) * P, :], o[:, m, :]).then_inc(s_out, 16)
            sp.wait_ge(s_out, 16 * ST)

        @block.scalar
        def _(act):
            for m in range(ST):
                act.activation(o[:, m, :], rows[:, m, :], ACT.Square, accum_out=stat[:, 0, m:m + 1]).then_inc(s_sq, 1)
            act.wait_ge(s_var, 1)
            act.activation(stat[:, 2, :], stat[:, 1, :], ACT.Sqrt).then_inc(s_sqrt, 1)

        @block.vector
        def _(dve):
            dve.wait_ge(s_sq, ST)
            dve.tensor_scalar(stat[:, 1, :], stat[:, 0, :], 1.0 / D, EPS, ALU.mult, ALU.add).then_inc(s_var, 1)
            dve.wait_ge(s_sqrt, 1)
            newton(Chain(dve, s_link), stat[:, 1, :], stat[:, 2, :], stat[:, 3, :], stat[:, 4, :])
            dve.wait_ge(s_g, 16)
            for m in range(ST):
                dve.scalar_tensor_tensor(out=o[:, m, :], in0=rows[:, m, :], scalar=stat[:, 3, m:m + 1], in1=gb[:], op0=ALU.mult, op1=ALU.mult).then_inc(s_o, 1)


def build(nc, w, out):
    gates = nc.dram_tensor("gates", [2 * D, SEQ], F32, kind="Internal").ap()
    partial = nc.dram_tensor("partial", [D, SEQ], F32, kind="Internal").ap()
    with ExitStack() as ctx:
        rows = ctx.enter_context(nc.sbuf_tensor("rows", [P, ST, D], F32))
        ident = ctx.enter_context(nc.sbuf_tensor("ident", [P, P], F32))
        psum = ctx.enter_context(nc.psum_tensor("psum", [P, 8, HALF], F32))
        make_ident(nc, ident, ctx.enter_context(nc.semaphore("ident_done")))
        ffn_phase(nc, "f1", w["ffn1_norm"][0], w["ffn1_w_gate"][0], w["ffn1_w_up"][0], w["ffn1_w_down"][0], rows, ident, psum, x=w["x"][0])
        with ExitStack() as latent:
            zrow = latent.enter_context(nc.sbuf_tensor("zrow", [P, ST, ZW], F32))
            with ExitStack() as inner:
                u = inner.enter_context(nc.sbuf_tensor("u", [P, GROUPS, T, SG], F32))
                project_phase(nc, w, rows, ident, psum, zrow, u, gates)
                with Phase(nc) as ssm:
                    ssm_phase(nc, w, ident, psum, u, ssm)
                glu_phase(nc, w, ident, psum, u, gates, partial)
            with ExitStack() as inner:
                aT_hi = inner.enter_context(nc.sbuf_tensor("aT_hi", [P, HEADS // 2, SEQ], F32R))
                aT_lo = inner.enter_context(nc.sbuf_tensor("aT_lo", [P, HEADS // 2, SEQ], F32R))
                attention_phase(nc, w, ident, psum, zrow, aT_hi, aT_lo)
                merge_phase(nc, w, psum, rows, aT_hi, aT_lo, gates, partial)
        ffn_phase(nc, "f2", w["ffn2_norm"][0], w["ffn2_w_gate"][0], w["ffn2_w_up"][0], w["ffn2_w_down"][0], rows, ident, psum)
        final_phase(nc, w, psum, rows, out)


INPUTS = ["x", "positions", "ffn1_norm", "ffn1_w_gate", "ffn1_w_up", "ffn1_w_down", "mix_norm", "w_in", "q_norm", "w_uq", "kv_norm",
          "w_ukv", "w_o_attn", "ssm_lambda_re", "ssm_lambda_im", "ssm_log_dt", "ssm_b_re", "ssm_b_im", "ssm_c_re", "ssm_c_im",
          "ssm_d", "w_glu", "b_glu", "w_o_ssm", "w_out", "ffn2_norm", "ffn2_w_gate", "ffn2_w_up", "ffn2_w_down", "final_norm"]


def rope_const():
    half = ROPE // 2
    freq = (np.float32(10000.0) ** (-np.arange(0, ROPE, 2, dtype=np.float32) / np.float32(ROPE))).astype(np.float32)
    sign = np.ones(P, np.float32)
    sign[P - ROPE:P - half] = -1.0
    return np.stack([np.tile(freq, P // half), sign], axis=1)


def kernel(**inputs):
    import concourse.bacc as bacc
    from concourse.bass_utils import run_bass_kernel_spmd

    nc = bacc.Bacc("TRN2", target_bir_lowering=False, num_devices=1)
    arrays = {name: np.ascontiguousarray(inputs[name]) for name in INPUTS}
    arrays["rope_const"] = rope_const()
    w = {name: nc.dram_tensor(name, a.shape, mybir.dt.from_np(a.dtype), kind="ExternalInput").ap() for name, a in arrays.items()}
    out = nc.dram_tensor("out", (1, SEQ, D), F32, kind="ExternalOutput").ap()
    build(nc, w, out)
    r = run_bass_kernel_spmd(nc, [arrays], core_ids=[0])
    return r.results[0]["out"]
```

```python
import math
from contextlib import ExitStack

import numpy as np
import concourse.bass as bass
from concourse import mybir

F32 = mybir.dt.float32
F32R = mybir.dt.float32r
I32 = mybir.dt.int32
ALU = mybir.AluOpType
ACT = mybir.ActivationFunctionType
AX = mybir.AxisListType


def two_pi_parts():
    rest, parts = 2 * math.pi, []
    for _ in range(3):
        unit = 2.0 ** (math.floor(math.log2(rest)) - 7)
        parts.append(math.floor(rest / unit) * unit)
        rest -= parts[-1]
    return parts + [float(np.float32(rest))]


P = 128
SEQ = 1024
D = 1024
F = 2816
ST = SEQ // P
KT = D // P
HALF = 512
EPS = 1e-6
ROUND = 1.5 * 2.0 ** 23
TWO_PI_PARTS = two_pi_parts()
PI_DOWN = 3.1415925


def three_passes(pe, out, lhs_hi, lhs_lo, rhs_hi, rhs_lo, first, last):
    pe.matmul(out, lhs_hi, rhs_hi, start=first, stop=False)
    pe.matmul(out, lhs_hi, rhs_lo, start=False, stop=False)
    return pe.matmul(out, lhs_lo, rhs_hi, start=False, stop=last)


class Phase(ExitStack):

    def __init__(self, nc):
        super().__init__()
        self.taken = []

        def clear():
            if self.taken:
                nc.clear_and_free_semaphores(self.taken)
                nc.all_engine_barrier()
        self.callback(clear)


def semaphores(nc, ctx, tag):
    def sem(name):
        ctx.taken.append(nc.alloc_semaphore(f"{tag}_{name}"))
        return ctx.taken[-1]
    return sem


class Chain:

    def __init__(self, eng, s, n=0):
        self.eng, self.s, self.n = eng, s, n

    def __call__(self, ins):
        self.n += 1
        ins.then_inc(self.s, 1)
        self.eng.wait_ge(self.s, self.n)


def newton(link, var, root, out, tmp):
    dve = link.eng
    link(dve.reciprocal(out, root))
    link(dve.tensor_tensor(tmp, out, out, ALU.mult))
    link(dve.tensor_tensor(tmp, tmp, var, ALU.mult))
    link(dve.tensor_scalar(tmp, tmp, -0.5, 1.5, ALU.mult, ALU.add))
    link(dve.tensor_tensor(out, out, tmp, ALU.mult))


def reduce_angle(link, ang, turns, tmp, quarter):
    dve = link.eng
    link(dve.tensor_scalar(turns, ang, 1.0 / (2 * math.pi), quarter, ALU.mult, ALU.add))
    link(dve.tensor_scalar(turns, turns, ROUND, None, ALU.add))
    link(dve.tensor_scalar(turns, turns, ROUND, None, ALU.subtract))
    for part in TWO_PI_PARTS:
        link(dve.scalar_tensor_tensor(out=ang, in0=turns, scalar=-part, in1=ang, op0=ALU.mult, op1=ALU.add))
    if quarter:
        link(dve.tensor_scalar(ang, ang, math.pi / 2, None, ALU.add))
    link(dve.tensor_scalar(ang, ang, PI_DOWN, -PI_DOWN, ALU.min, ALU.max))


class ColumnProduct:

    def __init__(self, nc, ctx, tag, w, tiles, rhs_hi, rhs_lo, psum, slot0=0, room=None):
        sb = lambda n, s, d=F32: ctx.enter_context(nc.sbuf_tensor(f"{tag}_{n}", s, d))
        sem = semaphores(nc, ctx, tag)
        self.K = w.shape[0] // P
        self.w, self.tiles, self.N = w.rearrange("(k p) f -> p k f", p=P), tiles, len(tiles)
        self.rhs_hi, self.rhs_lo = rhs_hi, rhs_lo
        self.raw = [sb(f"raw{i}", [P, self.K, P]) for i in range(2)]
        if room is None:
            self.hi = sb("hi", [P, 2, self.K, P], F32R)
            self.lo = sb("lo", [P, 2, self.K, P], F32R)
        else:
            size = 2 * self.K * P * 4
            self.hi, self.lo = (nc.alloc_sbuf_tensor_at(f"{tag}_{n}", [P, 2, self.K, P], F32R, offset=room + i * size) for i, n in enumerate(("hi", "lo")))
        self.ps = [psum[:, slot0 + 2 * i:slot0 + 2 * i + 2, :] for i in range(2)]
        self.raw_in = [sem(f"raw_in{i}") for i in range(2)]
        self.hi_done, self.lo_done, self.mm_done = sem("hi_done"), sem("lo_done"), sem("mm_done")
        self.read = [sem(f"read{i}") for i in range(2)]

    def load(self, sp, n):
        if n >= 2:
            sp.wait_ge(self.lo_done, n - 1)
        sp.dma_start(self.raw[n % 2][:], self.w[:, :, self.tiles[n]:self.tiles[n] + P]).then_inc(self.raw_in[n % 2], 16)

    def high(self, act, n):
        if n >= self.N:
            return
        act.wait_ge(self.raw_in[n % 2], 16 * (n // 2 + 1))
        if n >= 2:
            act.wait_ge(self.mm_done, n - 1)
        act.copy(self.hi[:, n % 2], self.raw[n % 2][:]).then_inc(self.hi_done, 1)

    def low(self, dve, n):
        if n >= self.N:
            return
        dve.wait_ge(self.hi_done, n + 1)
        if n >= 2:
            dve.wait_ge(self.mm_done, n - 1)
        dve.tensor_tensor(self.lo[:, n % 2], self.raw[n % 2][:], self.hi[:, n % 2].bitcast(F32), ALU.subtract).then_inc(self.lo_done, 1)

    def product(self, pe, n):
        pe.wait_ge(self.lo_done, n + 1)
        if n >= 2:
            pe.wait_ge(self.read[n % 2], n // 2)
        for half in range(2):
            sl = slice(half * HALF, (half + 1) * HALF)
            for k in range(self.K):
                mm = three_passes(pe, self.ps[n % 2][:, half, :], self.hi[:, n % 2, k, :], self.lo[:, n % 2, k, :],
                                  self.rhs_hi[:, k, sl], self.rhs_lo[:, k, sl], k == 0, k == self.K - 1)
        mm.then_inc(self.mm_done, 1)


class RowProduct:

    def __init__(self, nc, ctx, tag, jobs, lhs, psum):
        sb = lambda n, s, d=F32: ctx.enter_context(nc.sbuf_tensor(f"{tag}_{n}", s, d))
        sem = semaphores(nc, ctx, tag)
        self.jobs, self.lhs, self.psum = jobs, lhs, psum
        self.raw = [sb(f"raw{i}", [P, HALF]) for i in range(2)]
        self.hi = sb("hi", [P, 2, HALF], F32R)
        self.lo = sb("lo", [P, 2, HALF], F32R)
        self.raw_in = [sem(f"raw_in{i}") for i in range(2)]
        self.hi_done, self.lo_done, self.k_done, self.mm_done, self.read = (sem(n) for n in ("hi_done", "lo_done", "k_done", "mm_done", "read"))

    def units(self):
        return [(j, k) for j in range(len(self.jobs)) for k in range(self.jobs[j][0].shape[0] // P)]

    def load(self, sp, n):
        units = self.units()
        w, parts, width = self.jobs[units[n][0]]
        k = units[n][1]
        if n >= 2:
            sp.wait_ge(self.lo_done, n - 1)
        for at, cols in parts:
            sp.dma_start(self.raw[n % 2][:, at:at + cols.stop - cols.start], w[k * P:(k + 1) * P, cols]).then_inc(self.raw_in[n % 2], 16)

    def arrived(self, n):
        units = self.units()
        return sum(16 * len(self.jobs[units[i][0]][1]) for i in range(n % 2, n + 1, 2))

    def high(self, act, n):
        units = self.units()
        if n >= len(units):
            return
        width = self.jobs[units[n][0]][2]
        act.wait_ge(self.raw_in[n % 2], self.arrived(n))
        if n >= 2:
            act.wait_ge(self.k_done, n - 1)
        act.copy(self.hi[:, n % 2, 0:width], self.raw[n % 2][:, 0:width]).then_inc(self.hi_done, 1)

    def low(self, eng, n):
        units = self.units()
        if n >= len(units):
            return
        width = self.jobs[units[n][0]][2]
        eng.wait_ge(self.hi_done, n + 1)
        if n >= 2:
            eng.wait_ge(self.k_done, n - 1)
        eng.tensor_tensor(self.lo[:, n % 2, 0:width], self.raw[n % 2][:, 0:width], self.hi[:, n % 2, 0:width].bitcast(F32), ALU.subtract).then_inc(self.lo_done, 1)

    def products(self, pe, only=None):
        units = self.units()
        for n, (j, k) in enumerate(units):
            if only is not None and j != only:
                continue
            w, parts, width = self.jobs[j]
            last = k == w.shape[0] // P - 1
            pe.wait_ge(self.lo_done, n + 1)
            for m in range(ST):
                if k == 0 and j:
                    pe.wait_ge(self.read, (j - 1) * ST + m + 1)
                hi, lo = self.lhs(j, k, m)
                mm = three_passes(pe, self.psum[:, m, 0:width], hi, lo, self.hi[:, n % 2, 0:width], self.lo[:, n % 2, 0:width], k == 0, last)
                if m == ST - 1:
                    mm.then_inc(self.k_done, 1)
                elif last:
                    mm.then_inc(self.mm_done, 1)

    def wait_bank(self, eng, j, m):
        if m < ST - 1:
            eng.wait_ge(self.mm_done, j * (ST - 1) + m + 1)
        else:
            eng.wait_ge(self.k_done, sum(1 for u in self.units() if u[0] <= j))


class Norm:

    def __init__(self, nc, ctx, tag, gain, rows, ident, nT_hi, nT_lo, psum):
        sb = lambda n, s, d=F32: ctx.enter_context(nc.sbuf_tensor(f"{tag}_{n}", s, d))
        sem = semaphores(nc, ctx, tag)
        self.gain, self.rows, self.ident = gain, rows, ident
        self.hi, self.lo, self.psum = nT_hi, nT_lo, psum
        self.gb = sb("gb", [P, D])
        self.xn = sb("xn", [P, 2, D])
        self.stat = sb("stat", [P, 5, ST])
        self.s_gain, self.s_sq, self.s_var, self.s_sqrt, self.s_rstd = map(sem, ("gain", "sq", "var", "sqrt", "rstd"))
        self.s_xn, self.s_tr, self.s_hi, self.s_lo = map(sem, ("xn", "tr", "nhi", "nlo"))

    def load(self, sp):
        sp.dma_start(self.gb[:], self.gain.rearrange("(a d) -> a d", a=1).broadcast_to([P, D])).then_inc(self.s_gain, 16)

    def act_squares(self, act, rows_ready):
        for m in range(ST):
            rows_ready(act, m)
            if m >= 4:
                act.wait_ge(self.s_sq, m - 3)
            act.activation(self.psum[:, 2 * (m % 4):2 * (m % 4) + 2, :], self.rows[:, m, :].rearrange("p (a b) -> p a b", a=2), ACT.Square,
                           accum_out=self.stat[:, 0, m:m + 1]).then_inc(self.s_sq, 1)
        act.wait_ge(self.s_var, 1)
        act.activation(self.stat[:, 2, :], self.stat[:, 1, :], ACT.Sqrt).then_inc(self.s_sqrt, 1)

    def dve_rstd(self, dve):
        st, s = self.stat, self.s_rstd
        dve.wait_ge(self.s_sq, ST)
        dve.tensor_scalar(st[:, 1, :], st[:, 0, :], 1.0 / D, EPS, ALU.mult, ALU.add).then_inc(self.s_var, 1)
        dve.wait_ge(self.s_sqrt, 1)
        newton(Chain(dve, s), st[:, 1, :], st[:, 2, :], st[:, 3, :], st[:, 4, :])

    def dve_rows(self, dve, m):
        if m == 0:
            dve.wait_ge(self.s_gain, 16)
        if m >= 2:
            dve.wait_ge(self.s_tr, m - 1)
        dve.scalar_tensor_tensor(out=self.xn[:, m % 2, :], in0=self.rows[:, m, :], scalar=self.stat[:, 3, m:m + 1],
                                 in1=self.gb[:], op0=ALU.mult, op1=ALU.mult).then_inc(self.s_xn, 1)

    def dve_low(self, dve, m):
        sl = slice(m * P, (m + 1) * P)
        dve.wait_ge(self.s_hi, m + 1)
        ps = self.psum[:, 2 * (m % 4):2 * (m % 4) + 2, :].rearrange("p a (k s) -> p (a k) s", s=P)
        dve.tensor_tensor(self.lo[:, :, sl], ps, self.hi[:, :, sl].bitcast(F32), ALU.subtract).then_inc(self.s_lo, 1)

    def dve(self, dve):
        self.dve_rstd(dve)
        self.dve_rows(dve, 0)
        for m in range(ST):
            if m + 1 < ST:
                self.dve_rows(dve, m + 1)
            self.dve_low(dve, m)

    def act_high(self, act):
        for m in range(ST):
            act.wait_ge(self.s_tr, m + 1)
            ps = self.psum[:, 2 * (m % 4):2 * (m % 4) + 2, :].rearrange("p a (k s) -> p (a k) s", s=P)
            act.copy(self.hi[:, :, m * P:(m + 1) * P], ps).then_inc(self.s_hi, 1)

    def pe(self, pe):
        pe.wait_ge(self.s_sqrt, 1)
        for m in range(ST):
            pe.wait_ge(self.s_xn, m + 1)
            if m >= 4:
                pe.wait_ge(self.s_lo, m - 3)
            for k in range(KT):
                t = pe.transpose(self.psum[:, 2 * (m % 4) + k // 4, (k % 4) * P:(k % 4 + 1) * P],
                                 self.xn[:, m % 2, k * P:(k + 1) * P], self.ident[:])
            t.then_inc(self.s_tr, 1)


def ffn_phase(nc, tag, gain, w_gate, w_up, w_down, rows, ident, psum, x=None, finish=None):
    NP = F // (2 * P)
    with Phase(nc) as ctx:
        sb = lambda n, s, d=F32: ctx.enter_context(nc.sbuf_tensor(f"{tag}_{n}", s, d))
        sem = semaphores(nc, ctx, tag)
        nT_hi = sb("nT_hi", [P, KT, SEQ], F32R)
        nT_lo = sb("nT_lo", [P, KT, SEQ], F32R)
        norm = Norm(nc, ctx, tag, gain, rows, ident, nT_hi, nT_lo, psum)
        raw = [sb(f"raw{i}", [P, D]) for i in range(3)]
        w_hi = sb("w_hi", [P, 2, 2, D], F32R)
        w_lo = sb("w_lo", [P, 2, 2, D], F32R)
        d_hi = sb("d_hi", [P, 2, D], F32R)
        d_lo = sb("d_lo", [P, 2, D], F32R)
        h = norm.xn
        hT_hi = sb("hT_hi", [P, 2, 2, SEQ], F32R)
        hT_lo = sb("hT_lo", [P, 2, 2, SEQ], F32R)
        x_in = [sem(f"x_in{m}") for m in range(ST if x is not None else 0)]
        raw_in = [sem(f"raw_in{i}") for i in range(3)]
        w_hi_done, w_lo_done = sem("w_hi_done"), sem("w_lo_done")
        gu_done, silu_done, mult_done = sem("gu_done"), sem("silu_done"), sem("mult_done")
        h_hi_done, h_lo_done = sem("h_hi_done"), sem("h_lo_done")
        down_tile, added = sem("down_tile"), sem("added")

        gate_v = w_gate.rearrange("(k p) f -> p k f", p=P)
        up_v = w_up.rearrange("(k p) f -> p k f", p=P)
        ps = lambda slot, half: psum[:, 2 * slot + half, :]
        ps2 = lambda slot: psum[:, 2 * slot:2 * slot + 2, :]
        two = lambda ap: ap.rearrange("p (a b) -> p a b", a=2)

        def gu_units(p):
            return 4 + 6 * (p - 1)

        def down_unit(p):
            return 4 + 6 * p + 4

        block = ctx.enter_context(nc.Block())

        @block.sync
        def _(sp):
            if x is not None:
                for m in range(ST):
                    sp.dma_start(rows[:, m, :], x[m * P:(m + 1) * P, :]).then_inc(x_in[m], 16)
            norm.load(sp)

            def unit(n, slot, src, third):
                if not isinstance(n, int) or n >= 3:
                    sp.wait_ge(w_lo_done, n - 2)
                sp.dma_start(raw[slot][:] if len(src.shape) == 2 else raw[slot][:].rearrange("p (k f) -> p k f", k=KT), src).then_inc(raw_in[slot], 16)

            def gu(p, t, base):
                for j, v in enumerate((gate_v, up_v)):
                    n = base + 2 * t + j
                    unit(n, (slot0 + 2 * t + j) % 3, v[:, :, bass.ds((2 * p + t) * P, P)], None)

            def down(p, base, only=False):
                for j in range(2):
                    n = base + j
                    unit(n, (slotd + j) % 3, w_down[bass.ds((2 * p + j) * P, P), :], None)

            slot0 = 0
            for t in range(2):
                gu(0, t, 0)
            slot0, slotd = 4 % 3, (4 + 4) % 3
            with sp.Fori(0, NP - 1) as p:
                for t in range(2):
                    gu(p + 1, t, p * 6 + 4)
                down(p, p * 6 + 8)
            slotd = (4 + 6 * (NP - 1)) % 3
            down(NP - 1, 4 + 6 * (NP - 1))

        def split_high(act, slot, n3, dst):
            act.wait_ge(raw_in[slot], n3 * 16)
            act.copy(dst, raw[slot][:]).then_inc(w_hi_done, 1)

        def split_low(dve, slot, n, dst, hi):
            dve.wait_ge(w_hi_done, n + 1)
            dve.tensor_tensor(dst, raw[slot][:], hi.bitcast(F32), ALU.subtract).then_inc(w_lo_done, 1)

        @block.scalar
        def _(act):
            norm.act_squares(act, (lambda e, m: e.wait_ge(x_in[m], 16)) if x is not None else (lambda e, m: None))
            norm.act_high(act)
            for t in range(2):
                for j in range(2):
                    n = 2 * t + j
                    split_high(act, n % 3, n // 3 + 1, w_hi[:, t, j, :])

            def pair(p, par, first=False, last=False):
                for t in range(2):
                    tile = p * 2 + t
                    act.wait_ge(gu_done, p * 4 + 2 * t + 1)
                    if not first:
                        act.wait_ge(h_lo_done, p * 2 + t - 1)
                    else:
                        act.wait_ge(norm.s_tr, ST)
                    act.activation(two(h[:, t, :]), ps2(2 * t), ACT.Silu).then_inc(silu_done, 1)
                    if not last:
                        for j in range(2):
                            act.wait_ge(gu_done, p * 4 + 2 * t + 1 + j)
                            u = 2 * t + j + 4
                            split_high(act, u % 3, p * 2 + u // 3 + 1, w_hi[:, t, j, :])
                    act.wait_ge(mult_done, p * 2 + t + 1)
                    if isinstance(p, int) and p < 2:
                        pass
                    else:
                        act.wait_ge(down_tile, p * 8 - 8)
                    act.copy(hT_hi[:, par, t, :], h[:, t, :]).then_inc(h_hi_done, 1)
                if not first:
                    act.wait_ge(down_tile, p * 8)
                for j in range(2):
                    u = 8 + j if not last else 4 + j
                    split_high(act, u % 3, p * 2 + u // 3 + 1, d_hi[:, j, :])

            pair(0, 0, first=True)
            pair(1, 1)
            with act.Fori(1, NP // 2) as q:
                pair(q * 2, 0)
                pair(q * 2 + 1, 1)
            pair(NP - 1, (NP - 1) % 2, last=True)

        @block.vector
        def _(dve):
            norm.dve(dve)
            for t in range(2):
                for j in range(2):
                    n = 2 * t + j
                    split_low(dve, n % 3, n, w_lo[:, t, j, :], w_hi[:, t, j, :])

            def add(q, m):
                dve.wait_ge(down_tile, q * 8 + m + 1)
                dve.scalar_tensor_tensor(out=two(rows[:, m, :]), in0=ps2(m % 4), scalar=0.5, in1=two(rows[:, m, :]),
                                         op0=ALU.mult, op1=ALU.add).then_inc(added, 1)

            def pair(p, par, first=False, last=False):
                base = p * 6 + 4
                for t in range(2):
                    def low(j):
                        if not last:
                            dve.wait_ge(gu_done, p * 4 + 2 * t + 1 + j)
                            u = 2 * t + j
                            split_low(dve, (u + 4) % 3, base + u, w_lo[:, t, j, :], w_hi[:, t, j, :])
                    low(0)
                    dve.wait_ge(silu_done, p * 2 + t + 1)
                    dve.wait_ge(gu_done, p * 4 + 2 * t + 2)
                    dve.tensor_tensor(two(h[:, t, :]), ps2(2 * t + 1), two(h[:, t, :]), ALU.mult).then_inc(mult_done, 1)
                    low(1)
                    dve.wait_ge(h_hi_done, p * 2 + t + 1)
                    dve.tensor_tensor(hT_lo[:, par, t, :], h[:, t, :], hT_hi[:, par, t, :].bitcast(F32), ALU.subtract).then_inc(h_lo_done, 1)
                if not first:
                    for m in range(ST):
                        add(p - 1, m)
                for j in range(2):
                    u = 4 + j if not last else j
                    split_low(dve, (u + 4) % 3, base + u, d_lo[:, j, :], d_hi[:, j, :])

            pair(0, 0, first=True)
            pair(1, 1)
            with dve.Fori(1, NP // 2) as q:
                pair(q * 2, 0)
                pair(q * 2 + 1, 1)
            pair(NP - 1, (NP - 1) % 2, last=True)
            for m in range(ST):
                add(NP - 1, m)

        @block.tensor
        def _(pe):
            norm.pe(pe)
            pe.wait_ge(norm.s_lo, ST)

            def gate_up(p):
                for t in range(2):
                    for j in range(2):
                        if isinstance(p, int) and p == 0:
                            pe.wait_ge(w_lo_done, 2 * t + j + 1)
                        else:
                            pe.wait_ge(w_lo_done, p * 6 + 2 * t + j - 1)
                            pe.wait_ge(mult_done, p * 2 + t - 1)
                            if not isinstance(p, int) or p >= 2:
                                pe.wait_ge(added, p * 8 - 8)
                        for half in range(2):
                            for k in range(KT):
                                mm = three_passes(pe, ps(2 * t + j, half), w_hi[:, t, j, k * P:(k + 1) * P], w_lo[:, t, j, k * P:(k + 1) * P],
                                                  nT_hi[:, k, half * HALF:(half + 1) * HALF], nT_lo[:, k, half * HALF:(half + 1) * HALF],
                                                  k == 0, k == KT - 1)
                        mm.then_inc(gu_done, 1)

            def down(q, par, last=False):
                pe.wait_ge(h_lo_done, q * 2 + 2)
                pe.wait_ge(w_lo_done, q * 6 + 10 if not last else 4 + 6 * (NP - 1) + 2)
                for m in range(ST):
                    if m >= 4:
                        pe.wait_ge(added, q * 8 + m - 3)
                    elif last:
                        pe.wait_ge(added, 8 * (NP - 1) - 4 + m + 1)
                    else:
                        pe.wait_ge(mult_done, q * 2 + 2 + m // 2 + 1)
                    for half in range(2):
                        for t in range(2):
                            mm = three_passes(pe, ps(m % 4, half), hT_hi[:, par, t, m * P:(m + 1) * P], hT_lo[:, par, t, m * P:(m + 1) * P],
                                              d_hi[:, t, half * HALF:(half + 1) * HALF], d_lo[:, t, half * HALF:(half + 1) * HALF],
                                              t == 0, t == 1)
                    mm.then_inc(down_tile, 1)

            gate_up(0)
            gate_up(1)
            down(0, 0)
            with pe.Fori(1, NP // 2) as q:
                gate_up(q * 2)
                down(q * 2 - 1, 1)
                gate_up(q * 2 + 1)
                down(q * 2, 0)
            gate_up(NP - 1)
            down(NP - 2, 1)
            down(NP - 1, 0, last=True)


def make_ident(nc, ident, s_id):
    with nc.Block() as block:
        @block.gpsimd
        def _(pool):
            pool.memset(ident[:], 0.0).then_inc(s_id, 1)
            pool.wait_ge(s_id, 1)
            pool.affine_select(out=ident[:], in_=ident[:], compare_op=ALU.not_equal, fill=1.0, base=0,
                               pattern=[[-1, P]], channel_multiplier=1).then_inc(s_id, 1)


GROUPS, STATE, SG = 32, 64, 16
T = P // SG
CH = SEQ // T
WIDTH = GROUPS * SG
SLOTS = 2 * T - 1
QR, KVR, NOPE, ROPE, VH, HEADS = 256, 128, 64, 32, 64, 8
OFF_CKV = QR
OFF_KR = OFF_CKV + KVR
OFF_U = OFF_KR + ROPE
OFF_GA = OFF_U + WIDTH
OFF_GS = OFF_GA + D
ZW = OFF_KR + 2 * ROPE
GATES_BESIDE_SETUP = 7
TURN_AFTER = (3, 4)
SCALE = (NOPE + ROPE) ** -0.5


def tools(nc, ctx, tag):
    sb = lambda n, s, d=F32: ctx.enter_context(nc.sbuf_tensor(f"{tag}_{n}", s, d))
    return sb, semaphores(nc, ctx, tag)


def project_phase(nc, w, rows, ident, psum, nT_hi, nT_lo, u, kept, latent_rows):
    with Phase(nc) as ctx:
        sb, sem = tools(nc, ctx, "pj")
        zrow = sb("zrow", [P, ST, ZW])
        norm = Norm(nc, ctx, "pjn", w["mix_norm"][0], rows, ident, nT_hi, nT_lo, psum)
        w_in = w["w_in"][0]
        half = ROPE // 2
        latent = [(0, slice(0, OFF_U)), (OFF_U, slice(OFF_KR + half, OFF_U)), (OFF_U + half, slice(OFF_KR, OFF_KR + half))]

        def lhs(j, k, m):
            sl = slice(m * P, (m + 1) * P) if j == 0 else slice(m, SEQ, T)
            return nT_hi[:, k, sl], nT_lo[:, k, sl]

        rp = RowProduct(nc, ctx, "rp", [(w_in, latent, ZW), (w_in, [(0, slice(OFF_U, OFF_GA))], WIDTH)], lhs, psum)
        s_kept, s_latent = sem("kept"), sem("latent")
        NU = len(rp.units())
        block = ctx.enter_context(nc.Block())

        @block.sync
        def _(sp):
            norm.load(sp)
            rp.load(sp, 0)
            rp.load(sp, 1)
            sp.dma_start(kept.rearrange("(m p) d -> p m d", p=P), rows[:]).then_inc(s_kept, 16)
            for n in range(2, NU):
                rp.load(sp, n)
            sp.wait_ge(rp.read, ST)
            sp.dma_start(latent_rows.rearrange("(m p) z -> p m z", p=P), zrow[:]).then_inc(s_latent, 16)
            sp.wait_ge(s_kept, 16)
            sp.wait_ge(s_latent, 16)

        @block.scalar
        def _(act):
            norm.act_squares(act, lambda e, m: None)
            norm.act_high(act)
            for j in range(2):
                for k in range(KT):
                    rp.high(act, j * KT + k)
                    if j == 1 and k == 1:
                        for m in range(ST):
                            rp.wait_bank(act, 0, m)
                            act.copy(zrow[:, m, :], psum[:, m, 0:ZW]).then_inc(rp.read, 1)
            for m in range(ST):
                rp.wait_bank(act, 1, m)
                act.copy(u[:, :, m, :], psum[:, m, :].rearrange("p (g i) -> p g i", i=SG)).then_inc(rp.read, 1)

        @block.vector
        def _(dve):
            norm.dve(dve)
            for n in range(NU):
                rp.low(dve, n)

        @block.tensor
        def _(pe):
            norm.pe(pe)
            pe.wait_ge(norm.s_lo, ST)
            rp.products(pe)


class Gates:

    def __init__(self, nc, ctx, tag, w_in, first, end, nT_hi, nT_lo, psum, gates, sig, room=None):
        sem = semaphores(nc, ctx, tag)
        self.gp = ColumnProduct(nc, ctx, tag, w_in, [OFF_GA + n * P for n in range(first, end)], nT_hi, nT_lo, psum, room=room)
        self.first, self.N, self.gates, self.sig = first, end - first, gates, sig
        self.out = [sem("out0"), sem("out1")]

    def sync(self, sp):
        gp = self.gp
        for n in range(self.N):
            if n + 2 < self.N:
                gp.load(sp, n + 2)
            sp.wait_ge(gp.read[n % 2], n // 2 + 1)
            at = (self.first + n) * P
            sp.dma_start(self.gates[at:at + P, :], self.sig[:, n % 2, :]).then_inc(self.out[n % 2], 16)
        for i in range(2):
            sp.wait_ge(self.out[i], 16 * len(range(i, self.N, 2)))

    def sigmoid(self, act, n):
        gp = self.gp
        act.wait_ge(gp.mm_done, n + 1)
        if n >= 2:
            act.wait_ge(self.out[n % 2], 16 * (n // 2))
        act.activation(self.sig[:, n % 2, :].rearrange("p (a b) -> p a b", a=2), gp.ps[n % 2], ACT.Sigmoid).then_inc(gp.read[n % 2], 1)
        gp.high(act, n + 2)


def ssm_setup_phase(nc, w, ident, psum, nT_hi, nT_lo, gates, E_mat, C_mat, lam8, Bb, C0, tmp):
    with Phase(nc) as ctx:
        sb, sem = tools(nc, ctx, "sa")
        lam_raw = sb("lam_raw", [GROUPS, 2, P])
        ldt = sb("ldt", [P, GROUPS])
        b_raw = sb("b_raw", [P, 2, GROUPS, SG])
        c_raw = sb("c_raw", [P, 2, 4, P])
        lam = sb("lam", [P, 2, GROUPS])
        sc = sb("sc", [P, 9, GROUPS])
        pw = sb("pw", [P, T + 1, 2, GROUPS])
        PP = sb("PP", [P, 2, T, GROUPS])
        sig = sb("sig", [P, 2, SEQ])
        X = [e.rearrange("p g (t i) -> p g t i", i=SG) for e in E_mat]
        side = Gates(nc, ctx, "g1", w["w_in"][0], 0, GATES_BESIDE_SETUP, nT_hi, nT_lo, psum, gates, sig)
        names = "lam b c tr mag ang sin dve xt xe".split()
        s = {n: sem(n) for n in names}
        s_ldt, s_cf, s_negc = sem("ldt_in"), sem("cf"), sem("negc")
        block = ctx.enter_context(nc.Block())

        @block.sync
        def _(sp):
            side.gp.load(sp, 0)
            for c, a in enumerate((w["ssm_lambda_re"], w["ssm_lambda_im"])):
                sp.dma_start(lam_raw[:, c, :].rearrange("g (d p) -> g d p", d=2), a[0].rearrange("d g p -> g d p")).then_inc(s["lam"], 16)
            for d in range(2):
                h = slice(64 * d, 64 * d + 64)
                sp.dma_start(ldt[h, :], w["ssm_log_dt"][0, d:d + 1, :].broadcast_to([64, GROUPS])).then_inc(s_ldt, 16)
                for c, a in enumerate((w["ssm_b_re"], w["ssm_b_im"])):
                    sp.dma_start(b_raw[h, c], a[0, d].rearrange("g p i -> p g i")).then_inc(s["b"], 16)
                for c, a in enumerate((w["ssm_c_re"], w["ssm_c_im"])):
                    sp.dma_start(c_raw[:, c, :, h], a[0, d].rearrange("(b r) i p -> (r i) b p", b=4)).then_inc(s["c"], 16)
            side.gp.load(sp, 1)
            side.sync(sp)

        @block.tensor
        def _(pe):
            pe.wait_ge(s["lam"], 32)
            for c in range(2):
                mm = pe.transpose(psum[:, 4, c * GROUPS:(c + 1) * GROUPS], lam_raw[:, c, :], ident[0:GROUPS, 0:GROUPS])
            mm.then_inc(s["tr"], 1)
            pe.wait_ge(s["c"], 64)
            for c in range(2):
                for b in range(4):
                    mm = pe.transpose(psum[:, 5 + c, b * P:(b + 1) * P], c_raw[:, c, b, :], ident[:])
                mm.then_inc(s["tr"], 1)

            def turn(c):
                pe.wait_ge(s_cf, c + 1)
                if c == 0:
                    pe.wait_ge(s_negc, 2)
                for q in range(8 * c, 8 * c + 8):
                    if q >= 4:
                        pe.wait_ge(s["xe"], q - 3)
                    for g in range(4):
                        mm = pe.transpose(psum[:, 4 + q % 4, g * P:(g + 1) * P], X[c][:, q % 8 * 4 + g, :, :].rearrange("p t i -> p (t i)"), ident[:])
                    mm.then_inc(s["xt"], 1)
            for n in range(side.N):
                side.gp.product(pe, n)
                if n in TURN_AFTER:
                    turn(TURN_AFTER.index(n))

        @block.scalar
        def _(act):
            side.gp.high(act, 0)
            act.wait_ge(s["tr"], 1)
            act.copy(lam[:], psum[:, 4, 0:2 * GROUPS].rearrange("p (c g) -> p c g", c=2)).then_inc(s["mag"], 1)
            act.wait_ge(s_ldt, 32)
            act.activation(sc[:, 0, :], ldt[:], ACT.Exp).then_inc(s["mag"], 1)
            act.wait_ge(s["dve"], 2)
            act.activation(sc[:, 3, :], sc[:, 1, :], ACT.Exp).then_inc(s["mag"], 1)
            side.gp.high(act, 1)
            act.wait_ge(s["tr"], 3)
            act.copy(C0[:, 0].rearrange("p g i -> p (g i)"), psum[:, 5, :]).then_inc(s_negc, 1)
            act.mul(C0[:, 1].rearrange("p g i -> p (g i)"), psum[:, 6, :], -1.0).then_inc(s_negc, 1)
            act.wait_ge(s["ang"], 1)
            act.activation(sc[:, 4:6, :], sc[:, 4:6, :], ACT.Sin).then_inc(s["sin"], 1)
            for n in range(side.N):
                side.sigmoid(act, n)
                if n in TURN_AFTER:
                    c = TURN_AFTER.index(n)
                    for q in range(8 * c, 8 * c + 8):
                        g0 = q % 8 * 4
                        act.wait_ge(s["xt"], q + 1)
                        act.copy(E_mat[c][:, g0:g0 + 4, :], psum[:, 4 + q % 4, :].rearrange("p (g s) -> p g s", g=4)).then_inc(s["xe"], 1)

        @block.gpsimd
        def _(pool):
            for n in range(side.N):
                side.gp.low(pool, n)

        @block.vector
        def _(dve):
            link = Chain(dve, s["dve"])
            mul = lambda o, a, b: link(dve.tensor_tensor(o, a, b, ALU.mult))
            add = lambda o, a, b: link(dve.tensor_tensor(o, a, b, ALU.add))
            sub = lambda o, a, b: link(dve.tensor_tensor(o, a, b, ALU.subtract))
            dve.wait_ge(s["mag"], 2)
            row = lambda i: sc[:, i, :]
            mul(row(1), lam[:, 0], row(0))
            mul(row(2), lam[:, 1], row(0))
            link(dve.tensor_copy(row(4), row(2)))
            link(dve.tensor_copy(row(5), row(2)))
            reduce_angle(link, row(4), row(6), row(7), 0.0)
            reduce_angle(link, row(5), row(6), row(7), 0.25)
            dve.sem_inc(s["ang"], 1)
            dve.wait_ge(s["mag"], 3)
            dve.wait_ge(s["sin"], 1)
            link(dve.memset(pw[:, 0, 0], 1.0))
            link(dve.memset(pw[:, 0, 1], 0.0))
            mul(pw[:, 1, 0], row(3), row(5))
            mul(pw[:, 1, 1], row(3), row(4))
            lre, lim, bre, bim = lam[:, 0], lam[:, 1], pw[:, 1, 0], pw[:, 1, 1]
            mul(row(0), lre, lre)
            mul(row(1), lim, lim)
            add(row(0), row(0), row(1))
            link(dve.reciprocal(row(2), row(0)))
            link(dve.tensor_scalar(row(6), bre, -1.0, None, ALU.add))
            mul(row(7), row(6), lre)
            mul(row(8), bim, lim)
            add(row(7), row(7), row(8))
            mul(row(7), row(7), row(2))
            mul(row(8), bim, lre)
            mul(row(5), row(6), lim)
            sub(row(8), row(8), row(5))
            mul(row(8), row(8), row(2))
            dve.wait_ge(s["b"], 64)
            wide = lambda a: a.unsqueeze(2).broadcast_to([P, GROUPS, SG])
            t0, t1 = (tmp[:, z * WIDTH:(z + 1) * WIDTH].rearrange("p (g i) -> p g i", i=SG) for z in range(2))
            kre, kim = wide(row(7)), wide(row(8))
            mul(t0, b_raw[:, 0], kre)
            mul(t1, b_raw[:, 1], kim)
            sub(Bb[:, 0], t0, t1)
            mul(t0, b_raw[:, 1], kre)
            mul(t1, b_raw[:, 0], kim)
            add(Bb[:, 1], t0, t1)

            def complex_mul(o, a, b, n):
                br, bi = (b[:, i:i + 1, :].broadcast_to([P, n, GROUPS]) for i in range(2))
                x, y = (tmp[:, z * n * GROUPS:(z + 1) * n * GROUPS].rearrange("p (n g) -> p n g", n=n) for z in range(2))
                mul(x, a[:, :, 0], br)
                mul(y, a[:, :, 1], bi)
                sub(o[:, :, 0], x, y)
                mul(x, a[:, :, 0], bi)
                mul(y, a[:, :, 1], br)
                add(o[:, :, 1], x, y)
            complex_mul(pw[:, 2:3], pw[:, 1:2], pw[:, 1], 1)
            complex_mul(pw[:, 3:5], pw[:, 1:3], pw[:, 2], 2)
            complex_mul(pw[:, 5:9], pw[:, 1:5], pw[:, 4], 4)
            for ri in range(2):
                link(dve.tensor_copy(lam8[:, 0, ri], pw[:, T, 0]))
            link(dve.tensor_copy(lam8[:, 1, 0], pw[:, T, 1]))
            link(dve.tensor_scalar(lam8[:, 1, 1], pw[:, T, 1], -1.0, None, ALU.mult))
            F_, B_ = slice(0, 64), slice(64, 128)
            for ri in range(2):
                link(dve.tensor_copy(PP[F_, ri], pw[F_, T - 1::-1, ri]))
                link(dve.tensor_copy(PP[B_, ri], pw[B_, 0:T, ri]))
            power = lambda a: a.rearrange("p t g -> p g t").unsqueeze(3).broadcast_to([P, GROUPS, T, SG])
            chan = lambda a: a.unsqueeze(2).broadcast_to([P, GROUPS, T, SG])

            def outer_product(o, p0, v0, p1, v1, op):
                for half in range(2):
                    g = slice(half * GROUPS // 2, (half + 1) * GROUPS // 2)
                    other = tmp.rearrange("p (g t i) -> p g t i", t=T, i=SG)
                    mul(o[:, g], power(p0)[:, g], chan(v0)[:, g])
                    mul(other, power(p1)[:, g], chan(v1)[:, g])
                    link(dve.tensor_tensor(o[:, g], o[:, g], other, op))
            outer_product(X[0], PP[:, 0], Bb[:, 0], PP[:, 1], Bb[:, 1], ALU.subtract)
            dve.sem_inc(s_cf, 1)
            outer_product(X[1], PP[:, 0], Bb[:, 1], PP[:, 1], Bb[:, 0], ALU.add)
            dve.sem_inc(s_cf, 1)
            for ri in range(2):
                link(dve.tensor_copy(PP[F_, ri], pw[F_, 1:T + 1, ri]))
                link(dve.tensor_copy(PP[B_, ri], pw[B_, T:0:-1, ri]))
            dve.wait_ge(s_negc, 2)
            outer_product(C_mat[0], PP[:, 0], C0[:, 0], PP[:, 1], C0[:, 1], ALU.add)
            outer_product(C_mat[1], PP[:, 0], C0[:, 1], PP[:, 1], C0[:, 0], ALU.subtract)

def ssm_phase(nc, w, rows, rows_at, ident, psum, nT_hi, nT_lo, u, gates, C_mat):
    with ExitStack() as ctx:
        sb = lambda n, s: ctx.enter_context(nc.sbuf_tensor(f"ss_{n}", s, F32))
        lam8 = sb("lam8", [P, 2, 2, GROUPS])
        common = sb("common", [P, GROUPS * CH])
        E_mat = chunk_states(rows)
        part = lambda i: common[:, i * 2 * WIDTH:(i + 1) * 2 * WIDTH].rearrange("p (c g i) -> p c g i", c=2, i=SG)
        Bb, C0 = part(0), part(1)
        rest = common[:, 4 * WIDTH:]
        ssm_setup_phase(nc, w, ident, psum, nT_hi, nT_lo, gates, E_mat, C_mat, lam8, Bb, C0, rest)
        UT = common[:].rearrange("p (g c) -> p g c", g=GROUPS)
        with ExitStack() as inner:
            M = inner.enter_context(nc.sbuf_tensor("ss_M", [P, GROUPS, P], F32))
            with Phase(nc) as step:
                chunk_matrices(nc, step, psum, M, C_mat, Bb, C0, rest)
            with Phase(nc) as step:
                within_chunks(nc, step, w, ident, psum, u, M, UT)
        H = sb("H", [P, CH + 1, 2, GROUPS])
        with Phase(nc) as step:
            scan_chunks(nc, step, w, rows, rows_at, psum, nT_hi, nT_lo, gates, E_mat, UT, lam8, H)
        with Phase(nc) as step:
            chunk_outputs(nc, step, psum, u, UT, H, chunk_states(rows), C_mat)


def chunk_states(rows):
    return [rows[:, c * ST // 2:(c + 1) * ST // 2, :].rearrange("p a (b s) -> p (a b) s", s=P) for c in range(2)]


def chunk_matrices(nc, ctx, psum, M, C_mat, Bb, C0, rest):
    sb, sem = tools(nc, ctx, "sc")
    kern = sb("kern", [SG, GROUPS, SLOTS * SG])
    Bz = rest.rearrange("p (d c g i) -> p d c g i", d=2, c=2, i=SG)
    s_mm, s_cp, s_z, s_bz = map(sem, ("kern_mm", "kern_cp", "z", "bz"))
    s_m = [sem(f"m_in{b}") for b in range(4)]
    with nc.Block() as block:
        @block.tensor
        def _(pe):
            cm = lambda c, g, t0, t1: C_mat[c][:, g, t0:t1, :].rearrange("p t i -> p (t i)")
            pe.wait_ge(s_bz, 2)
            for g in range(GROUPS):
                q = g // 2
                if g % 2 == 0 and q >= 8:
                    pe.wait_ge(s_cp, q - 7)
                out = psum[0:SG, q % 8, g % 2 * 256:g % 2 * 256 + SLOTS * SG]
                for a, b, lhs, rhs in ((0, T - 1, lambda c: Bz[:, 1, c, g, :], lambda c: cm(c, g, 1, T)),
                                       (T - 1, T, lambda c: Bb[:, c, g, :], lambda c: C0[:, c, g, :]),
                                       (T, SLOTS, lambda c: Bz[:, 0, c, g, :], lambda c: cm(c, g, 0, T - 1))):
                    for c in range(2):
                        mm = pe.matmul(out[:, a * SG:b * SG], lhs(c), rhs(c), start=c == 0, stop=c == 1)
                if g % 2:
                    mm.then_inc(s_mm, 1)

        @block.scalar
        def _(act):
            for q in range(GROUPS // 2):
                act.wait_ge(s_mm, q + 1)
                act.copy(kern[:, 2 * q:2 * q + 2, :], psum[0:SG, q % 8, :].rearrange("p (g x) -> p g x", g=2)[:, :, 0:SLOTS * SG]).then_inc(s_cp, 1)

        @block.vector
        def _(dve):
            dve.memset(Bz, 0.0).then_inc(s_z, 1)
            dve.wait_ge(s_z, 1)
            for d, h in enumerate((slice(0, 64), slice(64, 128))):
                dve.tensor_copy(Bz[h, d], Bb[h]).then_inc(s_bz, 1)

        @block.sync
        def _(sp):
            for b in range(4):
                sp.wait_ge(s_cp, 4 * (b + 1))
                for t in range(T):
                    at = (T - 1 - t) * SG
                    sp.dma_start(M[t * SG:(t + 1) * SG, 8 * b:8 * b + 8, :], kern[:, 8 * b:8 * b + 8, at:at + P]).then_inc(s_m[b], 16)
            for b in range(4):
                sp.wait_ge(s_m[b], 16 * T)


def within_chunks(nc, ctx, w, ident, psum, u, M, UT):
    sb, sem = tools(nc, ctx, "sw")
    Db = sb("Db", [P, GROUPS, SG])
    s_d, s_du, s_y, s_sum, s_ut, s_utc = map(sem, ("d_in", "du", "y", "y_sum", "ut", "ut_cp"))
    NQ = GROUPS // 4
    with nc.Block() as block:
        @block.sync
        def _(sp):
            sp.dma_start(Db[:].rearrange("p g i -> p (g i)"), w["ssm_d"][0:1, :].broadcast_to([P, WIDTH])).then_inc(s_d, 16)

        @block.tensor
        def _(pe):
            def inside(q):
                pe.wait_ge(s_utc, q + 1)
                if q >= 4:
                    pe.wait_ge(s_sum, q - 3)
                for g in range(4 * q, 4 * q + 4):
                    mm = pe.matmul(psum[:, q % 4, g % 4 * P:(g % 4 + 1) * P], UT[:, g, :], M[:, g, :], start=True, stop=True)
                mm.then_inc(s_y, 1)
            for q in range(NQ):
                if q >= 4:
                    pe.wait_ge(s_utc, q - 3)
                for g in range(4):
                    mm = pe.transpose(psum[:, 4 + q % 4, g * P:(g + 1) * P], u[:, 4 * q + g, :, :].rearrange("p t i -> p (t i)"), ident[:])
                mm.then_inc(s_ut, 1)
                if q:
                    inside(q - 1)
            inside(NQ - 1)

        @block.scalar
        def _(act):
            for q in range(NQ):
                act.wait_ge(s_ut, q + 1)
                act.copy(UT[:, 4 * q:4 * q + 4, :], psum[:, 4 + q % 4, :].rearrange("p (g c) -> p g c", g=4)).then_inc(s_utc, 1)

        @block.vector
        def _(dve):
            dve.wait_ge(s_d, 16)
            for q in range(NQ):
                g = slice(4 * q, 4 * q + 4)
                dve.wait_ge(s_ut, q + 1)
                dve.tensor_tensor(u[:, g], u[:, g], Db[:, g].unsqueeze(2).broadcast_to([P, 4, T, SG]), ALU.mult).then_inc(s_du, 1)
                dve.wait_ge(s_du, q + 1)
                dve.wait_ge(s_y, q + 1)
                dve.tensor_tensor(u[:, g], psum[:, q % 4, :].rearrange("p (g t i) -> p g t i", g=4, i=SG), u[:, g], ALU.add).then_inc(s_sum, 1)


def scan_chunks(nc, ctx, w, rows, rows_at, psum, nT_hi, nT_lo, gates, E_mat, UT, lam8, H):
    sb, sem = tools(nc, ctx, "sd")
    prod = sb("prod", [P, 2, 2, GROUPS])
    s_e, s_ec, s_mul, s_sum, s_scan = map(sem, ("e", "e_cp", "mul", "sum", "scan"))
    side = Gates(nc, ctx, "g2", w["w_in"][0], GATES_BESIDE_SETUP, 2 * D // P, nT_hi, nT_lo, psum, gates, rows[:, 4:6, :], rows_at)
    NQ = 2 * GROUPS // 4
    with nc.Block() as block:
        @block.sync
        def _(sp):
            side.gp.load(sp, 0)
            side.gp.load(sp, 1)
            side.sync(sp)

        @block.tensor
        def _(pe):
            for q in range(NQ):
                c, g0 = q // 8, q % 8 * 4
                if q >= 4:
                    pe.wait_ge(s_ec, 2 * (q - 3))
                for g in range(4):
                    mm = pe.matmul(psum[:, 4 + q % 4, g * P:(g + 1) * P], E_mat[c][:, g0 + g, :], UT[:, g0 + g, :], start=True, stop=True)
                mm.then_inc(s_e, 1)
            for n in range(side.N):
                side.gp.product(pe, n)

        @block.scalar
        def _(act):
            for q in range(NQ):
                c, g0 = q // 8, q % 8 * 4
                act.wait_ge(s_e, q + 1)
                ps = psum[:, 4 + q % 4, :].rearrange("p (g c) -> p c g", g=4)
                act.copy(H[0:64, 1:CH + 1, c, g0:g0 + 4], ps[0:64]).then_inc(s_ec, 1)
                act.copy(H[64:128, CH:0:-1, c, g0:g0 + 4], ps[64:128]).then_inc(s_ec, 1)
            side.gp.high(act, 0)
            side.gp.high(act, 1)
            for n in range(side.N):
                side.sigmoid(act, n)

        @block.gpsimd
        def _(pool):
            for n in range(side.N):
                side.gp.low(pool, n)

        @block.vector
        def _(dve):
            dve.memset(H[:, 0], 0.0).then_inc(s_scan, 1)
            dve.wait_ge(s_ec, 2 * NQ)
            for n in range(CH - 1):
                now = H[:, n:n + 1].rearrange("p a r g -> p a (r g)").broadcast_to([P, 2, 2 * GROUPS])
                dve.wait_ge(s_scan, n + 1)
                dve.tensor_tensor(prod[:].rearrange("p c r g -> p c (r g)"), now, lam8[:].rearrange("p c r g -> p c (r g)"), ALU.mult).then_inc(s_mul, 1)
                dve.wait_ge(s_mul, n + 1)
                dve.tensor_tensor(H[:, n + 1], H[:, n + 1], prod[:, 0], ALU.add).then_inc(s_sum, 1)
                dve.wait_ge(s_sum, n + 1)
                dve.tensor_tensor(H[:, n + 1], H[:, n + 1], prod[:, 1, ::-1], ALU.add).then_inc(s_scan, 1)


def chunk_outputs(nc, ctx, psum, u, y, H, Hn, C_mat):
    sb, sem = tools(nc, ctx, "se")
    s_fw, s_bw, s_y, s_sum = map(sem, ("forward", "backward", "y", "y_sum"))
    with nc.Block() as block:
        @block.tensor
        def _(pe):
            for q in range(GROUPS // 4):
                pe.wait_ge(s_fw, q // 2 * 2 + 2)
                pe.wait_ge(s_bw, q // 2 * 2 + 2)
                for g in range(4 * q, 4 * q + 4):
                    for c in range(2):
                        mm = pe.matmul(psum[:, q, g % 4 * P:(g % 4 + 1) * P], Hn[c][:, g, :], C_mat[c][:, g].rearrange("p t i -> p (t i)"), start=c == 0, stop=c == 1)
                mm.then_inc(s_y, 1)

        @block.vector
        def _(dve):
            def block_sum(b):
                block_y = y[:, 8 * b:8 * b + 8, :].rearrange("p a b -> p (a b)").rearrange("p (t g i) -> p g t i", t=T, i=SG)
                for q in (2 * b, 2 * b + 1):
                    dve.wait_ge(s_y, q + 1)
                    dve.tensor_tensor(block_y[:, q % 2 * 4:q % 2 * 4 + 4], psum[:, q, :].rearrange("p (g t i) -> p g t i", g=4, i=SG),
                                      u[:, 4 * q:4 * q + 4], ALU.add).then_inc(s_sum, 1)
            for b in range(GROUPS // 8):
                for c in range(2):
                    dve.tensor_copy(Hn[c][64:128, 8 * b:8 * b + 8, :].rearrange("p g c -> p c g"), H[64:128, CH - 1::-1, c, 8 * b:8 * b + 8]).then_inc(s_bw, 1)
                if b:
                    block_sum(b - 1)
            block_sum(GROUPS // 8 - 1)

        @block.scalar
        def _(act):
            for b in range(GROUPS // 8):
                for c in range(2):
                    act.copy(Hn[c][0:64, 8 * b:8 * b + 8, :].rearrange("p g c -> p c g"), H[0:64, 0:CH, c, 8 * b:8 * b + 8]).then_inc(s_fw, 1)
            for b in range(GROUPS // 8):
                act.wait_ge(s_sum, 2 * b + 2)
                act.activation(u[:, 8 * b:8 * b + 8].rearrange("p g t i -> p (g t i)"), y[:, 8 * b:8 * b + 8, :].rearrange("p a b -> p (a b)"), ACT.Gelu_apprx_tanh)


def glu_phase(nc, w, rows, ident, psum, y, gates, partial, kept):
    with Phase(nc) as ctx:
        sb, sem = tools(nc, ctx, "gl")
        NB = WIDTH // P
        yT_hi, yT_lo = sb("yT_hi", [P, NB, SEQ], F32R), sb("yT_lo", [P, NB, SEQ], F32R)
        sT_hi, sT_lo = sb("sT_hi", [P, NB, SEQ], F32R), sb("sT_lo", [P, NB, SEQ], F32R)
        bias = sb("bias", [P, 2 * NB])
        sig, val = sb("sig", [P, SEQ]), sb("val", [P, 2, SEQ])
        gate, out = sb("gate", [P, 2, SEQ]), sb("out", [P, 2, SEQ])
        order = [c for b in range(NB) for c in (WIDTH + b * P, b * P)]
        glu = ColumnProduct(nc, ctx, "glu", w["w_glu"][0], order, yT_hi, yT_lo, psum)
        wos = ColumnProduct(nc, ctx, "wos", w["w_o_ssm"][0], [n * P for n in range(KT)], sT_hi, sT_lo, psum, 4)
        s_b, s_t, s_hi, s_lo, s_sig, s_vhi, s_vlo = map(sem, ("b", "t", "yhi", "ylo", "sig", "vhi", "vlo"))
        s_g, s_o, s_kept = [sem("g0"), sem("g1")], [sem("o0"), sem("o1")], sem("kept")
        block = ctx.enter_context(nc.Block())
        two = lambda ap: ap.rearrange("p (a b) -> p a b", a=2)
        NT = 2 * NB
        yb = y[:].rearrange("p g t i -> p (g t i)").rearrange("p (b t c) -> p b t c", b=NB, t=T)
        dest = lambda a, b, tq: a[:, b, :].rearrange("p (c t) -> p t c", t=T)[:, 4 * tq:4 * tq + 4, :]
        bank = lambda n: psum[:, 4 + n % 4, :].rearrange("p (t c) -> p t c", t=4)

        @block.sync
        def _(sp):
            sp.dma_start(bias[:], w["b_glu"][0].rearrange("(n p) -> p n", p=P), allow_slow_non_contiguous=True).then_inc(s_b, 16)
            for n in range(glu.N):
                glu.load(sp, n)
                if n == 3:
                    sp.dma_start(rows[:], kept.rearrange("(m p) d -> p m d", p=P)).then_inc(s_kept, 16)
            for n in range(2):
                wos.load(sp, n)
                sp.dma_start(gate[:, n, :], gates[D + n * P:D + (n + 1) * P, :]).then_inc(s_g[n], 16)
            for n in range(KT):
                if n + 2 < KT:
                    wos.load(sp, n + 2)
                sp.wait_ge(wos.read[n % 2], n // 2 + 1)
                if n + 2 < KT:
                    sp.dma_start(gate[:, n % 2, :], gates[D + (n + 2) * P:D + (n + 3) * P, :]).then_inc(s_g[n % 2], 16)
                sp.dma_start(partial[n * P:(n + 1) * P, :], out[:, n % 2, :]).then_inc(s_o[n % 2], 16)
            for i in range(2):
                sp.wait_ge(s_o[i], 16 * KT // 2)
            sp.wait_ge(s_kept, 16)

        @block.tensor
        def _(pe):
            for n in range(NT):
                b, tq = n // 2, n % 2
                if n >= 4:
                    pe.wait_ge(s_lo, n - 3)
                for t in range(4):
                    mm = pe.transpose(psum[:, 4 + n % 4, t * P:(t + 1) * P], yb[:, b, 4 * tq + t, :], ident[:])
                mm.then_inc(s_t, 1)
            pe.wait_ge(s_lo, NT)
            for n in range(glu.N):
                glu.product(pe, n)
            pe.wait_ge(s_vlo, NB)
            for n in range(KT):
                wos.product(pe, n)

        @block.scalar
        def _(act):
            glu.high(act, 0)
            glu.high(act, 1)
            for n in range(NT):
                act.wait_ge(s_t, n + 1)
                act.copy(dest(yT_hi, n // 2, n % 2), bank(n)).then_inc(s_hi, 1)
            act.wait_ge(s_b, 16)
            for b in range(NB):
                act.wait_ge(glu.mm_done, 2 * b + 1)
                if b:
                    act.wait_ge(glu.read[1], b)
                act.activation(two(sig[:]), glu.ps[0], ACT.Sigmoid, bias=bias[:, NB + b:NB + b + 1]).then_inc(glu.read[0], 1)
                glu.high(act, 2 * b + 2)
                act.wait_ge(glu.read[1], b + 1)
                act.copy(sT_hi[:, b, :], val[:, b % 2, :]).then_inc(s_vhi, 1)
                glu.high(act, 2 * b + 3)
            wos.high(act, 0)
            wos.high(act, 1)
            for n in range(KT):
                wos.high(act, n + 2)

        @block.vector
        def _(dve):
            glu.low(dve, 0)
            glu.low(dve, 1)
            for n in range(NT):
                dve.wait_ge(s_hi, n + 1)
                dve.tensor_tensor(dest(yT_lo, n // 2, n % 2), bank(n), dest(yT_hi, n // 2, n % 2).bitcast(F32), ALU.subtract).then_inc(s_lo, 1)
            dve.wait_ge(s_b, 16)
            for b in range(NB):
                dve.wait_ge(glu.mm_done, 2 * b + 2)
                dve.wait_ge(glu.read[0], b + 1)
                if b >= 2:
                    dve.wait_ge(s_vlo, b - 1)
                dve.scalar_tensor_tensor(out=two(val[:, b % 2, :]), in0=glu.ps[1], scalar=bias[:, b:b + 1], in1=two(sig[:]),
                                         op0=ALU.add, op1=ALU.mult).then_inc(glu.read[1], 1)
                glu.low(dve, 2 * b + 2)
                dve.wait_ge(s_vhi, b + 1)
                dve.tensor_tensor(sT_lo[:, b, :], val[:, b % 2, :], sT_hi[:, b, :].bitcast(F32), ALU.subtract).then_inc(s_vlo, 1)
                glu.low(dve, 2 * b + 3)
            wos.low(dve, 0)
            wos.low(dve, 1)
            for n in range(KT):
                dve.wait_ge(wos.mm_done, n + 1)
                dve.wait_ge(s_g[n % 2], 16 * (n // 2 + 1))
                if n >= 2:
                    dve.wait_ge(s_o[n % 2], 16 * (n // 2))
                dve.tensor_tensor(two(out[:, n % 2, :]), wos.ps[n % 2], two(gate[:, n % 2, :]), ALU.mult).then_inc(wos.read[n % 2], 1)
                wos.low(dve, n + 2)


def attention_phase(nc, w, ident, psum, latent_rows, aT_hi, aT_lo):
    with Phase(nc) as ctx:
        sb, sem = tools(nc, ctx, "at")
        NL = 3
        lT_hi, lT_lo = sb("lT_hi", [P, NL, SEQ], F32R), sb("lT_lo", [P, NL, SEQ], F32R)
        krT = sb("krT", [P, SEQ])
        trig = sb("trig", [P, SEQ])
        with Phase(nc) as inner:
            latents(nc, inner, w, ident, psum, latent_rows, lT_hi, lT_lo, krT, trig)
        head_loop(nc, ctx, w, ident, psum, lT_hi, lT_lo, krT, trig, aT_hi, aT_lo)


def latents(nc, ctx, w, ident, psum, latent_rows, lT_hi, lT_lo, krT, trig):
    sb, sem = tools(nc, ctx, "la")
    zrow = sb("zrow", [P, ST, ZW])
    s_rows = [sem(f"rows{i}") for i in range(4)]
    gb = sb("gb", [P, QR + KVR])
    zn = sb("zn", [P, 2, QR + KVR])
    stat = sb("stat", [P, 5, 2, ST])
    pos, ang, turns = sb("pos", [P, SEQ], I32), sb("ang", [P, SEQ]), sb("turns", [P, SEQ])
    cst = sb("cst", [P, 2])
    s_gb, s_pos, s_cst, s_sq, s_var, s_sqrt, s_link, s_zn, s_tr, s_hi, s_lo, s_ang, s_kr, s_sgn = map(
        sem, ("gb", "pos", "cst", "sq", "var", "sqrt", "link", "zn", "tr", "hi", "lo", "ang", "kr", "sgn"))
    Rp = slice(64, 128)
    bank = lambda m: psum[:, m, 0:3 * P].rearrange("p (k s) -> p k s", k=3)
    with nc.Block() as block:
        @block.sync
        def _(sp):
            for i in range(4):
                sp.dma_start(zrow[:, 2 * i:2 * i + 2, :], latent_rows[2 * i * P:(2 * i + 2) * P, :].rearrange("(m p) z -> p m z", p=P)).then_inc(s_rows[i], 16)
            sp.dma_start(pos[Rp, :], w["positions"][0:1, :].broadcast_to([64, SEQ])).then_inc(s_pos, 16)
            sp.dma_start(cst[:], w["rope_const"]).then_inc(s_cst, 16)
            sp.dma_start(gb[:, 0:QR], w["q_norm"][0:1, :].broadcast_to([P, QR])).then_inc(s_gb, 16)
            sp.dma_start(gb[:, QR:], w["kv_norm"][0:1, :].broadcast_to([P, KVR])).then_inc(s_gb, 16)

        @block.scalar
        def _(act):
            for m in range(ST):
                act.wait_ge(s_rows[m // 2], 16)
                act.activation(psum[:, m, 0:QR], zrow[:, m, 0:QR], ACT.Square, accum_out=stat[:, 0, 0, m:m + 1]).then_inc(s_sq, 1)
                act.activation(psum[:, m, QR:QR + KVR], zrow[:, m, QR:QR + KVR], ACT.Square, accum_out=stat[:, 0, 1, m:m + 1]).then_inc(s_sq, 1)
            act.wait_ge(s_var, 1)
            act.activation(stat[:, 2], stat[:, 1], ACT.Sqrt).then_inc(s_sqrt, 1)
            act.wait_ge(s_ang, 1)
            act.activation(trig[Rp, :], ang[Rp, :], ACT.Sin).then_inc(s_sgn, 1)
            for m in range(ST):
                act.wait_ge(s_tr, m + 1)
                act.copy(krT[Rp, m * P:(m + 1) * P], psum[Rp, m, 3 * P:4 * P])
                act.copy(lT_hi[:, :, m * P:(m + 1) * P], bank(m)).then_inc(s_hi, 1)

        @block.vector
        def _(dve):
            link = Chain(dve, s_link)

            def low(m):
                sl = slice(m * P, (m + 1) * P)
                dve.wait_ge(s_hi, m + 1)
                dve.tensor_tensor(lT_lo[:, :, sl], bank(m), lT_hi[:, :, sl].bitcast(F32), ALU.subtract)
            dve.wait_ge(s_pos, 16)
            dve.wait_ge(s_cst, 16)
            link(dve.tensor_copy(ang[Rp], pos[Rp]))
            link(dve.tensor_scalar(ang[Rp], ang[Rp], cst[Rp, 0:1], None, ALU.mult))
            C, S = slice(64, 96), slice(96, 128)
            reduce_angle(link, ang[C], turns[C], None, 0.25)
            reduce_angle(link, ang[S], turns[S], None, 0.0)
            dve.sem_inc(s_ang, 1)
            dve.wait_ge(s_sq, 2 * ST)
            for j, n in enumerate((QR, KVR)):
                link(dve.tensor_scalar(stat[:, 1, j], stat[:, 0, j], 1.0 / n, EPS, ALU.mult, ALU.add))
            dve.sem_inc(s_var, 1)
            dve.wait_ge(s_sqrt, 1)
            newton(link, stat[:, 1], stat[:, 2], stat[:, 3], stat[:, 4])
            dve.wait_ge(s_gb, 32)

            def row(m):
                if m >= 2:
                    dve.wait_ge(s_tr, m - 1)
                for j, sl in enumerate((slice(0, QR), slice(QR, QR + KVR))):
                    dve.scalar_tensor_tensor(out=zn[:, m % 2, sl], in0=zrow[:, m, sl], scalar=stat[:, 3, j, m:m + 1], in1=gb[:, sl],
                                             op0=ALU.mult, op1=ALU.mult).then_inc(s_zn, 1)
            for m in range(ST):
                row(m)
                if m:
                    low(m - 1)
            low(ST - 1)
            dve.wait_ge(s_sgn, 1)
            dve.tensor_scalar(trig[S], trig[S], cst[S, 1:2], None, ALU.mult)

        @block.tensor
        def _(pe):
            pe.wait_ge(s_sqrt, 1)
            for m in range(ST):
                pe.wait_ge(s_zn, 2 * m + 2)
                for k in range(3):
                    pe.transpose(psum[:, m, k * P:(k + 1) * P], zn[:, m % 2, k * P:(k + 1) * P], ident[:])
                pe.transpose(psum[:, m, 3 * P:4 * P], zrow[:, m, ZW - P:ZW], ident[:]).then_inc(s_tr, 1)


def head_loop(nc, ctx, w, ident, psum, lT_hi, lT_lo, krT, trig, aT_hi, aT_lo):
    sb, sem = tools(nc, ctx, "hd")
    KD = NOPE + ROPE
    raw = sb("raw", [P, 3, P])
    w_hi, w_lo = sb("w_hi", [P, 3, P], F32R), sb("w_lo", [P, 3, P], F32R)
    QT_hi, QT_lo = sb("QT_hi", [P, 2, SEQ], F32R), sb("QT_lo", [P, 2, SEQ], F32R)
    KT_hi, KT_lo = sb("KT_hi", [P, 2, SEQ], F32R), sb("KT_lo", [P, 2, SEQ], F32R)
    V_hi, V_lo = sb("V_hi", [P, 2, ST, VH], F32R), sb("V_lo", [P, 2, ST, VH], F32R)
    qf = sb("qf", [P, 2, HALF])
    rot = krT[:].rearrange("p (a b) -> p a b", a=2)
    prob = sb("prob", [P, 2, SEQ])
    PT_hi, PT_lo = sb("PT_hi", [P, 2, ST, 2 * P], F32R), sb("PT_lo", [P, 2, ST, 2 * P], F32R)
    mx, nmx, tot, inv = (sb(n, [P, 2]) for n in ("mx", "nmx", "tot", "inv"))
    diag = sb("diag", [P, 4, P])
    ones = sb("ones", [P, VH])
    spread = sb("spread", [VH, 2 * P])
    att = sb("att", [P, 2, 2 * P])
    names = "kr_rot raw_in w_hi w_lo proj proj_act proj_dve rot q_sum q_hi q_lo kr kr_hi kr_lo scores mx nmx exp inv diag ones tr tr_hi tr_lo pv spread av av_hi av_lo".split()
    s = {n: sem(n) for n in names}
    w_uq, w_ukv = w["w_uq"][0].rearrange("(k p) f -> p k f", p=P), w["w_ukv"][0]
    half_r = ROPE // 2
    C, S = slice(64, 96), slice(96, 128)
    hs = lambda x: slice(x * HALF, (x + 1) * HALF)
    bank = psum[:, 7, :]
    two = lambda ap: ap.rearrange("p (a b) -> p a b", a=2)
    tbank = lambda b: psum[:, 4 + b, :].rearrange("p (k q) -> p k q", k=4)
    pt = lambda a, qt, b: a[:, qt // 2 % 2, 4 * b:4 * b + 4, qt % 2 * P:(qt % 2 + 1) * P]
    pv_out, inv_out = psum[0:VH, 6, 0:2 * P], psum[0:VH, 6, 2 * P:4 * P]
    block = ctx.enter_context(nc.Block())

    def heads(step_of_head):
        def run(eng):
            for h in (0, 1):
                step_of_head(h, h // 2, h % 2)
            with eng.Fori(1, HEADS // 2 - 1) as q:
                for par in (0, 1):
                    step_of_head(q * 2 + par, q, par)
            for h in (HEADS - 2, HEADS - 1):
                step_of_head(h, h // 2, h % 2)
        return run

    def is_first(h):
        return isinstance(h, int) and h == 0

    def is_last(h):
        return isinstance(h, int) and h == HEADS - 1

    @block.sync
    def _(sp):
        def load(n):
            if not isinstance(n, int) or n > 0:
                sp.wait_ge(s["w_lo"], n)
            nq = n * KD
            sp.dma_start(raw[:, 0:2, 0:KD], w_uq[:, :, bass.ds(nq, KD)]).then_inc(s["raw_in"], 16)
            sp.dma_start(raw[:, 0:2, KD:KD + half_r], w_uq[:, :, bass.ds(nq + NOPE + half_r, half_r)]).then_inc(s["raw_in"], 16)
            sp.dma_start(raw[:, 0:2, KD + half_r:P], w_uq[:, :, bass.ds(nq + NOPE, half_r)]).then_inc(s["raw_in"], 16)
            sp.dma_start(raw[:, 2, :], w_ukv[:, bass.ds(n * P, P)]).then_inc(s["raw_in"], 16)
        load(0)
        with sp.Fori(1, HEADS) as n:
            load(n)

    def proj_mm(pe, n, x, par):
        job = n * 5 + x
        if not (isinstance(n, int) and n == 0 and x == 0):
            pe.wait_ge(s["proj_act"], job)
            pe.wait_ge(s["proj_dve"], job)
        if x == 0:
            pe.wait_ge(s["w_lo"], n + 1)
        if x < 2:
            for k in range(2):
                mm = three_passes(pe, bank, w_hi[:, k, :], w_lo[:, k, :], lT_hi[:, k, hs(x)], lT_lo[:, k, hs(x)], k == 0, k == 1)
        elif x < 4:
            mm = three_passes(pe, bank[0:NOPE], w_hi[:, 2, 0:NOPE], w_lo[:, 2, 0:NOPE], lT_hi[:, 2, hs(x - 2)], lT_lo[:, 2, hs(x - 2)], True, True)
        else:
            for m in range(ST):
                sl = slice(m * P, (m + 1) * P)
                mm = three_passes(pe, bank[:, m * VH:(m + 1) * VH], lT_hi[:, 2, sl], lT_lo[:, 2, sl],
                                  w_hi[:, 2, NOPE:], w_lo[:, 2, NOPE:], True, True)
        mm.then_inc(s["proj"], 1)

    def scores(pe, h, qt, par):
        g = h * 8 + qt
        if qt == 0:
            pe.wait_ge(s["q_lo"], h * 2 + 2)
            pe.wait_ge(s["proj_dve"], h * 5 + 5)
        if not (isinstance(h, int) and g < 2):
            pe.wait_ge(s["exp"], g - 1)
        for half in range(2):
            mm = three_passes(pe, psum[:, 2 * (qt % 2) + half, :], QT_hi[0:KD, par, qt * P:(qt + 1) * P], QT_lo[0:KD, par, qt * P:(qt + 1) * P],
                              KT_hi[0:KD, par, hs(half)], KT_lo[0:KD, par, hs(half)], True, True)
        mm.then_inc(s["scores"], 1)

    def turn(pe, g, qt):
        pe.wait_ge(s["exp"], g + 1)
        for b in range(2):
            if not (isinstance(g, int) and g == 0):
                pe.wait_ge(s["tr_lo"], g * 2 - 1 + b)
            for k in range(4):
                t = pe.transpose(psum[:, 4 + b, k * P:(k + 1) * P], prob[:, qt % 2, (4 * b + k) * P:(4 * b + k + 1) * P], ident[:])
            t.then_inc(s["tr"], 1)

    def values(pe, jj, j, par):
        if not (isinstance(jj, int) and jj == 0):
            pe.wait_ge(s["av"], jj)
        pe.wait_ge(s["diag"], jj * 2 + 2)
        for i in range(2):
            pe.matmul(inv_out[:, i * P:(i + 1) * P], ones[:], diag[:, j % 2 * 2 + i, :], start=True, stop=True)
        pe.wait_ge(s["tr_lo"], jj * 4 + 4)
        for k in range(ST):
            mm = three_passes(pe, pv_out, V_hi[:, par, k, :], V_lo[:, par, k, :], PT_hi[:, j % 2, k, :], PT_lo[:, j % 2, k, :], k == 0, k == ST - 1)
        mm.then_inc(s["pv"], 1)

    @block.tensor
    def _(pe):
        for x in range(5):
            proj_mm(pe, 0, x, 0)
        pe.wait_ge(s["kr_lo"], 2)
        pe.wait_ge(s["ones"], 1)

        def head(h, q, par):
            for qt in range(ST):
                scores(pe, h, qt, par)
                if qt >= 2 or not is_first(h):
                    turn(pe, h * 8 + qt - 2, (qt - 2) % ST)
                if qt % 2 == 0 and (qt >= 4 or not is_first(h)):
                    values(pe, h * 4 + qt // 2 - 2, (qt // 2 - 2) % 4, par if qt >= 4 else 1 - par)
                if not is_last(h) and 1 <= qt <= 5:
                    proj_mm(pe, h + 1, qt - 1, 1 - par)
        heads(head)(pe)
        N = HEADS * ST
        turn(pe, N - 2, ST - 2)
        values(pe, N // 2 - 2, 2, 1)
        turn(pe, N - 1, ST - 1)
        values(pe, N // 2 - 1, 3, 1)

    @block.scalar
    def _(act):
        def split(n):
            act.wait_ge(s["raw_in"], n * 64 + 64)
            if not isinstance(n, int) or n > 0:
                act.wait_ge(s["proj"], n * 5)
            act.copy(w_hi[:], raw[:]).then_inc(s["w_hi"], 1)

        def project(n, x, par):
            act.wait_ge(s["proj"], n * 5 + x + 1)
            if x < 2:
                if not (isinstance(n, int) and n == 0):
                    act.wait_ge(s["q_lo"], n * 2 + x - 1)
                act.copy(qf[0:NOPE, x, :], bank[0:NOPE]).then_inc(s["proj_act"], 1)
            elif x < 4:
                if not (isinstance(n, int) and n < 2):
                    act.wait_ge(s["scores"], n * 8 - 8)
                act.copy(KT_hi[0:NOPE, par, hs(x - 2)], bank[0:NOPE]).then_inc(s["proj_act"], 1)
            else:
                if not (isinstance(n, int) and n < 2):
                    act.wait_ge(s["pv"], n * 4 - 4)
                act.copy(V_hi[:, par], bank.rearrange("p (m v) -> p m v", m=ST)).then_inc(s["proj_act"], 1)

        def queries(n, x, par):
            act.wait_ge(s["q_sum"], n * 2 + x + 1)
            act.wait_ge(s["proj_act"], n * 5 + x + 1)
            if not (isinstance(n, int) and n < 2):
                act.wait_ge(s["scores"], n * 8 - 8)
            act.copy(QT_hi[0:KD, par, hs(x)], qf[0:KD, x, :]).then_inc(s["q_hi"], 1)

        def turned(g, qt, jj):
            if qt % 2 == 0 and not (isinstance(jj, int) and jj < 2):
                act.wait_ge(s["pv"], jj - 1)
            for b in range(2):
                act.wait_ge(s["tr"], g * 2 + b + 1)
                act.copy(pt(PT_hi, qt, b), tbank(b)).then_inc(s["tr_hi"], 1)

        def exponential(g, qt):
            act.wait_ge(s["nmx"], g + 1)
            if not (isinstance(g, int) and g < 2):
                act.wait_ge(s["tr"], g * 2 - 2)
                act.wait_ge(s["inv"], g - 1)
            sl = qt % 2
            act.activation(two(prob[:, sl, :]), psum[:, 2 * sl:2 * sl + 2, :], ACT.Exp, bias=nmx[:, sl:sl + 1], scale=SCALE,
                           accum_out=tot[:, sl:sl + 1]).then_inc(s["exp"], 1)

        def spread_out(jj):
            act.wait_ge(s["pv"], jj + 1)
            if not (isinstance(jj, int) and jj == 0):
                act.wait_ge(s["av"], jj)
            act.copy(spread[:], inv_out).then_inc(s["spread"], 1)

        def attended(jj, j, hpar, hq):
            rows = slice(hpar * VH, (hpar + 1) * VH)
            act.wait_ge(s["av"], jj + 1)
            act.copy(aT_hi[rows, bass.ds(hq, 1), j * 256:(j + 1) * 256].rearrange("p a q -> p (a q)"), att[rows, j % 2, :]).then_inc(s["av_hi"], 1)

        split(0)
        act.wait_ge(s["kr"], 1)
        for par in range(2):
            act.copy(KT_hi[C, par, :], krT[C, :]).then_inc(s["kr_hi"], 1)
        for x in range(5):
            project(0, x, 0)
            if x < 2:
                queries(0, x, 0)
        split(1)

        def head(h, q, par):
            for qt in range(ST):
                same = qt >= 5
                j = (qt // 2 - 2) % 4
                if qt % 2 == 1 and (same or not is_first(h)):
                    spread_out(h * 4 + qt // 2 - 2)
                if not is_last(h) and 2 <= qt <= 6:
                    project(h + 1, qt - 2, 1 - par)
                if not is_last(h) and 3 <= qt <= 4:
                    queries(h + 1, qt - 3, 1 - par)
                if qt >= 2 or not is_first(h):
                    turned(h * 8 + qt - 2, (qt - 2) % ST, h * 4 + (qt - 2) // 2)
                exponential(h * 8 + qt, qt)
                if qt % 2 == 1 and (same or not is_first(h)):
                    attended(h * 4 + qt // 2 - 2, j, par if same else 1 - par, q if same or par else q - 1)
                if qt == 7 and not (isinstance(h, int) and h >= HEADS - 2):
                    split(h + 2)
        heads(head)(act)
        N = HEADS * ST
        turned(N - 2, ST - 2, N // 2 - 1)
        spread_out(N // 2 - 2)
        attended(N // 2 - 2, 2, 1, HEADS // 2 - 1)
        turned(N - 1, ST - 1, N // 2 - 1)
        spread_out(N // 2 - 1)
        attended(N // 2 - 1, 3, 1, HEADS // 2 - 1)

    @block.vector
    def _(dve):
        def split(n):
            dve.wait_ge(s["w_hi"], n + 1)
            dve.tensor_tensor(w_lo[:], raw[:], w_hi[:].bitcast(F32), ALU.subtract).then_inc(s["w_lo"], 1)

        def project(n, x, par):
            dve.wait_ge(s["proj"], n * 5 + x + 1)
            if x < 2:
                if not (isinstance(n, int) and n == 0):
                    dve.wait_ge(s["q_lo"], n * 2 + x - 1)
                dve.wait_ge(s["proj_act"], n * 5 + x + 1)
                dve.tensor_tensor(rot[C, x, :], bank[S], trig[S, hs(x)], ALU.mult).then_inc(s["rot"], 1)
                dve.tensor_tensor(qf[C, x, :], bank[C], trig[C, hs(x)], ALU.mult).then_inc(s["proj_dve"], 1)
            else:
                dve.wait_ge(s["proj_act"], n * 5 + x + 1)
                if x < 4:
                    dve.tensor_tensor(KT_lo[0:NOPE, par, hs(x - 2)], bank[0:NOPE], KT_hi[0:NOPE, par, hs(x - 2)].bitcast(F32), ALU.subtract).then_inc(s["proj_dve"], 1)
                else:
                    dve.tensor_tensor(V_lo[:, par].rearrange("p m v -> p (m v)"), bank, V_hi[:, par].rearrange("p m v -> p (m v)").bitcast(F32), ALU.subtract).then_inc(s["proj_dve"], 1)

        def maximum(g, qt):
            sl = qt % 2
            dve.wait_ge(s["scores"], g + 1)
            if not (isinstance(g, int) and g < 2):
                dve.wait_ge(s["nmx"], g - 1)
            dve.tensor_reduce(mx[:, sl:sl + 1], psum[:, 2 * sl:2 * sl + 2, :], AX.XY, ALU.max).then_inc(s["mx"], 1)
            dve.wait_ge(s["mx"], g + 1)
            dve.tensor_scalar(nmx[:, sl:sl + 1], mx[:, sl:sl + 1], -SCALE, None, ALU.mult).then_inc(s["nmx"], 1)

        def turned(g, qt):
            for b in range(2):
                dve.wait_ge(s["tr_hi"], g * 2 + b + 1)
                dve.tensor_tensor(pt(PT_lo, qt, b), tbank(b), pt(PT_hi, qt, b).bitcast(F32), ALU.subtract).then_inc(s["tr_lo"], 1)

        def inverse(g, qt):
            sl = qt % 2
            dve.wait_ge(s["exp"], g + 1)
            if not (isinstance(g, int) and g < 2):
                dve.wait_ge(s["diag"], g - 1)
            dve.reciprocal(inv[:, sl:sl + 1], tot[:, sl:sl + 1]).then_inc(s["inv"], 1)

        def attended(jj, j, hpar, hq):
            rows = slice(hpar * VH, (hpar + 1) * VH)
            dve.wait_ge(s["spread"], jj + 1)
            if not (isinstance(jj, int) and jj < 2):
                dve.wait_ge(s["av_lo"], jj - 1)
            dve.tensor_tensor(att[rows, j % 2, :], pv_out, spread[:], ALU.mult).then_inc(s["av"], 1)

        dve.memset(ones[:], 1.0).then_inc(s["ones"], 1)
        dve.tensor_tensor(prob[C, 0, :], krT[S], trig[S], ALU.mult).then_inc(s["kr_rot"], 1)
        dve.tensor_tensor(krT[C], krT[C], trig[C], ALU.mult).then_inc(s["kr_rot"], 1)
        dve.wait_ge(s["kr_rot"], 2)
        dve.tensor_tensor(krT[C], krT[C], prob[C, 0, :], ALU.add).then_inc(s["kr"], 1)
        for par in range(2):
            dve.wait_ge(s["kr_hi"], par + 1)
            dve.tensor_tensor(KT_lo[C, par, :], krT[C, :], KT_hi[C, par, :].bitcast(F32), ALU.subtract).then_inc(s["kr_lo"], 1)
        split(0)
        for x in range(5):
            project(0, x, 0)
        split(1)

        def head(h, q, par):
            for qt in range(ST):
                if qt % 2 == 1 and (qt >= 5 or not is_first(h)):
                    j = (qt // 2 - 2) % 4
                    same = qt >= 5
                    attended(h * 4 + qt // 2 - 2, j, par if same else 1 - par, q if same or par else q - 1)
                if not is_last(h) and 2 <= qt <= 6:
                    project(h + 1, qt - 2, 1 - par)
                maximum(h * 8 + qt, qt)
                if qt >= 1 or not is_first(h):
                    inverse(h * 8 + qt - 1, (qt - 1) % ST)
                if qt >= 2 or not is_first(h):
                    turned(h * 8 + qt - 2, (qt - 2) % ST)
                if qt == 7 and not (isinstance(h, int) and h >= HEADS - 2):
                    split(h + 2)
        heads(head)(dve)
        N = HEADS * ST
        inverse(N - 1, ST - 1)
        turned(N - 2, ST - 2)
        attended(N // 2 - 2, 2, 1, HEADS // 2 - 1)
        turned(N - 1, ST - 1)
        attended(N // 2 - 1, 3, 1, HEADS // 2 - 1)

    @block.gpsimd
    def _(pool):
        def queries(n, x, par):
            if not (isinstance(n, int) and n == 0 and x == 0):
                pool.wait_ge(s["q_lo"], n * 2 + x)
            if not (isinstance(n, int) and n == 0):
                pool.wait_ge(s["diag"], n * 8 + x - 6)
                if not (isinstance(n, int) and n == 1):
                    pool.wait_ge(s["av_lo"], n * 4 - 6)
            pool.wait_ge(s["rot"], n * 2 + x + 1)
            pool.wait_ge(s["proj_dve"], n * 5 + x + 1)
            pool.tensor_tensor(qf[C, x, :], qf[C, x, :], rot[C, x, :], ALU.add).then_inc(s["q_sum"], 1)
            pool.wait_ge(s["q_hi"], n * 2 + x + 1)
            pool.tensor_tensor(QT_lo[0:KD, par, hs(x)], qf[0:KD, x, :], QT_hi[0:KD, par, hs(x)].bitcast(F32), ALU.subtract).then_inc(s["q_lo"], 1)

        def diagonal(g, qt, jj):
            pool.wait_ge(s["inv"], g + 1)
            if not (isinstance(jj, int) and jj < 2):
                pool.wait_ge(s["pv"], jj - 1)
            pool.tensor_tensor(diag[:, qt % 4, :], ident[:], inv[:, qt % 2:qt % 2 + 1].broadcast_to([P, P]), ALU.mult).then_inc(s["diag"], 1)

        def attended(jj, j, hpar, hq, g):
            rows = slice(hpar * VH, (hpar + 1) * VH)
            dst = lambda a: a[rows, bass.ds(hq, 1), j * 256:(j + 1) * 256].rearrange("p a q -> p (a q)")
            pool.wait_ge(s["diag"], g + 1)
            pool.wait_ge(s["av_hi"], jj + 1)
            pool.tensor_tensor(dst(aT_lo), att[rows, j % 2, :], dst(aT_hi).bitcast(F32), ALU.subtract).then_inc(s["av_lo"], 1)

        for x in range(2):
            queries(0, x, 0)

        def head(h, q, par):
            for qt in range(ST):
                if not is_last(h) and 3 <= qt <= 4:
                    queries(h + 1, qt - 3, 1 - par)
                g = h * 8 + qt - 1
                if qt >= 1 or not is_first(h):
                    if qt % 2 == 0 and (qt >= 6 or not is_first(h)):
                        pool.wait_ge(s["av_lo"], h * 4 + qt // 2 - 2)
                    diagonal(g, (qt - 1) % ST, h * 4 + (qt - 1) // 2)
                same = qt >= 5
                if qt % 2 == 1 and (same or not is_first(h)):
                    attended(h * 4 + qt // 2 - 2, (qt // 2 - 2) % 4, par if same else 1 - par, q if same or par else q - 1, g)
        heads(head)(pool)
        N = HEADS * ST
        pool.wait_ge(s["av_lo"], N // 2 - 2)
        diagonal(N - 1, ST - 1, N // 2 - 1)
        attended(N // 2 - 2, 2, 1, HEADS // 2 - 1, N - 1)
        attended(N // 2 - 1, 3, 1, HEADS // 2 - 1, N - 1)


def merge_phase(nc, w, psum, rows, aT_hi, aT_lo, gates, partial):
    with Phase(nc) as ctx:
        sb, sem = tools(nc, ctx, "mg")
        mT_hi, mT_lo = sb("mT_hi", [P, KT, SEQ], F32R), sb("mT_lo", [P, KT, SEQ], F32R)
        gate, part, val = sb("gate", [P, 2, SEQ]), sb("part", [P, 2, SEQ]), sb("val", [P, 2, SEQ])
        woa = ColumnProduct(nc, ctx, "woa", w["w_o_attn"][0], [n * P for n in range(KT)], aT_hi, aT_lo, psum)
        lhs = lambda j, k, m: (mT_hi[:, k, m * P:(m + 1) * P], mT_lo[:, k, m * P:(m + 1) * P])
        w_out = w["w_out"][0]
        rp = RowProduct(nc, ctx, "wo", [(w_out, [(0, slice(j * HALF, (j + 1) * HALF))], HALF) for j in range(2)], lhs, psum)
        s_g, s_p = [sem("g0"), sem("g1")], [sem("p0"), sem("p1")]
        s_sum, s_hi, s_lo = sem("sum"), sem("hi"), sem("lo")
        NU = len(rp.units())
        two = lambda ap: ap.rearrange("p (a b) -> p a b", a=2)
        block = ctx.enter_context(nc.Block())

        def add(dve, j, m):
            rp.wait_bank(dve, j, m)
            sl = slice(j * HALF, (j + 1) * HALF)
            dve.tensor_tensor(rows[:, m, sl], psum[:, m, :], rows[:, m, sl], ALU.add).then_inc(rp.read, 1)

        @block.sync
        def _(sp):
            for n in range(KT):
                woa.load(sp, n)
                if n >= 2:
                    sp.wait_ge(s_sum, n - 1)
                sp.dma_start(gate[:, n % 2, :], gates[n * P:(n + 1) * P, :]).then_inc(s_g[n % 2], 16)
                sp.dma_start(part[:, n % 2, :], partial[n * P:(n + 1) * P, :]).then_inc(s_p[n % 2], 16)
            for n in range(NU):
                rp.load(sp, n)

        @block.scalar
        def _(act):
            woa.high(act, 0)
            woa.high(act, 1)
            for n in range(KT):
                woa.high(act, n + 2)
                act.wait_ge(s_sum, n + 1)
                act.copy(mT_hi[:, n, :], val[:, n % 2, :]).then_inc(s_hi, 1)
            for n in range(NU):
                rp.high(act, n)

        @block.vector
        def _(dve):
            woa.low(dve, 0)
            woa.low(dve, 1)
            for n in range(KT):
                dve.wait_ge(woa.mm_done, n + 1)
                dve.wait_ge(s_g[n % 2], 16 * (n // 2 + 1))
                if n >= 2:
                    dve.wait_ge(s_lo, n - 1)
                dve.tensor_tensor(two(val[:, n % 2, :]), woa.ps[n % 2], two(gate[:, n % 2, :]), ALU.mult).then_inc(woa.read[n % 2], 1)
                woa.low(dve, n + 2)
                dve.wait_ge(woa.read[n % 2], n // 2 + 1)
                dve.wait_ge(s_p[n % 2], 16 * (n // 2 + 1))
                dve.tensor_tensor(val[:, n % 2, :], val[:, n % 2, :], part[:, n % 2, :], ALU.add).then_inc(s_sum, 1)
                dve.wait_ge(s_hi, n + 1)
                dve.tensor_tensor(mT_lo[:, n, :], val[:, n % 2, :], mT_hi[:, n, :].bitcast(F32), ALU.subtract).then_inc(s_lo, 1)
            for j in range(2):
                for k in range(KT):
                    rp.low(dve, j * KT + k)
                    if j and k == 1:
                        for m in range(ST):
                            add(dve, 0, m)
            for m in range(ST):
                add(dve, 1, m)

        @block.tensor
        def _(pe):
            for n in range(KT):
                woa.product(pe, n)
            pe.wait_ge(s_lo, KT)
            rp.products(pe)


def final_phase(nc, w, psum, rows, out):
    with Phase(nc) as ctx:
        sb, sem = tools(nc, ctx, "fi")
        gb, stat, o = sb("gb", [P, D]), sb("stat", [P, 5, ST]), sb("o", [P, ST, D])
        s_g, s_sq, s_var, s_sqrt, s_link, s_o, s_out = map(sem, ("g", "sq", "var", "sqrt", "link", "o", "out"))
        block = ctx.enter_context(nc.Block())

        @block.sync
        def _(sp):
            sp.dma_start(gb[:], w["final_norm"].rearrange("(a d) -> a d", a=1).broadcast_to([P, D])).then_inc(s_g, 16)
            for m in range(ST):
                sp.wait_ge(s_o, m + 1)
                sp.dma_start(out[0, m * P:(m + 1) * P, :], o[:, m, :]).then_inc(s_out, 16)
            sp.wait_ge(s_out, 16 * ST)

        @block.scalar
        def _(act):
            for m in range(ST):
                act.activation(o[:, m, :], rows[:, m, :], ACT.Square, accum_out=stat[:, 0, m:m + 1]).then_inc(s_sq, 1)
            act.wait_ge(s_var, 1)
            act.activation(stat[:, 2, :], stat[:, 1, :], ACT.Sqrt).then_inc(s_sqrt, 1)

        @block.vector
        def _(dve):
            dve.wait_ge(s_sq, ST)
            dve.tensor_scalar(stat[:, 1, :], stat[:, 0, :], 1.0 / D, EPS, ALU.mult, ALU.add).then_inc(s_var, 1)
            dve.wait_ge(s_sqrt, 1)
            newton(Chain(dve, s_link), stat[:, 1, :], stat[:, 2, :], stat[:, 3, :], stat[:, 4, :])
            dve.wait_ge(s_g, 16)
            for m in range(ST):
                dve.scalar_tensor_tensor(out=o[:, m, :], in0=rows[:, m, :], scalar=stat[:, 3, m:m + 1], in1=gb[:], op0=ALU.mult, op1=ALU.mult).then_inc(s_o, 1)


def build(nc, w, out):
    gates = nc.dram_tensor("gates", [2 * D, SEQ], F32, kind="Internal").ap()
    partial = nc.dram_tensor("partial", [D, SEQ], F32, kind="Internal").ap()
    kept = nc.dram_tensor("kept", [SEQ, D], F32, kind="Internal").ap()
    latent_rows = nc.dram_tensor("latent_rows", [SEQ, ZW], F32, kind="Internal").ap()
    with ExitStack() as ctx:
        rows_at = -(-nc.sbuf_base // 32) * 32
        rows = ctx.enter_context(nc.sbuf_tensor("rows", [P, ST, D], F32))
        ident = ctx.enter_context(nc.sbuf_tensor("ident", [P, P], F32))
        psum = ctx.enter_context(nc.psum_tensor("psum", [P, 8, HALF], F32))
        make_ident(nc, ident, ctx.enter_context(nc.semaphore("ident_done")))
        ffn_phase(nc, "f1", w["ffn1_norm"][0], w["ffn1_w_gate"][0], w["ffn1_w_up"][0], w["ffn1_w_down"][0], rows, ident, psum, x=w["x"][0])
        with ExitStack() as outer:
            u = outer.enter_context(nc.sbuf_tensor("u", [P, GROUPS, T, SG], F32))
            with ExitStack() as inner:
                C_mat = [inner.enter_context(nc.sbuf_tensor(f"C_mat{c}", [P, GROUPS, T, SG], F32)) for c in range(2)]
                nT_hi, nT_lo = (inner.enter_context(nc.sbuf_tensor(n, [P, KT, SEQ], F32R)) for n in ("nT_hi", "nT_lo"))
                project_phase(nc, w, rows, ident, psum, nT_hi, nT_lo, u, kept, latent_rows)
                ssm_phase(nc, w, rows, rows_at, ident, psum, nT_hi, nT_lo, u, gates, C_mat)
            glu_phase(nc, w, rows, ident, psum, u, gates, partial, kept)
        with ExitStack() as outer:
            aT_hi, aT_lo = (outer.enter_context(nc.sbuf_tensor(n, [P, HEADS // 2, SEQ], F32R)) for n in ("aT_hi", "aT_lo"))
            attention_phase(nc, w, ident, psum, latent_rows, aT_hi, aT_lo)
            merge_phase(nc, w, psum, rows, aT_hi, aT_lo, gates, partial)
        ffn_phase(nc, "f2", w["ffn2_norm"][0], w["ffn2_w_gate"][0], w["ffn2_w_up"][0], w["ffn2_w_down"][0], rows, ident, psum)
        final_phase(nc, w, psum, rows, out)


INPUTS = ["x", "positions", "ffn1_norm", "ffn1_w_gate", "ffn1_w_up", "ffn1_w_down", "mix_norm", "w_in", "q_norm", "w_uq", "kv_norm",
          "w_ukv", "w_o_attn", "ssm_lambda_re", "ssm_lambda_im", "ssm_log_dt", "ssm_b_re", "ssm_b_im", "ssm_c_re", "ssm_c_im",
          "ssm_d", "w_glu", "b_glu", "w_o_ssm", "w_out", "ffn2_norm", "ffn2_w_gate", "ffn2_w_up", "ffn2_w_down", "final_norm"]


def rope_const():
    half = ROPE // 2
    freq = (np.float32(10000.0) ** (-np.arange(0, ROPE, 2, dtype=np.float32) / np.float32(ROPE))).astype(np.float32)
    sign = np.ones(P, np.float32)
    sign[P - ROPE:P - half] = -1.0
    return np.stack([np.tile(freq, P // half), sign], axis=1)


def kernel(**inputs):
    import concourse.bacc as bacc
    from concourse.bass_utils import run_bass_kernel_spmd

    nc = bacc.Bacc("TRN2", target_bir_lowering=False, num_devices=1)
    arrays = {name: np.ascontiguousarray(inputs[name]) for name in INPUTS}
    arrays["rope_const"] = rope_const()
    w = {name: nc.dram_tensor(name, a.shape, mybir.dt.from_np(a.dtype), kind="ExternalInput").ap() for name, a in arrays.items()}
    out = nc.dram_tensor("out", (1, SEQ, D), F32, kind="ExternalOutput").ap()
    build(nc, w, out)
    r = run_bass_kernel_spmd(nc, [arrays], core_ids=[0])
    return r.results[0]["out"]
```

```python
import math
from contextlib import ExitStack

import numpy as np
import concourse.bass as bass
from concourse import mybir

F32 = mybir.dt.float32
F32R = mybir.dt.float32r
I32 = mybir.dt.int32
ALU = mybir.AluOpType
ACT = mybir.ActivationFunctionType
AX = mybir.AxisListType


def two_pi_parts():
    rest, parts = 2 * math.pi, []
    for _ in range(3):
        unit = 2.0 ** (math.floor(math.log2(rest)) - 7)
        parts.append(math.floor(rest / unit) * unit)
        rest -= parts[-1]
    return parts + [float(np.float32(rest))]


P = 128
SEQ = 1024
D = 1024
F = 2816
ST = SEQ // P
KT = D // P
HALF = 512
EPS = 1e-6
ROUND = 1.5 * 2.0 ** 23
TWO_PI_PARTS = two_pi_parts()
PI_DOWN = 3.1415925


def three_passes(pe, out, lhs_hi, lhs_lo, rhs_hi, rhs_lo, first, last):
    pe.matmul(out, lhs_hi, rhs_hi, start=first, stop=False)
    pe.matmul(out, lhs_hi, rhs_lo, start=False, stop=False)
    return pe.matmul(out, lhs_lo, rhs_hi, start=False, stop=last)


class Phase(ExitStack):

    def __init__(self, nc):
        super().__init__()
        self.taken = []

        def clear():
            if self.taken:
                nc.clear_and_free_semaphores(self.taken)
                nc.all_engine_barrier()
        self.callback(clear)


def semaphores(nc, ctx, tag):
    def sem(name):
        ctx.taken.append(nc.alloc_semaphore(f"{tag}_{name}"))
        return ctx.taken[-1]
    return sem


class Chain:

    def __init__(self, eng, s, n=0):
        self.eng, self.s, self.n = eng, s, n

    def __call__(self, ins):
        self.n += 1
        ins.then_inc(self.s, 1)
        self.eng.wait_ge(self.s, self.n)


NEWTON_STEPS = 5


def newton(link, var, root, out, tmp):
    dve = link.eng
    link(dve.reciprocal(out, root))
    link(dve.tensor_tensor(tmp, out, out, ALU.mult))
    link(dve.tensor_tensor(tmp, tmp, var, ALU.mult))
    link(dve.tensor_scalar(tmp, tmp, -0.5, 1.5, ALU.mult, ALU.add))
    link(dve.tensor_tensor(out, out, tmp, ALU.mult))


def whole_turns(link, ang, turns, scale, quarter):
    dve = link.eng
    link(dve.tensor_scalar(turns, ang, scale, quarter, ALU.mult, ALU.add))
    link(dve.tensor_scalar(turns, turns, ROUND, None, ALU.add))
    link(dve.tensor_scalar(turns, turns, ROUND, None, ALU.subtract))


def take_off_turns(link, ang, turns, shift):
    dve = link.eng
    for part in TWO_PI_PARTS:
        link(dve.scalar_tensor_tensor(out=ang, in0=turns, scalar=-part, in1=ang, op0=ALU.mult, op1=ALU.add))
    link(dve.tensor_scalar(ang, ang, shift, None, ALU.add))
    link(dve.tensor_scalar(ang, ang, PI_DOWN, -PI_DOWN, ALU.min, ALU.max))


class ColumnProduct:

    def __init__(self, nc, ctx, tag, w, tiles, rhs_hi, rhs_lo, psum, slot0=0, room=None, S=2):
        sb = lambda n, s, d=F32: ctx.enter_context(nc.sbuf_tensor(f"{tag}_{n}", s, d))
        sem = semaphores(nc, ctx, tag)
        self.K, self.S = w.shape[0] // P, S
        self.w, self.tiles, self.N = w.rearrange("(k p) f -> p k f", p=P), tiles, len(tiles)
        self.rhs_hi, self.rhs_lo = rhs_hi, rhs_lo
        self.raw = [sb(f"raw{i}", [P, self.K, P]) for i in range(S)]
        if room is None:
            self.hi = sb("hi", [P, S, self.K, P], F32R)
            self.lo = sb("lo", [P, S, self.K, P], F32R)
        else:
            size = S * self.K * P * 4
            self.hi, self.lo = (nc.alloc_sbuf_tensor_at(f"{tag}_{n}", [P, S, self.K, P], F32R, offset=room + i * size) for i, n in enumerate(("hi", "lo")))
        self.ps = [psum[:, slot0 + 2 * i:slot0 + 2 * i + 2, :] for i in range(2)]
        self.raw_in = [sem(f"raw_in{i}") for i in range(S)]
        self.hi_done, self.lo_done, self.mm_done = sem("hi_done"), sem("lo_done"), sem("mm_done")
        self.read = [sem(f"read{i}") for i in range(2)]

    def load(self, sp, n):
        if n >= self.N:
            return
        if n >= self.S:
            sp.wait_ge(self.lo_done, n - self.S + 1)
        sp.dma_start(self.raw[n % self.S][:], self.w[:, :, self.tiles[n]:self.tiles[n] + P]).then_inc(self.raw_in[n % self.S], 16)

    def high(self, act, n):
        if n >= self.N:
            return
        act.wait_ge(self.raw_in[n % self.S], 16 * (n // self.S + 1))
        if n >= self.S:
            act.wait_ge(self.mm_done, n - self.S + 1)
        act.copy(self.hi[:, n % self.S], self.raw[n % self.S][:]).then_inc(self.hi_done, 1)

    def low(self, dve, n):
        if n >= self.N:
            return
        dve.wait_ge(self.hi_done, n + 1)
        if n >= self.S:
            dve.wait_ge(self.mm_done, n - self.S + 1)
        dve.tensor_tensor(self.lo[:, n % self.S], self.raw[n % self.S][:], self.hi[:, n % self.S].bitcast(F32), ALU.subtract).then_inc(self.lo_done, 1)

    def product(self, pe, n, ready=None):
        pe.wait_ge(self.lo_done, n + 1)
        if n >= 2:
            pe.wait_ge(self.read[n % 2], n // 2)
        for k in range(self.K):
            if ready:
                ready(k)
            for half in range(2):
                sl = slice(half * HALF, (half + 1) * HALF)
                mm = three_passes(pe, self.ps[n % 2][:, half, :], self.hi[:, n % self.S, k, :], self.lo[:, n % self.S, k, :],
                                  self.rhs_hi[:, k, sl], self.rhs_lo[:, k, sl], k == 0, k == self.K - 1)
        mm.then_inc(self.mm_done, 1)


class RowProduct:

    def __init__(self, nc, ctx, tag, jobs, lhs, psum):
        sb = lambda n, s, d=F32: ctx.enter_context(nc.sbuf_tensor(f"{tag}_{n}", s, d))
        sem = semaphores(nc, ctx, tag)
        self.jobs, self.lhs, self.psum = jobs, lhs, psum
        self.raw = [sb(f"raw{i}", [P, HALF]) for i in range(2)]
        self.hi = sb("hi", [P, 2, HALF], F32R)
        self.lo = sb("lo", [P, 2, HALF], F32R)
        self.raw_in = [sem(f"raw_in{i}") for i in range(2)]
        self.hi_done, self.lo_done, self.k_done, self.mm_done, self.read = (sem(n) for n in ("hi_done", "lo_done", "k_done", "mm_done", "read"))

    def units(self):
        return [(j, k) for j in range(len(self.jobs)) for k in range(self.jobs[j][0].shape[0] // P)]

    def load(self, sp, n):
        units = self.units()
        w, parts, width = self.jobs[units[n][0]]
        k = units[n][1]
        if n >= 2:
            sp.wait_ge(self.lo_done, n - 1)
        for at, cols in parts:
            sp.dma_start(self.raw[n % 2][:, at:at + cols.stop - cols.start], w[k * P:(k + 1) * P, cols]).then_inc(self.raw_in[n % 2], 16)

    def arrived(self, n):
        units = self.units()
        return sum(16 * len(self.jobs[units[i][0]][1]) for i in range(n % 2, n + 1, 2))

    def high(self, act, n):
        units = self.units()
        if n >= len(units):
            return
        width = self.jobs[units[n][0]][2]
        act.wait_ge(self.raw_in[n % 2], self.arrived(n))
        if n >= 2:
            act.wait_ge(self.k_done, n - 1)
        act.copy(self.hi[:, n % 2, 0:width], self.raw[n % 2][:, 0:width]).then_inc(self.hi_done, 1)

    def low(self, eng, n):
        units = self.units()
        if n >= len(units):
            return
        width = self.jobs[units[n][0]][2]
        eng.wait_ge(self.hi_done, n + 1)
        if n >= 2:
            eng.wait_ge(self.k_done, n - 1)
        eng.tensor_tensor(self.lo[:, n % 2, 0:width], self.raw[n % 2][:, 0:width], self.hi[:, n % 2, 0:width].bitcast(F32), ALU.subtract).then_inc(self.lo_done, 1)

    def products(self, pe, ready=None):
        units = self.units()
        for n, (j, k) in enumerate(units):
            if ready and j == 0:
                ready(k)
            w, parts, width = self.jobs[j]
            last = k == w.shape[0] // P - 1
            pe.wait_ge(self.lo_done, n + 1)
            for m in range(ST):
                if k == 0 and j:
                    pe.wait_ge(self.read, (j - 1) * ST + m + 1)
                hi, lo = self.lhs(j, k, m)
                mm = three_passes(pe, self.psum[:, m, 0:width], hi, lo, self.hi[:, n % 2, 0:width], self.lo[:, n % 2, 0:width], k == 0, last)
                if m == ST - 1:
                    mm.then_inc(self.k_done, 1)
                elif last:
                    mm.then_inc(self.mm_done, 1)

    def wait_bank(self, eng, j, m):
        if m < ST - 1:
            eng.wait_ge(self.mm_done, j * (ST - 1) + m + 1)
        else:
            eng.wait_ge(self.k_done, sum(1 for u in self.units() if u[0] <= j))


class Norm:

    def __init__(self, nc, ctx, tag, gain, rows, ident, nT_hi, nT_lo, psum, dump):
        sb = lambda n, s, d=F32: ctx.enter_context(nc.sbuf_tensor(f"{tag}_{n}", s, d))
        sem = semaphores(nc, ctx, tag)
        self.gain, self.rows, self.ident = gain, rows, ident
        self.hi, self.lo, self.psum, self.dump = nT_hi, nT_lo, psum, dump
        self.gb = sb("gb", [P, D])
        self.xn = sb("xn", [P, 2, D])
        self.stat = sb("stat", [P, 5, ST])
        self.s_gain, self.s_sq, self.s_var, self.s_sqrt, self.s_rstd = map(sem, ("gain", "sq", "var", "sqrt", "rstd"))
        self.s_xn, self.s_tr, self.s_hi, self.s_lo = map(sem, ("xn", "tr", "nhi", "nlo"))

    def load(self, sp):
        sp.dma_start(self.gb[:], self.gain.rearrange("(a d) -> a d", a=1).broadcast_to([P, D])).then_inc(self.s_gain, 16)

    GROUP = ST // 2

    def act_square(self, act, m):
        if m >= 4:
            act.wait_ge(self.s_sq, m - 3)
        act.activation(self.dump(m % 4), self.rows[:, m, :], ACT.Square, accum_out=self.stat[:, 0, m:m + 1]).then_inc(self.s_sq, 1)

    def act_root(self, act, g):
        sl = slice(g * self.GROUP, (g + 1) * self.GROUP)
        act.wait_ge(self.s_var, g + 1)
        act.activation(self.stat[:, 2, sl], self.stat[:, 1, sl], ACT.Sqrt).then_inc(self.s_sqrt, 1)

    def act(self, act, rows_ready, between):
        def square(m):
            rows_ready(act, m)
            self.act_square(act, m)
        for m in range(4):
            square(m)
        self.act_root(act, 0)
        square(4)
        square(5)
        for m in range(ST):
            self.act_high(act, m)
            between(m)
            if m < 2:
                square(m + 6)
            if m == 1:
                self.act_root(act, 1)

    def dve_var(self, dve, g):
        st, sl = self.stat, slice(g * self.GROUP, (g + 1) * self.GROUP)
        dve.wait_ge(self.s_sq, (g + 1) * self.GROUP)
        dve.tensor_scalar(st[:, 1, sl], st[:, 0, sl], 1.0 / D, EPS, ALU.mult, ALU.add).then_inc(self.s_var, 1)

    def dve_rstd(self, dve, g):
        st, sl = self.stat, slice(g * self.GROUP, (g + 1) * self.GROUP)
        dve.wait_ge(self.s_sqrt, g + 1)
        newton(Chain(dve, self.s_rstd, g * NEWTON_STEPS), st[:, 1, sl], st[:, 2, sl], st[:, 3, sl], st[:, 4, sl])

    def dve_rows(self, dve, m):
        if m == 0:
            dve.wait_ge(self.s_gain, 16)
        if m >= 2:
            dve.wait_ge(self.s_tr, m - 1)
        dve.scalar_tensor_tensor(out=self.xn[:, m % 2, :], in0=self.rows[:, m, :], scalar=self.stat[:, 3, m:m + 1],
                                 in1=self.gb[:], op0=ALU.mult, op1=ALU.mult).then_inc(self.s_xn, 1)

    def banks(self, m):
        first = 2 * m if m < 4 else 4 + 2 * (m % 2)
        return self.psum[:, first:first + 2, :]

    def turned(self, m):
        return self.banks(m).rearrange("p a (k s) -> p (a k) s", s=P)

    def dve_low(self, dve, m):
        part = lambda a: a[:, :, m * P:(m + 1) * P]
        dve.wait_ge(self.s_hi, m + 1)
        dve.tensor_tensor(part(self.lo), self.turned(m), part(self.hi).bitcast(F32), ALU.subtract).then_inc(self.s_lo, 1)

    def dve(self, dve):
        self.dve_var(dve, 0)
        self.dve_rstd(dve, 0)
        self.dve_rows(dve, 0)
        self.dve_rows(dve, 1)
        for m in range(ST):
            self.dve_low(dve, m)
            if m == 1:
                self.dve_var(dve, 1)
                self.dve_rstd(dve, 1)
            if m + 2 < ST:
                self.dve_rows(dve, m + 2)

    def act_high(self, act, m):
        act.wait_ge(self.s_tr, m + 1)
        act.copy(self.hi[:, :, m * P:(m + 1) * P], self.turned(m)).then_inc(self.s_hi, 1)

    def pe(self, pe, m):
        pe.wait_ge(self.s_xn, m + 1)
        if m >= 4:
            pe.wait_ge(self.s_lo, m - 1)
        banks = self.banks(m)
        for k in range(KT):
            t = pe.transpose(banks[:, k // 4, (k % 4) * P:(k % 4 + 1) * P], self.xn[:, m % 2, k * P:(k + 1) * P], self.ident[:])
        t.then_inc(self.s_tr, 1)


class Finish:
    GROUPS = (slice(0, 4), slice(4, 7), slice(7, 8))

    def __init__(self, nc, ctx, tag, finish, norm, added, raw, dump):
        sem = semaphores(nc, ctx, tag)
        (self.gain, self.out), self.norm, self.dump = finish, norm, dump
        self.slots = [r[:] for r in raw] + [norm.xn[:, i, :] for i in range(2)]
        self.added, self.before = added, (F // (2 * P) - 1) * ST
        self.s_gain, self.s_sq, self.s_var, self.s_sqrt, self.s_link, self.s_o = map(sem, ("fgain", "fsq", "fvar", "fsqrt", "flink", "fo"))
        self.s_out = [sem(f"out{i}") for i in range(len(self.slots))]

    def sync(self, sp):
        sp.wait_ge(self.norm.s_xn, ST)
        sp.dma_start(self.norm.gb[:], self.gain.rearrange("(a d) -> a d", a=1).broadcast_to([P, D])).then_inc(self.s_gain, 16)
        NS = len(self.slots)
        for m in range(ST):
            sp.wait_ge(self.s_o, m + 1)
            sp.dma_start(self.out[m * P:(m + 1) * P, :], self.slots[m % NS]).then_inc(self.s_out[m % NS], 16)
        for i in range(NS):
            sp.wait_ge(self.s_out[i], 16 * len(range(i, ST, NS)))

    def scalar(self, act):
        st = self.norm.stat
        for g, sl in enumerate(self.GROUPS):
            for m in range(sl.start, sl.stop):
                act.wait_ge(self.added, self.before + m + 1)
                act.activation(self.dump[:, m, :], self.norm.rows[:, m, :], ACT.Square, accum_out=st[:, 0, m:m + 1]).then_inc(self.s_sq, 1)
            act.wait_ge(self.s_var, g + 1)
            act.activation(st[:, 2, sl], st[:, 1, sl], ACT.Sqrt).then_inc(self.s_sqrt, 1)

    def vector(self, dve, add):
        st, NS = self.norm.stat, len(self.slots)

        def var(g):
            sl = self.GROUPS[g]
            dve.wait_ge(self.s_sq, sl.stop)
            dve.tensor_scalar(st[:, 1, sl], st[:, 0, sl], 1.0 / D, EPS, ALU.mult, ALU.add).then_inc(self.s_var, 1)

        def rstd(g):
            sl = self.GROUPS[g]
            dve.wait_ge(self.s_sqrt, g + 1)
            newton(Chain(dve, self.s_link, g * NEWTON_STEPS), st[:, 1, sl], st[:, 2, sl], st[:, 3, sl], st[:, 4, sl])

        def row(m):
            if m >= NS:
                dve.wait_ge(self.s_out[m % NS], 16)
            dve.scalar_tensor_tensor(out=self.slots[m % NS], in0=self.norm.rows[:, m, :], scalar=st[:, 3, m:m + 1], in1=self.norm.gb[:],
                                     op0=ALU.mult, op1=ALU.mult).then_inc(self.s_o, 1)
        for m in range(5):
            add(m)
        var(0)
        add(5)
        rstd(0)
        dve.wait_ge(self.s_gain, 16)
        row(0)
        row(1)
        add(6)
        row(2)
        row(3)
        add(7)
        var(1)
        rstd(1)
        row(4)
        var(2)
        row(5)
        rstd(2)
        row(6)
        row(7)


def ffn_phase(nc, tag, gain, w_gate, w_up, w_down, rows, ident, psum, x=None, finish=None):
    NP = F // (2 * P)
    with Phase(nc) as ctx:
        sb = lambda n, s, d=F32: ctx.enter_context(nc.sbuf_tensor(f"{tag}_{n}", s, d))
        sem = semaphores(nc, ctx, tag)
        nT_hi = sb("nT_hi", [P, KT, SEQ], F32R)
        nT_lo = sb("nT_lo", [P, KT, SEQ], F32R)
        raw = [sb(f"raw{i}", [P, D]) for i in range(3)]
        w_hi = sb("w_hi", [P, 2, 2, D], F32R)
        w_lo = sb("w_lo", [P, 2, 2, D], F32R)
        d_hi = sb("d_hi", [P, 2, D], F32R)
        d_lo = sb("d_lo", [P, 2, D], F32R)
        hT_hi = sb("hT_hi", [P, 2, 2, SEQ], F32R)
        hT_lo = sb("hT_lo", [P, 2, 2, SEQ], F32R)
        norm = Norm(nc, ctx, tag, gain, rows, ident, nT_hi, nT_lo, psum, lambda i: hT_lo[:, i // 2, i % 2, :])
        h = norm.xn
        x_in = [sem(f"x_in{m}") for m in range(ST if x is not None else 0)]
        raw_in = [sem(f"raw_in{i}") for i in range(3)]
        w_hi_done, w_lo_done = sem("w_hi_done"), sem("w_lo_done")
        gu_done, silu_done, mult_done = sem("gu_done"), sem("silu_done"), sem("mult_done")
        h_hi_done, h_lo_done = sem("h_hi_done"), sem("h_lo_done")
        down_tile, added = sem("down_tile"), sem("added")

        tail = Finish(nc, ctx, tag, finish, norm, added, raw, nT_lo) if finish else None

        gate_v = w_gate.rearrange("(k p) f -> p k f", p=P)
        up_v = w_up.rearrange("(k p) f -> p k f", p=P)
        ps = lambda slot, half: psum[:, 2 * slot + half, :]
        ps2 = lambda slot: psum[:, 2 * slot:2 * slot + 2, :]
        two = lambda ap: ap.rearrange("p (a b) -> p a b", a=2)

        def gu_units(p):
            return 4 + 6 * (p - 1)

        def down_unit(p):
            return 4 + 6 * p + 4

        block = ctx.enter_context(nc.Block())

        @block.sync
        def _(sp):
            def load_rows(tiles):
                if x is not None:
                    for m in tiles:
                        sp.dma_start(rows[:, m, :], x[m * P:(m + 1) * P, :]).then_inc(x_in[m], 16)

            def unit(n, slot, src, third):
                if not isinstance(n, int) or n >= 3:
                    sp.wait_ge(w_lo_done, n - 2)
                sp.dma_start(raw[slot][:] if len(src.shape) == 2 else raw[slot][:].rearrange("p (k f) -> p k f", k=KT), src).then_inc(raw_in[slot], 16)

            def gu(p, t, base):
                for j, v in enumerate((gate_v, up_v)):
                    n = base + 2 * t + j
                    unit(n, (slot0 + 2 * t + j) % 3, v[:, :, bass.ds((2 * p + t) * P, P)], None)

            def down(p, base, only=False):
                for j in range(2):
                    n = base + j
                    unit(n, (slotd + j) % 3, w_down[bass.ds((2 * p + j) * P, P), :], None)

            slot0 = 0
            load_rows(range(ST // 2))
            norm.load(sp)
            load_rows(range(ST // 2, ST))
            for t in range(2):
                gu(0, t, 0)
            slot0, slotd = 4 % 3, (4 + 4) % 3
            with sp.Fori(0, NP - 1) as p:
                for t in range(2):
                    gu(p + 1, t, p * 6 + 4)
                down(p, p * 6 + 8)
            slotd = (4 + 6 * (NP - 1)) % 3
            down(NP - 1, 4 + 6 * (NP - 1))
            if tail:
                tail.sync(sp)

        def split_high(act, slot, n3, dst):
            act.wait_ge(raw_in[slot], n3 * 16)
            act.copy(dst, raw[slot][:]).then_inc(w_hi_done, 1)

        def split_low(dve, slot, n, dst, hi):
            dve.wait_ge(w_hi_done, n + 1)
            dve.tensor_tensor(dst, raw[slot][:], hi.bitcast(F32), ALU.subtract).then_inc(w_lo_done, 1)

        @block.scalar
        def _(act):
            def between(m):
                if 2 <= m < 6:
                    n = m - 2
                    split_high(act, n % 3, n // 3 + 1, w_hi[:, n // 2, n % 2, :])
            norm.act(act, (lambda e, m: e.wait_ge(x_in[m], 16)) if x is not None else (lambda e, m: None), between)

            def pair(p, par, first=False, last=False):
                for t in range(2):
                    tile = p * 2 + t
                    act.wait_ge(gu_done, p * 4 + 2 * t + 1)
                    if not first:
                        act.wait_ge(h_lo_done, p * 2 + t - 1)
                    else:
                        act.wait_ge(norm.s_tr, ST)
                    act.activation(two(h[:, t, :]), ps2(2 * t), ACT.Silu).then_inc(silu_done, 1)
                    if not last:
                        for j in range(2):
                            act.wait_ge(gu_done, p * 4 + 2 * t + 1 + j)
                            u = 2 * t + j + 4
                            split_high(act, u % 3, p * 2 + u // 3 + 1, w_hi[:, t, j, :])
                    act.wait_ge(mult_done, p * 2 + t + 1)
                    if isinstance(p, int) and p < 2:
                        pass
                    else:
                        act.wait_ge(down_tile, p * 8 - 8)
                    act.copy(hT_hi[:, par, t, :], h[:, t, :]).then_inc(h_hi_done, 1)
                if not first:
                    act.wait_ge(down_tile, p * 8)
                for j in range(2):
                    u = 8 + j if not last else 4 + j
                    split_high(act, u % 3, p * 2 + u // 3 + 1, d_hi[:, j, :])

            pair(0, 0, first=True)
            pair(1, 1)
            with act.Fori(1, NP // 2) as q:
                pair(q * 2, 0)
                pair(q * 2 + 1, 1)
            pair(NP - 1, (NP - 1) % 2, last=True)
            if tail:
                tail.scalar(act)

        @block.vector
        def _(dve):
            norm.dve(dve)

            def add(q, m):
                dve.wait_ge(down_tile, q * 8 + m + 1)
                dve.scalar_tensor_tensor(out=two(rows[:, m, :]), in0=ps2(m % 4), scalar=0.5, in1=two(rows[:, m, :]),
                                         op0=ALU.mult, op1=ALU.add).then_inc(added, 1)

            def pair(p, par, first=False, last=False):
                base = p * 6 + 4
                for t in range(2):
                    def low(j):
                        if not last:
                            dve.wait_ge(gu_done, p * 4 + 2 * t + 1 + j)
                            u = 2 * t + j
                            split_low(dve, (u + 4) % 3, base + u, w_lo[:, t, j, :], w_hi[:, t, j, :])
                    low(0)
                    dve.wait_ge(silu_done, p * 2 + t + 1)
                    dve.wait_ge(gu_done, p * 4 + 2 * t + 2)
                    dve.tensor_tensor(two(h[:, t, :]), ps2(2 * t + 1), two(h[:, t, :]), ALU.mult).then_inc(mult_done, 1)
                    low(1)
                    dve.wait_ge(h_hi_done, p * 2 + t + 1)
                    dve.tensor_tensor(hT_lo[:, par, t, :], h[:, t, :], hT_hi[:, par, t, :].bitcast(F32), ALU.subtract).then_inc(h_lo_done, 1)
                if not first:
                    for m in range(ST):
                        add(p - 1, m)
                for j in range(2):
                    u = 4 + j if not last else j
                    split_low(dve, (u + 4) % 3, base + u, d_lo[:, j, :], d_hi[:, j, :])

            pair(0, 0, first=True)
            pair(1, 1)
            with dve.Fori(1, NP // 2) as q:
                pair(q * 2, 0)
                pair(q * 2 + 1, 1)
            pair(NP - 1, (NP - 1) % 2, last=True)
            if tail:
                tail.vector(dve, lambda m: add(NP - 1, m))
            else:
                for m in range(ST):
                    add(NP - 1, m)

        @block.gpsimd
        def _(pool):
            for n in range(4):
                split_low(pool, n % 3, n, w_lo[:, n // 2, n % 2, :], w_hi[:, n // 2, n % 2, :])

        @block.tensor
        def _(pe):
            def gate_up_half(t, j, half):
                for k in range(KT):
                    mm = three_passes(pe, ps(2 * t + j, half), w_hi[:, t, j, k * P:(k + 1) * P], w_lo[:, t, j, k * P:(k + 1) * P],
                                      nT_hi[:, k, half * HALF:(half + 1) * HALF], nT_lo[:, k, half * HALF:(half + 1) * HALF],
                                      k == 0, k == KT - 1)
                return mm

            def gate_up_first():
                for m in range(6):
                    norm.pe(pe, m)
                for n in range(4):
                    pe.wait_ge(w_lo_done, n + 1)
                    pe.wait_ge(norm.s_lo, (4, 4, 7, 8)[n])
                    gate_up_half(n // 2, n % 2, 0)
                    if n < 2:
                        norm.pe(pe, n + 6)
                pe.wait_ge(norm.s_lo, ST)
                for n in range(4):
                    gate_up_half(n // 2, n % 2, 1).then_inc(gu_done, 1)

            def gate_up(p):
                for t in range(2):
                    for j in range(2):
                        pe.wait_ge(w_lo_done, p * 6 + 2 * t + j - 1)
                        pe.wait_ge(mult_done, p * 2 + t - 1)
                        if not isinstance(p, int) or p >= 2:
                            pe.wait_ge(added, p * 8 - 8)
                        for half in range(2):
                            mm = gate_up_half(t, j, half)
                        mm.then_inc(gu_done, 1)

            def down(q, par, last=False):
                pe.wait_ge(h_lo_done, q * 2 + 2)
                pe.wait_ge(w_lo_done, q * 6 + 10 if not last else 4 + 6 * (NP - 1) + 2)
                for m in range(ST):
                    if m >= 4:
                        pe.wait_ge(added, q * 8 + m - 3)
                    elif last:
                        pe.wait_ge(added, 8 * (NP - 1) - 4 + m + 1)
                    else:
                        pe.wait_ge(mult_done, q * 2 + 2 + m // 2 + 1)
                    for half in range(2):
                        for t in range(2):
                            mm = three_passes(pe, ps(m % 4, half), hT_hi[:, par, t, m * P:(m + 1) * P], hT_lo[:, par, t, m * P:(m + 1) * P],
                                              d_hi[:, t, half * HALF:(half + 1) * HALF], d_lo[:, t, half * HALF:(half + 1) * HALF],
                                              t == 0, t == 1)
                    mm.then_inc(down_tile, 1)

            gate_up_first()
            gate_up(1)
            down(0, 0)
            with pe.Fori(1, NP // 2) as q:
                gate_up(q * 2)
                down(q * 2 - 1, 1)
                gate_up(q * 2 + 1)
                down(q * 2, 0)
            gate_up(NP - 1)
            down(NP - 2, 1)
            down(NP - 1, 0, last=True)


def make_ident(nc, ident, s_id):
    with nc.Block() as block:
        @block.gpsimd
        def _(pool):
            pool.memset(ident[:], 0.0).then_inc(s_id, 1)
            pool.wait_ge(s_id, 1)
            pool.affine_select(out=ident[:], in_=ident[:], compare_op=ALU.not_equal, fill=1.0, base=0,
                               pattern=[[-1, P]], channel_multiplier=1).then_inc(s_id, 1)


GROUPS, STATE, SG = 32, 64, 16
T = P // SG
CH = SEQ // T
WIDTH = GROUPS * SG
SLOTS = 2 * T - 1
QR, KVR, NOPE, ROPE, VH, HEADS = 256, 128, 64, 32, 64, 8
OFF_CKV = QR
OFF_KR = OFF_CKV + KVR
OFF_U = OFF_KR + ROPE
OFF_GA = OFF_U + WIDTH
OFF_GS = OFF_GA + D
ZW = OFF_KR + 2 * ROPE
GATES_BESIDE_SETUP = 6
TURN_AFTER = (3, 4)
SCALE = (NOPE + ROPE) ** -0.5


def tools(nc, ctx, tag):
    sb = lambda n, s, d=F32: ctx.enter_context(nc.sbuf_tensor(f"{tag}_{n}", s, d))
    return sb, semaphores(nc, ctx, tag)


def project_phase(nc, w, rows, ident, psum, nT_hi, nT_lo, u, kept, latent_rows, trig_rows):
    with Phase(nc) as ctx:
        sb, sem = tools(nc, ctx, "pj")
        zrow = sb("zrow", [P, ST, ZW])
        norm = Norm(nc, ctx, "pjn", w["mix_norm"][0], rows, ident, nT_hi, nT_lo, psum, lambda i: u[:, 8 * i:8 * i + 8].rearrange("p g t i -> p (g t i)"))
        w_in = w["w_in"][0]
        half = ROPE // 2
        latent = [(0, slice(0, OFF_U)), (OFF_U, slice(OFF_KR + half, OFF_U)), (OFF_U + half, slice(OFF_KR, OFF_KR + half))]

        def lhs(j, k, m):
            sl = slice(m * P, (m + 1) * P) if j == 0 else slice(m, SEQ, T)
            return nT_hi[:, k, sl], nT_lo[:, k, sl]

        rp = RowProduct(nc, ctx, "rp", [(w_in, latent, ZW), (w_in, [(0, slice(OFF_U, OFF_GA))], WIDTH)], lhs, psum)
        pos, ang, turns, cst = sb("pos", [P, SEQ], I32), sb("ang", [P, SEQ]), sb("turns", [P, SEQ]), sb("cst", [P, 4])
        gz, zstat = sb("gz", [P, QR + KVR]), sb("zstat", [P, 5, 2, ST])
        Rp, parts = slice(64, 128), (slice(0, QR), slice(QR, QR + KVR))
        dump = norm.xn[:].rearrange("p a d -> p (a d)")
        s_kept, s_latent, s_pos, s_cst, s_gz, s_zsq, s_zvar, s_zsqrt, s_zlink, s_zrow, s_ang, s_trig, s_trig_out = map(
            sem, ("kept", "latent", "pos", "cst", "gz", "zsq", "zvar", "zsqrt", "zlink", "zrow", "ang", "trig", "trig_out"))
        NU = len(rp.units())
        block = ctx.enter_context(nc.Block())

        @block.sync
        def _(sp):
            norm.load(sp)
            rp.load(sp, 0)
            rp.load(sp, 1)
            sp.dma_start(kept.rearrange("(m p) d -> p m d", p=P), rows[:]).then_inc(s_kept, 16)
            sp.dma_start(pos[Rp, :], w["positions"][0:1, :].broadcast_to([64, SEQ])).then_inc(s_pos, 16)
            sp.dma_start(cst[:], w["rope_const"]).then_inc(s_cst, 16)
            for part, gain in zip(parts, (w["q_norm"], w["kv_norm"])):
                sp.dma_start(gz[:, part], gain[0:1, :].broadcast_to([P, part.stop - part.start])).then_inc(s_gz, 16)
            for n in range(2, NU):
                rp.load(sp, n)
            sp.wait_ge(s_trig, 1)
            sp.dma_start(trig_rows, ang[Rp, :]).then_inc(s_trig_out, 16)
            sp.wait_ge(s_zrow, 2 * ST)
            sp.dma_start(latent_rows.rearrange("(m p) z -> p m z", p=P), zrow[:]).then_inc(s_latent, 16)
            sp.wait_ge(s_kept, 16)
            sp.wait_ge(s_latent, 16)
            sp.wait_ge(s_trig_out, 16)

        @block.scalar
        def _(act):
            norm.act(act, lambda e, m: None, lambda m: None)
            for j in range(2):
                for k in range(KT):
                    rp.high(act, j * KT + k)
                    if j == 1 and k == 1:
                        for m in range(ST):
                            rp.wait_bank(act, 0, m)
                            act.copy(zrow[:, m, :], psum[:, m, 0:ZW]).then_inc(rp.read, 1)
                    if j == 1 and k in (2, 3):
                        for m in range(4 * k - 8, 4 * k - 4):
                            act.wait_ge(rp.read, m + 1)
                            if m >= 5:
                                act.wait_ge(s_zsq, 2 * (m - 4))
                            for i, part in enumerate(parts):
                                at = m % 5 * (QR + KVR)
                                act.activation(dump[:, at + part.start:at + part.stop], zrow[:, m, part], ACT.Square,
                                               accum_out=zstat[:, 0, i, m:m + 1]).then_inc(s_zsq, 1)
                    if j == 1 and k == 5:
                        act.wait_ge(s_zvar, 2)
                        act.activation(zstat[:, 2], zstat[:, 1], ACT.Sqrt).then_inc(s_zsqrt, 1)
                        act.wait_ge(s_ang, 1)
                        act.activation(ang[Rp, :], ang[Rp, :], ACT.Sin).then_inc(s_trig, 1)
            for m in range(ST):
                rp.wait_bank(act, 1, m)
                act.copy(u[:, :, m, :], psum[:, m, :].rearrange("p (g i) -> p g i", i=SG)).then_inc(rp.read, 1)

        @block.vector
        def _(dve):
            norm.dve(dve)
            link = Chain(dve, s_zlink)
            for n in range(NU):
                rp.low(dve, n)
                if n == 1:
                    dve.wait_ge(s_pos, 16)
                    dve.wait_ge(s_cst, 16)
                    link(dve.tensor_copy(ang[Rp], pos[Rp]))
                    link(dve.tensor_scalar(ang[Rp], ang[Rp], cst[Rp, 0:1], None, ALU.mult))
                if n == 2:
                    whole_turns(link, ang[Rp], turns[Rp], cst[Rp, 1:2], cst[Rp, 2:3])
                if n == 4:
                    take_off_turns(link, ang[Rp], turns[Rp], cst[Rp, 3:4])
                    dve.sem_inc(s_ang, 1)
                if n == KT + 5:
                    dve.wait_ge(s_zsq, 2 * ST)
                    for i, part in enumerate(parts):
                        dve.tensor_scalar(zstat[:, 1, i], zstat[:, 0, i], 1.0 / (part.stop - part.start), EPS, ALU.mult, ALU.add).then_inc(s_zvar, 1)
                if n == KT + 6:
                    dve.wait_ge(s_zvar, 2)
                    dve.wait_ge(s_zsqrt, 1)
                    newton(link, zstat[:, 1], zstat[:, 2], zstat[:, 3], zstat[:, 4])
                    dve.wait_ge(s_gz, 32)
                if n >= KT + 6:
                    for m in range(ST // 2 * (n - KT - 6), ST // 2 * (n - KT - 5)):
                        for i, part in enumerate(parts):
                            dve.scalar_tensor_tensor(out=zrow[:, m, part], in0=zrow[:, m, part], scalar=zstat[:, 3, i, m:m + 1], in1=gz[:, part],
                                                     op0=ALU.mult, op1=ALU.mult).then_inc(s_zrow, 1)

        @block.tensor
        def _(pe):
            for m in range(ST):
                norm.pe(pe, m)
            pe.wait_ge(norm.s_lo, ST)
            rp.products(pe)


class Gates:

    def __init__(self, nc, ctx, tag, w_in, first, end, nT_hi, nT_lo, psum, gates, sig, room=None):
        sem = semaphores(nc, ctx, tag)
        self.gp = ColumnProduct(nc, ctx, tag, w_in, [OFF_GA + n * P for n in range(first, end)], nT_hi, nT_lo, psum, room=room)
        self.first, self.N, self.gates, self.sig = first, end - first, gates, sig
        self.out = [sem("out0"), sem("out1")]

    def sync(self, sp):
        gp = self.gp
        for n in range(self.N):
            if n + 2 < self.N:
                gp.load(sp, n + 2)
            sp.wait_ge(gp.read[n % 2], n // 2 + 1)
            at = (self.first + n) * P
            sp.dma_start(self.gates[at:at + P, :], self.sig[:, n % 2, :]).then_inc(self.out[n % 2], 16)
        for i in range(2):
            sp.wait_ge(self.out[i], 16 * len(range(i, self.N, 2)))

    def sigmoid(self, act, n):
        gp = self.gp
        act.wait_ge(gp.mm_done, n + 1)
        if n >= 2:
            act.wait_ge(self.out[n % 2], 16 * (n // 2))
        act.activation(self.sig[:, n % 2, :].rearrange("p (a b) -> p a b", a=2), gp.ps[n % 2], ACT.Sigmoid).then_inc(gp.read[n % 2], 1)
        gp.high(act, n + 2)


def ssm_setup_phase(nc, w, ident, psum, nT_hi, nT_lo, gates, E_mat, C_mat, lam8, Bb, C0, tmp):
    with Phase(nc) as ctx:
        sb, sem = tools(nc, ctx, "sa")
        lam_raw = sb("lam_raw", [GROUPS, 2, P])
        ldt = sb("ldt", [P, GROUPS])
        b_raw = sb("b_raw", [P, 2, GROUPS, SG])
        c_raw = sb("c_raw", [P, 2, 4, P])
        lam = sb("lam", [P, 2, GROUPS])
        sc = sb("sc", [P, 9, GROUPS])
        pw = sb("pw", [P, T + 1, 2, GROUPS])
        PP = sb("PP", [P, 2, T, GROUPS])
        sig = sb("sig", [P, 2, SEQ])
        X = [e.rearrange("p g (t i) -> p g t i", i=SG) for e in E_mat]
        side = Gates(nc, ctx, "g1", w["w_in"][0], 0, GATES_BESIDE_SETUP, nT_hi, nT_lo, psum, gates, sig)
        names = "lam b c tr mag ang sin dve xt xe".split()
        s = {n: sem(n) for n in names}
        s_ldt, s_cf, s_negc = sem("ldt_in"), sem("cf"), sem("negc")
        block = ctx.enter_context(nc.Block())

        @block.sync
        def _(sp):
            side.gp.load(sp, 0)
            side.gp.load(sp, 1)
            for c, a in enumerate((w["ssm_lambda_re"], w["ssm_lambda_im"])):
                sp.dma_start(lam_raw[:, c, :].rearrange("g (d p) -> g d p", d=2), a[0].rearrange("d g p -> g d p")).then_inc(s["lam"], 16)
            for d in range(2):
                h = slice(64 * d, 64 * d + 64)
                sp.dma_start(ldt[h, :], w["ssm_log_dt"][0, d:d + 1, :].broadcast_to([64, GROUPS])).then_inc(s_ldt, 16)
                for c, a in enumerate((w["ssm_b_re"], w["ssm_b_im"])):
                    sp.dma_start(b_raw[h, c], a[0, d].rearrange("g p i -> p g i")).then_inc(s["b"], 16)
                for c, a in enumerate((w["ssm_c_re"], w["ssm_c_im"])):
                    sp.dma_start(c_raw[:, c, :, h], a[0, d].rearrange("(b r) i p -> (r i) b p", b=4)).then_inc(s["c"], 16)
            side.sync(sp)

        @block.tensor
        def _(pe):
            pe.wait_ge(s["lam"], 32)
            for c in range(2):
                mm = pe.transpose(psum[:, 4, c * GROUPS:(c + 1) * GROUPS], lam_raw[:, c, :], ident[0:GROUPS, 0:GROUPS])
            mm.then_inc(s["tr"], 1)
            side.gp.product(pe, 0)
            pe.wait_ge(s["c"], 64)
            for c in range(2):
                for b in range(4):
                    mm = pe.transpose(psum[:, 5 + c, b * P:(b + 1) * P], c_raw[:, c, b, :], ident[:])
                mm.then_inc(s["tr"], 1)

            def turn(c):
                pe.wait_ge(s_cf, c + 1)
                if c == 0:
                    pe.wait_ge(s_negc, 2)
                for q in range(8 * c, 8 * c + 8):
                    if q >= 4:
                        pe.wait_ge(s["xe"], q - 3)
                    for g in range(4):
                        mm = pe.transpose(psum[:, 4 + q % 4, g * P:(g + 1) * P], X[c][:, q % 8 * 4 + g, :, :].rearrange("p t i -> p (t i)"), ident[:])
                    mm.then_inc(s["xt"], 1)
            for n in range(1, side.N):
                side.gp.product(pe, n)
                if n in TURN_AFTER:
                    turn(TURN_AFTER.index(n))

        @block.scalar
        def _(act):
            side.gp.high(act, 0)
            act.wait_ge(s["tr"], 1)
            act.copy(lam[:], psum[:, 4, 0:2 * GROUPS].rearrange("p (c g) -> p c g", c=2)).then_inc(s["mag"], 1)
            act.wait_ge(s_ldt, 32)
            act.activation(sc[:, 0, :], ldt[:], ACT.Exp).then_inc(s["mag"], 1)
            act.wait_ge(s["dve"], 2)
            act.activation(sc[:, 3, :], sc[:, 1, :], ACT.Exp).then_inc(s["mag"], 1)
            side.gp.high(act, 1)
            act.wait_ge(s["ang"], 1)
            act.activation(sc[:, 4:6, :], sc[:, 4:6, :], ACT.Sin).then_inc(s["sin"], 1)
            act.wait_ge(s["tr"], 3)
            act.copy(C0[:, 0].rearrange("p g i -> p (g i)"), psum[:, 5, :]).then_inc(s_negc, 1)
            act.mul(C0[:, 1].rearrange("p g i -> p (g i)"), psum[:, 6, :], -1.0).then_inc(s_negc, 1)
            for n in range(side.N):
                side.sigmoid(act, n)
                if n in TURN_AFTER:
                    c = TURN_AFTER.index(n)
                    for q in range(8 * c, 8 * c + 8):
                        g0 = q % 8 * 4
                        act.wait_ge(s["xt"], q + 1)
                        act.copy(E_mat[c][:, g0:g0 + 4, :], psum[:, 4 + q % 4, :].rearrange("p (g s) -> p g s", g=4)).then_inc(s["xe"], 1)

        @block.gpsimd
        def _(pool):
            pool.wait_ge(side.gp.lo_done, 1)
            for n in range(1, side.N):
                side.gp.low(pool, n)

        @block.vector
        def _(dve):
            side.gp.low(dve, 0)
            link = Chain(dve, s["dve"])
            mul = lambda o, a, b: link(dve.tensor_tensor(o, a, b, ALU.mult))
            add = lambda o, a, b: link(dve.tensor_tensor(o, a, b, ALU.add))
            sub = lambda o, a, b: link(dve.tensor_tensor(o, a, b, ALU.subtract))
            dve.wait_ge(s["mag"], 2)
            row = lambda i: sc[:, i, :]
            mul(row(1), lam[:, 0], row(0))
            mul(row(2), lam[:, 1], row(0))
            link(dve.tensor_copy(row(4), row(2)))
            link(dve.tensor_copy(row(5), row(2)))
            for ang, quarter in ((row(4), 0.0), (row(5), 0.25)):
                whole_turns(link, ang, row(6), 1 / (2 * math.pi), quarter)
                take_off_turns(link, ang, row(6), 2 * math.pi * quarter)
            dve.sem_inc(s["ang"], 1)
            dve.wait_ge(s["mag"], 3)
            dve.wait_ge(s["sin"], 1)
            link(dve.memset(pw[:, 0, 0], 1.0))
            link(dve.memset(pw[:, 0, 1], 0.0))
            mul(pw[:, 1, 0], row(3), row(5))
            mul(pw[:, 1, 1], row(3), row(4))
            lre, lim, bre, bim = lam[:, 0], lam[:, 1], pw[:, 1, 0], pw[:, 1, 1]
            mul(row(0), lre, lre)
            mul(row(1), lim, lim)
            add(row(0), row(0), row(1))
            link(dve.reciprocal(row(2), row(0)))
            link(dve.tensor_scalar(row(6), bre, -1.0, None, ALU.add))
            mul(row(7), row(6), lre)
            mul(row(8), bim, lim)
            add(row(7), row(7), row(8))
            mul(row(7), row(7), row(2))
            mul(row(8), bim, lre)
            mul(row(5), row(6), lim)
            sub(row(8), row(8), row(5))
            mul(row(8), row(8), row(2))
            dve.wait_ge(s["b"], 64)
            wide = lambda a: a.unsqueeze(2).broadcast_to([P, GROUPS, SG])
            t0, t1 = (tmp[:, z * WIDTH:(z + 1) * WIDTH].rearrange("p (g i) -> p g i", i=SG) for z in range(2))
            kre, kim = wide(row(7)), wide(row(8))
            mul(t0, b_raw[:, 0], kre)
            mul(t1, b_raw[:, 1], kim)
            sub(Bb[:, 0], t0, t1)
            mul(t0, b_raw[:, 1], kre)
            mul(t1, b_raw[:, 0], kim)
            add(Bb[:, 1], t0, t1)

            def complex_mul(o, a, b, n):
                br, bi = (b[:, i:i + 1, :].broadcast_to([P, n, GROUPS]) for i in range(2))
                x, y = (tmp[:, z * n * GROUPS:(z + 1) * n * GROUPS].rearrange("p (n g) -> p n g", n=n) for z in range(2))
                mul(x, a[:, :, 0], br)
                mul(y, a[:, :, 1], bi)
                sub(o[:, :, 0], x, y)
                mul(x, a[:, :, 0], bi)
                mul(y, a[:, :, 1], br)
                add(o[:, :, 1], x, y)
            complex_mul(pw[:, 2:3], pw[:, 1:2], pw[:, 1], 1)
            complex_mul(pw[:, 3:5], pw[:, 1:3], pw[:, 2], 2)
            complex_mul(pw[:, 5:9], pw[:, 1:5], pw[:, 4], 4)
            for ri in range(2):
                link(dve.tensor_copy(lam8[:, 0, ri], pw[:, T, 0]))
            link(dve.tensor_copy(lam8[:, 1, 0], pw[:, T, 1]))
            link(dve.tensor_scalar(lam8[:, 1, 1], pw[:, T, 1], -1.0, None, ALU.mult))
            F_, B_ = slice(0, 64), slice(64, 128)
            for ri in range(2):
                link(dve.tensor_copy(PP[F_, ri], pw[F_, T - 1::-1, ri]))
                link(dve.tensor_copy(PP[B_, ri], pw[B_, 0:T, ri]))
            power = lambda a: a.rearrange("p t g -> p g t").unsqueeze(3).broadcast_to([P, GROUPS, T, SG])
            chan = lambda a: a.unsqueeze(2).broadcast_to([P, GROUPS, T, SG])

            def outer_product(o, p0, v0, p1, v1, op):
                for half in range(2):
                    g = slice(half * GROUPS // 2, (half + 1) * GROUPS // 2)
                    other = tmp.rearrange("p (g t i) -> p g t i", t=T, i=SG)
                    mul(o[:, g], power(p0)[:, g], chan(v0)[:, g])
                    mul(other, power(p1)[:, g], chan(v1)[:, g])
                    link(dve.tensor_tensor(o[:, g], o[:, g], other, op))
            outer_product(X[0], PP[:, 0], Bb[:, 0], PP[:, 1], Bb[:, 1], ALU.subtract)
            dve.sem_inc(s_cf, 1)
            outer_product(X[1], PP[:, 0], Bb[:, 1], PP[:, 1], Bb[:, 0], ALU.add)
            dve.sem_inc(s_cf, 1)
            for ri in range(2):
                link(dve.tensor_copy(PP[F_, ri], pw[F_, 1:T + 1, ri]))
                link(dve.tensor_copy(PP[B_, ri], pw[B_, T:0:-1, ri]))
            dve.wait_ge(s_negc, 2)
            outer_product(C_mat[0], PP[:, 0], C0[:, 0], PP[:, 1], C0[:, 1], ALU.add)
            outer_product(C_mat[1], PP[:, 0], C0[:, 1], PP[:, 1], C0[:, 0], ALU.subtract)

def ssm_phase(nc, w, rows, rows_at, ident, psum, nT_hi, nT_lo, u, gates, C_mat):
    with ExitStack() as ctx:
        sb = lambda n, s: ctx.enter_context(nc.sbuf_tensor(f"ss_{n}", s, F32))
        lam8 = sb("lam8", [P, 2, 2, GROUPS])
        common = sb("common", [P, GROUPS * CH])
        E_mat = chunk_states(rows)
        part = lambda i: common[:, i * 2 * WIDTH:(i + 1) * 2 * WIDTH].rearrange("p (c g i) -> p c g i", c=2, i=SG)
        Bb, C0 = part(0), part(1)
        rest = common[:, 4 * WIDTH:]
        ssm_setup_phase(nc, w, ident, psum, nT_hi, nT_lo, gates, E_mat, C_mat, lam8, Bb, C0, rest)
        UT = common[:].rearrange("p (g c) -> p g c", g=GROUPS)
        with ExitStack() as inner:
            M = inner.enter_context(nc.sbuf_tensor("ss_M", [P, GROUPS, P], F32))
            with Phase(nc) as step:
                chunk_matrices(nc, step, ident, psum, u, M, UT, C_mat, Bb, C0, rest)
            with Phase(nc) as step:
                within_chunks(nc, step, w, psum, u, M, UT)
        H = sb("H", [P, CH + 1, 2, GROUPS])
        with Phase(nc) as step:
            scan_chunks(nc, step, w, rows, rows_at, psum, nT_hi, nT_lo, gates, E_mat, UT, lam8, H)
        with Phase(nc) as step:
            chunk_outputs(nc, step, psum, u, UT, H, chunk_states(rows), C_mat)


def chunk_states(rows):
    return [rows[:, c * ST // 2:(c + 1) * ST // 2, :].rearrange("p a (b s) -> p (a b) s", s=P) for c in range(2)]


def chunk_matrices(nc, ctx, ident, psum, u, M, UT, C_mat, Bb, C0, rest):
    sb, sem = tools(nc, ctx, "sc")
    kern = sb("kern", [SG, GROUPS, SLOTS * SG])
    Bz = rest.rearrange("p (d c g i) -> p d c g i", d=2, c=2, i=SG)
    s_mm, s_cp, s_z, s_bz, s_ut = map(sem, ("kern_mm", "kern_cp", "z", "bz", "ut"))
    s_m = [sem(f"m_in{b}") for b in range(4)]
    with nc.Block() as block:
        @block.tensor
        def _(pe):
            cm = lambda c, g, t0, t1: C_mat[c][:, g, t0:t1, :].rearrange("p t i -> p (t i)")
            pe.wait_ge(s_bz, 2)
            pe.wait_ge(s_z, 2)
            for g in range(GROUPS):
                q = g // 2
                if g % 2 == 0 and q >= 8:
                    pe.wait_ge(s_cp, q - 7)
                out = psum[0:SG, q % 8, g % 2 * 256:g % 2 * 256 + SLOTS * SG]
                for a, b, lhs, rhs in ((0, T - 1, lambda c: Bz[:, 1, c, g, :], lambda c: cm(c, g, 1, T)),
                                       (T - 1, T, lambda c: Bb[:, c, g, :], lambda c: C0[:, c, g, :]),
                                       (T, SLOTS, lambda c: Bz[:, 0, c, g, :], lambda c: cm(c, g, 0, T - 1))):
                    for c in range(2):
                        mm = pe.matmul(out[:, a * SG:b * SG], lhs(c), rhs(c), start=c == 0, stop=c == 1)
                if g % 2:
                    mm.then_inc(s_mm, 1)
            for q in range(GROUPS // 4):
                pe.wait_ge(s_cp, q + 9)
                for g in range(4):
                    mm = pe.transpose(psum[:, q, g * P:(g + 1) * P], u[:, 4 * q + g, :, :].rearrange("p t i -> p (t i)"), ident[:])
                mm.then_inc(s_ut, 1)

        @block.scalar
        def _(act):
            for d, h in enumerate((slice(0, 64), slice(64, 128))):
                act.copy(Bz[h, d], Bb[h]).then_inc(s_bz, 1)
            for q in range(GROUPS // 2):
                act.wait_ge(s_mm, q + 1)
                act.copy(kern[:, 2 * q:2 * q + 2, :], psum[0:SG, q % 8, :].rearrange("p (g x) -> p g x", g=2)[:, :, 0:SLOTS * SG]).then_inc(s_cp, 1)

        @block.vector
        def _(dve):
            for d, h in enumerate((slice(64, 128), slice(0, 64))):
                dve.memset(Bz[h, d], 0.0).then_inc(s_z, 1)
            for q in range(GROUPS // 4):
                dve.wait_ge(s_ut, q + 1)
                dve.tensor_copy(UT[:, 4 * q:4 * q + 4, :], psum[:, q, :].rearrange("p (g c) -> p g c", g=4))

        @block.sync
        def _(sp):
            for b in range(4):
                sp.wait_ge(s_cp, 4 * (b + 1))
                for t in range(T):
                    at = (T - 1 - t) * SG
                    sp.dma_start(M[t * SG:(t + 1) * SG, 8 * b:8 * b + 8, :], kern[:, 8 * b:8 * b + 8, at:at + P]).then_inc(s_m[b], 16)
            for b in range(4):
                sp.wait_ge(s_m[b], 16 * T)


def within_chunks(nc, ctx, w, psum, u, M, UT):
    sb, sem = tools(nc, ctx, "sw")
    Db = sb("Db", [P, GROUPS, SG])
    s_d, s_du, s_du2, s_y = map(sem, ("d_in", "du", "du2", "y"))
    NQ = GROUPS // 4
    with nc.Block() as block:
        @block.sync
        def _(sp):
            sp.dma_start(Db[:].rearrange("p g i -> p (g i)"), w["ssm_d"][0:1, :].broadcast_to([P, WIDTH])).then_inc(s_d, 16)

        @block.tensor
        def _(pe):
            for q in range(NQ):
                for g in range(4 * q, 4 * q + 4):
                    mm = pe.matmul(psum[:, q, g % 4 * P:(g % 4 + 1) * P], UT[:, g, :], M[:, g, :], start=True, stop=True)
                mm.then_inc(s_y, 1)

        def times_d(eng, q, s):
            g = slice(4 * q, 4 * q + 4)
            eng.tensor_tensor(u[:, g], u[:, g], Db[:, g].unsqueeze(2).broadcast_to([P, 4, T, SG]), ALU.mult).then_inc(s, 1)

        @block.gpsimd
        def _(pool):
            pool.wait_ge(s_d, 16)
            for q in range(NQ // 2, NQ):
                times_d(pool, q, s_du2)

        @block.vector
        def _(dve):
            dve.wait_ge(s_d, 16)
            for q in range(NQ // 2):
                times_d(dve, q, s_du)
            for q in range(NQ):
                g = slice(4 * q, 4 * q + 4)
                if q < NQ // 2:
                    dve.wait_ge(s_du, q + 1)
                else:
                    dve.wait_ge(s_du2, q + 1 - NQ // 2)
                dve.wait_ge(s_y, q + 1)
                dve.tensor_tensor(u[:, g], psum[:, q, :].rearrange("p (g t i) -> p g t i", g=4, i=SG), u[:, g], ALU.add)


def scan_chunks(nc, ctx, w, rows, rows_at, psum, nT_hi, nT_lo, gates, E_mat, UT, lam8, H):
    sb, sem = tools(nc, ctx, "sd")
    prod = sb("prod", [P, 2, 2, GROUPS])
    s_e, s_ec, s_mul, s_sum, s_scan = map(sem, ("e", "e_cp", "mul", "sum", "scan"))
    side = Gates(nc, ctx, "g2", w["w_in"][0], GATES_BESIDE_SETUP, 2 * D // P, nT_hi, nT_lo, psum, gates, rows[:, 4:6, :], rows_at)
    NQ = 2 * GROUPS // 4
    with nc.Block() as block:
        @block.sync
        def _(sp):
            side.gp.load(sp, 0)
            side.gp.load(sp, 1)
            side.sync(sp)

        @block.tensor
        def _(pe):
            for q in range(NQ):
                c, g0 = q // 8, q % 8 * 4
                if q >= 4:
                    pe.wait_ge(s_ec, 2 * (q - 3))
                for g in range(4):
                    mm = pe.matmul(psum[:, 4 + q % 4, g * P:(g + 1) * P], E_mat[c][:, g0 + g, :], UT[:, g0 + g, :], start=True, stop=True)
                mm.then_inc(s_e, 1)
            for n in range(side.N):
                side.gp.product(pe, n)

        @block.scalar
        def _(act):
            for q in range(NQ):
                c, g0 = q // 8, q % 8 * 4
                act.wait_ge(s_e, q + 1)
                ps = psum[:, 4 + q % 4, :].rearrange("p (g c) -> p c g", g=4)
                act.copy(H[0:64, 1:CH + 1, c, g0:g0 + 4], ps[0:64]).then_inc(s_ec, 1)
                act.copy(H[64:128, CH:0:-1, c, g0:g0 + 4], ps[64:128]).then_inc(s_ec, 1)
            side.gp.high(act, 0)
            side.gp.high(act, 1)
            for n in range(side.N):
                side.sigmoid(act, n)

        @block.gpsimd
        def _(pool):
            for n in range(side.N):
                side.gp.low(pool, n)

        @block.vector
        def _(dve):
            dve.memset(H[:, 0], 0.0).then_inc(s_scan, 1)
            dve.wait_ge(s_ec, 2 * NQ)
            for n in range(CH - 1):
                now = H[:, n:n + 1].rearrange("p a r g -> p a (r g)").broadcast_to([P, 2, 2 * GROUPS])
                dve.wait_ge(s_scan, n + 1)
                dve.tensor_tensor(prod[:].rearrange("p c r g -> p c (r g)"), now, lam8[:].rearrange("p c r g -> p c (r g)"), ALU.mult).then_inc(s_mul, 1)
                dve.wait_ge(s_mul, n + 1)
                dve.tensor_tensor(H[:, n + 1], H[:, n + 1], prod[:, 0], ALU.add).then_inc(s_sum, 1)
                dve.wait_ge(s_sum, n + 1)
                dve.tensor_tensor(H[:, n + 1], H[:, n + 1], prod[:, 1, ::-1], ALU.add).then_inc(s_scan, 1)


def chunk_outputs(nc, ctx, psum, u, y, H, Hn, C_mat):
    sb, sem = tools(nc, ctx, "se")
    s_fw, s_bw, s_y, s_sum = map(sem, ("forward", "backward", "y", "y_sum"))
    with nc.Block() as block:
        @block.tensor
        def _(pe):
            for q in range(GROUPS // 4):
                pe.wait_ge(s_fw, q // 2 * 2 + 2)
                pe.wait_ge(s_bw, q // 2 * 2 + 2)
                for g in range(4 * q, 4 * q + 4):
                    for c in range(2):
                        mm = pe.matmul(psum[:, q, g % 4 * P:(g % 4 + 1) * P], Hn[c][:, g, :], C_mat[c][:, g].rearrange("p t i -> p (t i)"), start=c == 0, stop=c == 1)
                mm.then_inc(s_y, 1)

        @block.vector
        def _(dve):
            def block_sum(b):
                block_y = y[:, 8 * b:8 * b + 8, :].rearrange("p a b -> p (a b)").rearrange("p (t g i) -> p g t i", t=T, i=SG)
                for q in (2 * b, 2 * b + 1):
                    dve.wait_ge(s_y, q + 1)
                    dve.tensor_tensor(block_y[:, q % 2 * 4:q % 2 * 4 + 4], psum[:, q, :].rearrange("p (g t i) -> p g t i", g=4, i=SG),
                                      u[:, 4 * q:4 * q + 4], ALU.add).then_inc(s_sum, 1)
            for b in range(GROUPS // 8):
                for c in range(2):
                    dve.tensor_copy(Hn[c][64:128, 8 * b:8 * b + 8, :].rearrange("p g c -> p c g"), H[64:128, CH - 1::-1, c, 8 * b:8 * b + 8]).then_inc(s_bw, 1)
                if b:
                    block_sum(b - 1)
            block_sum(GROUPS // 8 - 1)

        @block.scalar
        def _(act):
            for b in range(GROUPS // 8):
                for c in range(2):
                    act.copy(Hn[c][0:64, 8 * b:8 * b + 8, :].rearrange("p g c -> p c g"), H[0:64, 0:CH, c, 8 * b:8 * b + 8]).then_inc(s_fw, 1)
            for b in range(GROUPS // 8):
                act.wait_ge(s_sum, 2 * b + 2)
                act.activation(u[:, 8 * b:8 * b + 8].rearrange("p g t i -> p (g t i)"), y[:, 8 * b:8 * b + 8, :].rearrange("p a b -> p (a b)"), ACT.Gelu_apprx_tanh)


def glu_phase(nc, w, rows, ident, psum, y, gates, partial, kept):
    with Phase(nc) as ctx:
        sb, sem = tools(nc, ctx, "gl")
        NB = WIDTH // P
        yT_hi, yT_lo = sb("yT_hi", [P, NB, SEQ], F32R), sb("yT_lo", [P, NB, SEQ], F32R)
        sT_hi, sT_lo = sb("sT_hi", [P, NB, SEQ], F32R), sb("sT_lo", [P, NB, SEQ], F32R)
        bias = sb("bias", [P, 2 * NB])
        sig, val = sb("sig", [P, SEQ]), sb("val", [P, 2, SEQ])
        gate, out = sb("gate", [P, 2, SEQ]), sb("out", [P, 2, SEQ])
        order = [c for b in range(NB) for c in (WIDTH + b * P, b * P)]
        glu = ColumnProduct(nc, ctx, "glu", w["w_glu"][0], order, yT_hi, yT_lo, psum, S=3)
        wos = ColumnProduct(nc, ctx, "wos", w["w_o_ssm"][0], [n * P for n in range(KT)], sT_hi, sT_lo, psum, 4, S=3)
        s_b, s_t, s_hi, s_lo, s_sig, s_vhi, s_vlo = map(sem, ("b", "t", "yhi", "ylo", "sig", "vhi", "vlo"))
        s_g, s_o, s_kept = [sem("g0"), sem("g1")], [sem("o0"), sem("o1")], sem("kept")
        block = ctx.enter_context(nc.Block())
        two = lambda ap: ap.rearrange("p (a b) -> p a b", a=2)
        NT = 2 * NB
        yb = y[:].rearrange("p g t i -> p (g t i)").rearrange("p (b t c) -> p b t c", b=NB, t=T)
        dest = lambda a, b, tq: a[:, b, :].rearrange("p (c t) -> p t c", t=T)[:, 4 * tq:4 * tq + 4, :]
        bank = lambda n: psum[:, 4 + n % 4, :].rearrange("p (t c) -> p t c", t=4)

        @block.sync
        def _(sp):
            sp.dma_start(bias[:], w["b_glu"][0].rearrange("(n p) -> p n", p=P), allow_slow_non_contiguous=True).then_inc(s_b, 16)
            for n in range(glu.N):
                glu.load(sp, n)
                if n == 3:
                    sp.dma_start(rows[:], kept.rearrange("(m p) d -> p m d", p=P)).then_inc(s_kept, 16)
            for n in range(3):
                wos.load(sp, n)
            for n in range(2):
                sp.dma_start(gate[:, n, :], gates[D + n * P:D + (n + 1) * P, :]).then_inc(s_g[n], 16)
            for n in range(KT):
                wos.load(sp, n + 3)
                sp.wait_ge(wos.read[n % 2], n // 2 + 1)
                if n + 2 < KT:
                    sp.dma_start(gate[:, n % 2, :], gates[D + (n + 2) * P:D + (n + 3) * P, :]).then_inc(s_g[n % 2], 16)
                sp.dma_start(partial[n * P:(n + 1) * P, :], out[:, n % 2, :]).then_inc(s_o[n % 2], 16)
            for i in range(2):
                sp.wait_ge(s_o[i], 16 * KT // 2)
            sp.wait_ge(s_kept, 16)

        @block.tensor
        def _(pe):
            for n in range(NT):
                b, tq = n // 2, n % 2
                if n >= 4:
                    pe.wait_ge(s_lo, n - 3)
                for t in range(4):
                    mm = pe.transpose(psum[:, 4 + n % 4, t * P:(t + 1) * P], yb[:, b, 4 * tq + t, :], ident[:])
                mm.then_inc(s_t, 1)
            pe.wait_ge(s_lo, NT)
            for n in range(glu.N):
                glu.product(pe, n)
            for n in range(KT):
                wos.product(pe, n, (lambda k: pe.wait_ge(s_vlo, k + 1)) if n == 0 else None)

        @block.scalar
        def _(act):
            for n in range(NT):
                act.wait_ge(s_t, n + 1)
                act.copy(dest(yT_hi, n // 2, n % 2), bank(n)).then_inc(s_hi, 1)
                if n >= 3 and n < 6:
                    glu.high(act, n - 3)
            act.wait_ge(s_b, 16)
            for b in range(NB):
                if b == NB - 1:
                    for n in range(3):
                        wos.high(act, n)
                act.wait_ge(glu.mm_done, 2 * b + 1)
                if b:
                    act.wait_ge(glu.read[1], b)
                act.activation(two(sig[:]), glu.ps[0], ACT.Sigmoid, bias=bias[:, NB + b:NB + b + 1]).then_inc(glu.read[0], 1)
                glu.high(act, 2 * b + 3)
                act.wait_ge(glu.read[1], b + 1)
                act.copy(sT_hi[:, b, :], val[:, b % 2, :]).then_inc(s_vhi, 1)
                glu.high(act, 2 * b + 4)
            for n in range(KT):
                wos.high(act, n + 3)

        @block.vector
        def _(dve):
            for n in range(NT):
                dve.wait_ge(s_hi, n + 1)
                dve.tensor_tensor(dest(yT_lo, n // 2, n % 2), bank(n), dest(yT_hi, n // 2, n % 2).bitcast(F32), ALU.subtract).then_inc(s_lo, 1)
                if n >= 3 and n < 6:
                    glu.low(dve, n - 3)
            dve.wait_ge(s_b, 16)
            for b in range(NB):
                if b == NB - 1:
                    for n in range(3):
                        wos.low(dve, n)
                dve.wait_ge(glu.mm_done, 2 * b + 2)
                dve.wait_ge(glu.read[0], b + 1)
                if b >= 2:
                    dve.wait_ge(s_vlo, b - 1)
                dve.scalar_tensor_tensor(out=two(val[:, b % 2, :]), in0=glu.ps[1], scalar=bias[:, b:b + 1], in1=two(sig[:]),
                                         op0=ALU.add, op1=ALU.mult).then_inc(glu.read[1], 1)
                glu.low(dve, 2 * b + 3)
                dve.wait_ge(s_vhi, b + 1)
                dve.tensor_tensor(sT_lo[:, b, :], val[:, b % 2, :], sT_hi[:, b, :].bitcast(F32), ALU.subtract).then_inc(s_vlo, 1)
                glu.low(dve, 2 * b + 4)
            for n in range(KT):
                dve.wait_ge(wos.mm_done, n + 1)
                dve.wait_ge(s_g[n % 2], 16 * (n // 2 + 1))
                if n >= 2:
                    dve.wait_ge(s_o[n % 2], 16 * (n // 2))
                dve.tensor_tensor(two(out[:, n % 2, :]), wos.ps[n % 2], two(gate[:, n % 2, :]), ALU.mult).then_inc(wos.read[n % 2], 1)
                wos.low(dve, n + 3)


def attention_phase(nc, w, ident, psum, latent_rows, trig_rows, aT_hi, aT_lo):
    with Phase(nc) as ctx:
        sb, sem = tools(nc, ctx, "at")
        NL = 3
        lT_hi, lT_lo = sb("lT_hi", [P, NL, SEQ], F32R), sb("lT_lo", [P, NL, SEQ], F32R)
        krT = sb("krT", [P, SEQ])
        trig = sb("trig", [P, SEQ])
        with Phase(nc) as inner:
            latents(nc, inner, ident, psum, latent_rows, trig_rows, lT_hi, lT_lo, krT, trig)
        head_loop(nc, ctx, w, ident, psum, lT_hi, lT_lo, krT, trig, aT_hi, aT_lo)


def latents(nc, ctx, ident, psum, latent_rows, trig_rows, lT_hi, lT_lo, krT, trig):
    sb, sem = tools(nc, ctx, "la")
    other = sb("other", [P, SEQ])
    zrow = sb("zrow", [P, ST, ZW])
    s_rows = [sem(f"rows{i}") for i in range(4)]
    s_trig, s_tr, s_hi, s_rot = sem("trig"), sem("tr"), sem("hi"), sem("rot")
    Rp = slice(64, 128)
    bank = lambda m: psum[:, m, 0:3 * P].rearrange("p (k s) -> p k s", k=3)
    with nc.Block() as block:
        @block.sync
        def _(sp):
            sp.dma_start(trig[Rp, :], trig_rows).then_inc(s_trig, 16)
            for i in range(4):
                sp.dma_start(zrow[:, 2 * i:2 * i + 2, :], latent_rows[2 * i * P:(2 * i + 2) * P, :].rearrange("(m p) z -> p m z", p=P)).then_inc(s_rows[i], 16)

        @block.scalar
        def _(act):
            for m in range(ST):
                act.wait_ge(s_tr, m + 1)
                act.copy(krT[Rp, m * P:(m + 1) * P], psum[Rp, m, 3 * P:4 * P])
                act.copy(lT_hi[:, :, m * P:(m + 1) * P], bank(m)).then_inc(s_hi, 1)

        @block.vector
        def _(dve):
            for m in range(ST):
                sl = slice(m * P, (m + 1) * P)
                dve.wait_ge(s_hi, m + 1)
                dve.tensor_tensor(lT_lo[:, :, sl], bank(m), lT_hi[:, :, sl].bitcast(F32), ALU.subtract)
                if m % 4 == 3:
                    if m == 3:
                        dve.wait_ge(s_trig, 16)
                    C, S, half, n = slice(64, 96), slice(96, 128), slice((m - 3) * P, (m + 1) * P), m // 4 * 2
                    dve.tensor_tensor(other[C, half], krT[S, half], trig[S, half], ALU.mult).then_inc(s_rot, 1)
                    dve.tensor_tensor(krT[C, half], krT[C, half], trig[C, half], ALU.mult).then_inc(s_rot, 1)
                    dve.wait_ge(s_rot, n + 2)
                    dve.tensor_tensor(krT[C, half], krT[C, half], other[C, half], ALU.add)

        @block.tensor
        def _(pe):
            for m in range(ST):
                pe.wait_ge(s_rows[m // 2], 16)
                for k in range(3):
                    pe.transpose(psum[:, m, k * P:(k + 1) * P], zrow[:, m, k * P:(k + 1) * P], ident[:])
                pe.transpose(psum[:, m, 3 * P:4 * P], zrow[:, m, ZW - P:ZW], ident[:]).then_inc(s_tr, 1)


def head_loop(nc, ctx, w, ident, psum, lT_hi, lT_lo, krT, trig, aT_hi, aT_lo):
    sb, sem = tools(nc, ctx, "hd")
    KD = NOPE + ROPE
    raw = sb("raw", [P, 3, P])
    w_hi, w_lo = sb("w_hi", [P, 3, P], F32R), sb("w_lo", [P, 3, P], F32R)
    QT_hi, QT_lo = sb("QT_hi", [P, 2, SEQ], F32R), sb("QT_lo", [P, 2, SEQ], F32R)
    KT_hi, KT_lo = sb("KT_hi", [P, 2, SEQ], F32R), sb("KT_lo", [P, 2, SEQ], F32R)
    V_hi, V_lo = sb("V_hi", [P, 2, ST, VH], F32R), sb("V_lo", [P, 2, ST, VH], F32R)
    qf = sb("qf", [P, 2, HALF])
    prob = sb("prob", [P, 2, SEQ])
    rot = lambda n, x: prob[C, 1, hs(x)] if isinstance(n, int) and n == 0 else krT[C, hs(x)]
    PT_hi, PT_lo = sb("PT_hi", [P, 2, ST, 2 * P], F32R), sb("PT_lo", [P, 2, ST, 2 * P], F32R)
    mx, nmx, tot, inv = (sb(n, [P, 2]) for n in ("mx", "nmx", "tot", "inv"))
    diag = sb("diag", [P, 4, P])
    ones = sb("ones", [P, VH])
    spread = sb("spread", [VH, 2 * P])
    att = sb("att", [P, 2, 2 * P])
    names = "raw_in w_hi w_lo proj proj_act proj_dve rot q_sum q_hi q_lo kr_hi kr_lo scores mx nmx exp inv diag ones tr tr_hi tr_lo pv spread av av_hi av_lo".split()
    s = {n: sem(n) for n in names}
    w_uq, w_ukv = w["w_uq"][0].rearrange("(k p) f -> p k f", p=P), w["w_ukv"][0]
    half_r = ROPE // 2
    C, S = slice(64, 96), slice(96, 128)
    hs = lambda x: slice(x * HALF, (x + 1) * HALF)
    bank = psum[:, 7, :]
    two = lambda ap: ap.rearrange("p (a b) -> p a b", a=2)
    tbank = lambda b: psum[:, 4 + b, :].rearrange("p (k q) -> p k q", k=4)
    pt = lambda a, qt, b: a[:, qt // 2 % 2, 4 * b:4 * b + 4, qt % 2 * P:(qt % 2 + 1) * P]
    pv_out, inv_out = psum[0:VH, 6, 0:2 * P], psum[0:VH, 6, 2 * P:4 * P]
    block = ctx.enter_context(nc.Block())

    def heads(step_of_head):
        def run(eng):
            for h in (0, 1):
                step_of_head(h, h // 2, h % 2)
            with eng.Fori(1, HEADS // 2 - 1) as q:
                for par in (0, 1):
                    step_of_head(q * 2 + par, q, par)
            for h in (HEADS - 2, HEADS - 1):
                step_of_head(h, h // 2, h % 2)
        return run

    def is_first(h):
        return isinstance(h, int) and h == 0

    def is_last(h):
        return isinstance(h, int) and h == HEADS - 1

    @block.sync
    def _(sp):
        def load(n):
            if not isinstance(n, int) or n > 0:
                sp.wait_ge(s["w_lo"], n)
            nq = n * KD
            sp.dma_start(raw[:, 0:2, 0:KD], w_uq[:, :, bass.ds(nq, KD)]).then_inc(s["raw_in"], 16)
            sp.dma_start(raw[:, 0:2, KD:KD + half_r], w_uq[:, :, bass.ds(nq + NOPE + half_r, half_r)]).then_inc(s["raw_in"], 16)
            sp.dma_start(raw[:, 0:2, KD + half_r:P], w_uq[:, :, bass.ds(nq + NOPE, half_r)]).then_inc(s["raw_in"], 16)
            sp.dma_start(raw[:, 2, :], w_ukv[:, bass.ds(n * P, P)]).then_inc(s["raw_in"], 16)
        load(0)
        with sp.Fori(1, HEADS) as n:
            load(n)

    def proj_mm(pe, n, x, par):
        job = n * 5 + x
        if not (isinstance(n, int) and n == 0 and x == 0):
            pe.wait_ge(s["proj_act"], job)
            pe.wait_ge(s["proj_dve"], job)
        if x == 0:
            pe.wait_ge(s["w_lo"], n + 1)
        if x < 2:
            for k in range(2):
                mm = three_passes(pe, bank, w_hi[:, k, :], w_lo[:, k, :], lT_hi[:, k, hs(x)], lT_lo[:, k, hs(x)], k == 0, k == 1)
        elif x < 4:
            mm = three_passes(pe, bank[0:NOPE], w_hi[:, 2, 0:NOPE], w_lo[:, 2, 0:NOPE], lT_hi[:, 2, hs(x - 2)], lT_lo[:, 2, hs(x - 2)], True, True)
        else:
            for m in range(ST):
                sl = slice(m * P, (m + 1) * P)
                mm = three_passes(pe, bank[:, m * VH:(m + 1) * VH], lT_hi[:, 2, sl], lT_lo[:, 2, sl],
                                  w_hi[:, 2, NOPE:], w_lo[:, 2, NOPE:], True, True)
        mm.then_inc(s["proj"], 1)

    def scores(pe, h, qt, par):
        g = h * 8 + qt
        if qt == 0:
            pe.wait_ge(s["q_lo"], h * 2 + 2)
            pe.wait_ge(s["proj_dve"], h * 5 + 5)
        if not (isinstance(h, int) and g < 2):
            pe.wait_ge(s["exp"], g - 1)
        for half in range(2):
            mm = three_passes(pe, psum[:, 2 * (qt % 2) + half, :], QT_hi[0:KD, par, qt * P:(qt + 1) * P], QT_lo[0:KD, par, qt * P:(qt + 1) * P],
                              KT_hi[0:KD, par, hs(half)], KT_lo[0:KD, par, hs(half)], True, True)
        mm.then_inc(s["scores"], 1)

    def turn(pe, g, qt):
        pe.wait_ge(s["exp"], g + 1)
        for b in range(2):
            if not (isinstance(g, int) and g == 0):
                pe.wait_ge(s["tr_lo"], g * 2 - 1 + b)
            for k in range(4):
                t = pe.transpose(psum[:, 4 + b, k * P:(k + 1) * P], prob[:, qt % 2, (4 * b + k) * P:(4 * b + k + 1) * P], ident[:])
            t.then_inc(s["tr"], 1)

    def values(pe, jj, j, par):
        if not (isinstance(jj, int) and jj == 0):
            pe.wait_ge(s["av"], jj)
        pe.wait_ge(s["diag"], jj * 2 + 2)
        for i in range(2):
            pe.matmul(inv_out[:, i * P:(i + 1) * P], ones[:], diag[:, j % 2 * 2 + i, :], start=True, stop=True)
        pe.wait_ge(s["tr_lo"], jj * 4 + 4)
        for k in range(ST):
            mm = three_passes(pe, pv_out, V_hi[:, par, k, :], V_lo[:, par, k, :], PT_hi[:, j % 2, k, :], PT_lo[:, j % 2, k, :], k == 0, k == ST - 1)
        mm.then_inc(s["pv"], 1)

    @block.tensor
    def _(pe):
        for x in range(5):
            proj_mm(pe, 0, x, 0)
        pe.wait_ge(s["kr_lo"], 1)
        pe.wait_ge(s["ones"], 1)

        def head(h, q, par):
            for qt in range(ST):
                scores(pe, h, qt, par)
                if qt >= 2 or not is_first(h):
                    turn(pe, h * 8 + qt - 2, (qt - 2) % ST)
                if qt % 2 == 0 and (qt >= 4 or not is_first(h)):
                    values(pe, h * 4 + qt // 2 - 2, (qt // 2 - 2) % 4, par if qt >= 4 else 1 - par)
                if not is_last(h) and 1 <= qt <= 5:
                    proj_mm(pe, h + 1, qt - 1, 1 - par)
        heads(head)(pe)
        N = HEADS * ST
        turn(pe, N - 2, ST - 2)
        values(pe, N // 2 - 2, 2, 1)
        turn(pe, N - 1, ST - 1)
        values(pe, N // 2 - 1, 3, 1)

    @block.scalar
    def _(act):
        def split(n):
            act.wait_ge(s["raw_in"], n * 64 + 64)
            if not isinstance(n, int) or n > 0:
                act.wait_ge(s["proj"], n * 5)
            act.copy(w_hi[:], raw[:]).then_inc(s["w_hi"], 1)

        def project(n, x, par):
            act.wait_ge(s["proj"], n * 5 + x + 1)
            if x < 2:
                if not (isinstance(n, int) and n == 0):
                    act.wait_ge(s["q_lo"], n * 2 + x - 1)
                act.copy(qf[0:NOPE, x, :], bank[0:NOPE]).then_inc(s["proj_act"], 1)
            elif x < 4:
                if not (isinstance(n, int) and n < 2):
                    act.wait_ge(s["scores"], n * 8 - 8)
                act.copy(KT_hi[0:NOPE, par, hs(x - 2)], bank[0:NOPE]).then_inc(s["proj_act"], 1)
            else:
                if not (isinstance(n, int) and n < 2):
                    act.wait_ge(s["pv"], n * 4 - 4)
                act.copy(V_hi[:, par], bank.rearrange("p (m v) -> p m v", m=ST)).then_inc(s["proj_act"], 1)

        def queries(n, x, par):
            act.wait_ge(s["q_sum"], n * 2 + x + 1)
            act.wait_ge(s["proj_act"], n * 5 + x + 1)
            if not (isinstance(n, int) and n < 2):
                act.wait_ge(s["scores"], n * 8 - 8)
            act.copy(QT_hi[0:KD, par, hs(x)], qf[0:KD, x, :]).then_inc(s["q_hi"], 1)

        def turned(g, qt, jj):
            if qt % 2 == 0 and not (isinstance(jj, int) and jj < 2):
                act.wait_ge(s["pv"], jj - 1)
            for b in range(2):
                act.wait_ge(s["tr"], g * 2 + b + 1)
                act.copy(pt(PT_hi, qt, b), tbank(b)).then_inc(s["tr_hi"], 1)

        def exponential(g, qt):
            act.wait_ge(s["nmx"], g + 1)
            if not (isinstance(g, int) and g < 2):
                act.wait_ge(s["tr"], g * 2 - 2)
                act.wait_ge(s["inv"], g - 1)
            sl = qt % 2
            act.activation(two(prob[:, sl, :]), psum[:, 2 * sl:2 * sl + 2, :], ACT.Exp, bias=nmx[:, sl:sl + 1], scale=SCALE,
                           accum_out=tot[:, sl:sl + 1]).then_inc(s["exp"], 1)

        def spread_out(jj):
            act.wait_ge(s["pv"], jj + 1)
            if not (isinstance(jj, int) and jj == 0):
                act.wait_ge(s["av"], jj)
            act.copy(spread[:], inv_out).then_inc(s["spread"], 1)

        def attended(jj, j, hpar, hq):
            rows = slice(hpar * VH, (hpar + 1) * VH)
            act.wait_ge(s["av"], jj + 1)
            act.copy(aT_hi[rows, bass.ds(hq, 1), j * 256:(j + 1) * 256].rearrange("p a q -> p (a q)"), att[rows, j % 2, :]).then_inc(s["av_hi"], 1)

        split(0)
        for x in range(5):
            project(0, x, 0)
            if x < 2:
                queries(0, x, 0)
        for par in range(2):
            act.copy(KT_hi[C, par, :], krT[C, :]).then_inc(s["kr_hi"], 1)
        split(1)

        def head(h, q, par):
            for qt in range(ST):
                same = qt >= 5
                j = (qt // 2 - 2) % 4
                if qt % 2 == 1 and (same or not is_first(h)):
                    spread_out(h * 4 + qt // 2 - 2)
                if not is_last(h) and 2 <= qt <= 6:
                    project(h + 1, qt - 2, 1 - par)
                if not is_last(h) and 3 <= qt <= 4:
                    queries(h + 1, qt - 3, 1 - par)
                if qt >= 2 or not is_first(h):
                    turned(h * 8 + qt - 2, (qt - 2) % ST, h * 4 + (qt - 2) // 2)
                exponential(h * 8 + qt, qt)
                if qt % 2 == 1 and (same or not is_first(h)):
                    attended(h * 4 + qt // 2 - 2, j, par if same else 1 - par, q if same or par else q - 1)
                if qt == 7 and not (isinstance(h, int) and h >= HEADS - 2):
                    split(h + 2)
        heads(head)(act)
        N = HEADS * ST
        turned(N - 2, ST - 2, N // 2 - 1)
        spread_out(N // 2 - 2)
        attended(N // 2 - 2, 2, 1, HEADS // 2 - 1)
        turned(N - 1, ST - 1, N // 2 - 1)
        spread_out(N // 2 - 1)
        attended(N // 2 - 1, 3, 1, HEADS // 2 - 1)

    @block.vector
    def _(dve):
        def split(n):
            dve.wait_ge(s["w_hi"], n + 1)
            dve.tensor_tensor(w_lo[:], raw[:], w_hi[:].bitcast(F32), ALU.subtract).then_inc(s["w_lo"], 1)

        def project(n, x, par):
            dve.wait_ge(s["proj"], n * 5 + x + 1)
            if x < 2:
                if not (isinstance(n, int) and n == 0):
                    dve.wait_ge(s["q_lo"], n * 2 + x - 1)
                dve.wait_ge(s["proj_act"], n * 5 + x + 1)
                dve.tensor_tensor(rot(n, x), bank[S], trig[S, hs(x)], ALU.mult).then_inc(s["rot"], 1)
                dve.tensor_tensor(qf[C, x, :], bank[C], trig[C, hs(x)], ALU.mult).then_inc(s["proj_dve"], 1)
            else:
                dve.wait_ge(s["proj_act"], n * 5 + x + 1)
                if x < 4:
                    dve.tensor_tensor(KT_lo[0:NOPE, par, hs(x - 2)], bank[0:NOPE], KT_hi[0:NOPE, par, hs(x - 2)].bitcast(F32), ALU.subtract).then_inc(s["proj_dve"], 1)
                else:
                    dve.tensor_tensor(V_lo[:, par].rearrange("p m v -> p (m v)"), bank, V_hi[:, par].rearrange("p m v -> p (m v)").bitcast(F32), ALU.subtract).then_inc(s["proj_dve"], 1)

        def maximum(g, qt):
            sl = qt % 2
            dve.wait_ge(s["scores"], g + 1)
            if not (isinstance(g, int) and g < 2):
                dve.wait_ge(s["nmx"], g - 1)
            dve.tensor_reduce(mx[:, sl:sl + 1], psum[:, 2 * sl:2 * sl + 2, :], AX.XY, ALU.max).then_inc(s["mx"], 1)
            dve.wait_ge(s["mx"], g + 1)
            dve.tensor_scalar(nmx[:, sl:sl + 1], mx[:, sl:sl + 1], -SCALE, None, ALU.mult).then_inc(s["nmx"], 1)

        def turned(g, qt):
            for b in range(2):
                dve.wait_ge(s["tr_hi"], g * 2 + b + 1)
                dve.tensor_tensor(pt(PT_lo, qt, b), tbank(b), pt(PT_hi, qt, b).bitcast(F32), ALU.subtract).then_inc(s["tr_lo"], 1)

        def inverse(g, qt):
            sl = qt % 2
            dve.wait_ge(s["exp"], g + 1)
            if not (isinstance(g, int) and g < 2):
                dve.wait_ge(s["diag"], g - 1)
            dve.reciprocal(inv[:, sl:sl + 1], tot[:, sl:sl + 1]).then_inc(s["inv"], 1)

        def attended(jj, j, hpar, hq):
            rows = slice(hpar * VH, (hpar + 1) * VH)
            dve.wait_ge(s["spread"], jj + 1)
            if not (isinstance(jj, int) and jj < 2):
                dve.wait_ge(s["av_lo"], jj - 1)
            dve.tensor_tensor(att[rows, j % 2, :], pv_out, spread[:], ALU.mult).then_inc(s["av"], 1)

        split(0)
        project(0, 0, 0)
        project(0, 1, 0)
        dve.memset(ones[:], 1.0).then_inc(s["ones"], 1)
        for x in range(2, 5):
            project(0, x, 0)
        for par in range(2):
            dve.wait_ge(s["kr_hi"], par + 1)
            dve.tensor_tensor(KT_lo[C, par, :], krT[C, :], KT_hi[C, par, :].bitcast(F32), ALU.subtract).then_inc(s["kr_lo"], 1)
        dve.wait_ge(s["kr_lo"], 2)
        split(1)

        def head(h, q, par):
            for qt in range(ST):
                if qt % 2 == 1 and (qt >= 5 or not is_first(h)):
                    j = (qt // 2 - 2) % 4
                    same = qt >= 5
                    attended(h * 4 + qt // 2 - 2, j, par if same else 1 - par, q if same or par else q - 1)
                if not is_last(h) and 2 <= qt <= 6:
                    project(h + 1, qt - 2, 1 - par)
                maximum(h * 8 + qt, qt)
                if qt >= 1 or not is_first(h):
                    inverse(h * 8 + qt - 1, (qt - 1) % ST)
                if qt >= 2 or not is_first(h):
                    turned(h * 8 + qt - 2, (qt - 2) % ST)
                if qt == 7 and not (isinstance(h, int) and h >= HEADS - 2):
                    split(h + 2)
        heads(head)(dve)
        N = HEADS * ST
        inverse(N - 1, ST - 1)
        turned(N - 2, ST - 2)
        attended(N // 2 - 2, 2, 1, HEADS // 2 - 1)
        turned(N - 1, ST - 1)
        attended(N // 2 - 1, 3, 1, HEADS // 2 - 1)

    @block.gpsimd
    def _(pool):
        def queries(n, x, par):
            if not (isinstance(n, int) and n == 0 and x == 0):
                pool.wait_ge(s["q_lo"], n * 2 + x)
            if not (isinstance(n, int) and n == 0):
                pool.wait_ge(s["diag"], n * 8 + x - 6)
                if not (isinstance(n, int) and n == 1):
                    pool.wait_ge(s["av_lo"], n * 4 - 6)
            pool.wait_ge(s["rot"], n * 2 + x + 1)
            pool.wait_ge(s["proj_dve"], n * 5 + x + 1)
            pool.tensor_tensor(qf[C, x, :], qf[C, x, :], rot(n, x), ALU.add).then_inc(s["q_sum"], 1)
            pool.wait_ge(s["q_hi"], n * 2 + x + 1)
            pool.tensor_tensor(QT_lo[0:KD, par, hs(x)], qf[0:KD, x, :], QT_hi[0:KD, par, hs(x)].bitcast(F32), ALU.subtract).then_inc(s["q_lo"], 1)

        def diagonal(g, qt, jj):
            pool.wait_ge(s["inv"], g + 1)
            if not (isinstance(jj, int) and jj < 2):
                pool.wait_ge(s["pv"], jj - 1)
            pool.tensor_tensor(diag[:, qt % 4, :], ident[:], inv[:, qt % 2:qt % 2 + 1].broadcast_to([P, P]), ALU.mult).then_inc(s["diag"], 1)

        def attended(jj, j, hpar, hq, g):
            rows = slice(hpar * VH, (hpar + 1) * VH)
            dst = lambda a: a[rows, bass.ds(hq, 1), j * 256:(j + 1) * 256].rearrange("p a q -> p (a q)")
            pool.wait_ge(s["diag"], g + 1)
            pool.wait_ge(s["av_hi"], jj + 1)
            pool.tensor_tensor(dst(aT_lo), att[rows, j % 2, :], dst(aT_hi).bitcast(F32), ALU.subtract).then_inc(s["av_lo"], 1)

        for x in range(2):
            queries(0, x, 0)

        def head(h, q, par):
            for qt in range(ST):
                if not is_last(h) and 3 <= qt <= 4:
                    queries(h + 1, qt - 3, 1 - par)
                g = h * 8 + qt - 1
                if qt >= 1 or not is_first(h):
                    if qt % 2 == 0 and (qt >= 6 or not is_first(h)):
                        pool.wait_ge(s["av_lo"], h * 4 + qt // 2 - 2)
                    diagonal(g, (qt - 1) % ST, h * 4 + (qt - 1) // 2)
                same = qt >= 5
                if qt % 2 == 1 and (same or not is_first(h)):
                    attended(h * 4 + qt // 2 - 2, (qt // 2 - 2) % 4, par if same else 1 - par, q if same or par else q - 1, g)
        heads(head)(pool)
        N = HEADS * ST
        pool.wait_ge(s["av_lo"], N // 2 - 2)
        diagonal(N - 1, ST - 1, N // 2 - 1)
        attended(N // 2 - 2, 2, 1, HEADS // 2 - 1, N - 1)
        attended(N // 2 - 1, 3, 1, HEADS // 2 - 1, N - 1)


def merge_phase(nc, w, psum, rows, aT_hi, aT_lo, gates, partial):
    with Phase(nc) as ctx:
        sb, sem = tools(nc, ctx, "mg")
        mT_hi, mT_lo = sb("mT_hi", [P, KT, SEQ], F32R), sb("mT_lo", [P, KT, SEQ], F32R)
        gate, part, val = sb("gate", [P, 2, SEQ]), sb("part", [P, 2, SEQ]), sb("val", [P, 2, SEQ])
        woa = ColumnProduct(nc, ctx, "woa", w["w_o_attn"][0], [n * P for n in range(KT)], aT_hi, aT_lo, psum, S=3)
        lhs = lambda j, k, m: (mT_hi[:, k, m * P:(m + 1) * P], mT_lo[:, k, m * P:(m + 1) * P])
        w_out = w["w_out"][0]
        rp = RowProduct(nc, ctx, "wo", [(w_out, [(0, slice(j * HALF, (j + 1) * HALF))], HALF) for j in range(2)], lhs, psum)
        s_g, s_p = [sem("g0"), sem("g1")], [sem("p0"), sem("p1")]
        s_sum, s_hi, s_lo = sem("sum"), sem("hi"), sem("lo")
        NU = len(rp.units())
        two = lambda ap: ap.rearrange("p (a b) -> p a b", a=2)
        block = ctx.enter_context(nc.Block())

        def add(dve, j, m):
            rp.wait_bank(dve, j, m)
            sl = slice(j * HALF, (j + 1) * HALF)
            dve.tensor_tensor(rows[:, m, sl], psum[:, m, :], rows[:, m, sl], ALU.add).then_inc(rp.read, 1)

        @block.sync
        def _(sp):
            for n in range(3):
                woa.load(sp, n)
            for n in range(KT):
                if n >= 2:
                    sp.wait_ge(s_sum, n - 1)
                sp.dma_start(gate[:, n % 2, :], gates[n * P:(n + 1) * P, :]).then_inc(s_g[n % 2], 16)
                sp.dma_start(part[:, n % 2, :], partial[n * P:(n + 1) * P, :]).then_inc(s_p[n % 2], 16)
                woa.load(sp, n + 3)
                if n == 4:
                    rp.load(sp, 0)
                    rp.load(sp, 1)
            for n in range(2, NU):
                rp.load(sp, n)

        @block.scalar
        def _(act):
            woa.high(act, 0)
            woa.high(act, 1)
            woa.high(act, 2)
            for n in range(KT):
                woa.high(act, n + 3)
                act.wait_ge(s_sum, n + 1)
                act.copy(mT_hi[:, n, :], val[:, n % 2, :]).then_inc(s_hi, 1)
                if n == KT - 2:
                    rp.high(act, 0)
                    rp.high(act, 1)
            for n in range(2, NU):
                rp.high(act, n)

        @block.vector
        def _(dve):
            woa.low(dve, 0)
            woa.low(dve, 1)
            woa.low(dve, 2)
            for n in range(KT):
                dve.wait_ge(woa.mm_done, n + 1)
                dve.wait_ge(s_g[n % 2], 16 * (n // 2 + 1))
                if n >= 2:
                    dve.wait_ge(s_lo, n - 1)
                dve.tensor_tensor(two(val[:, n % 2, :]), woa.ps[n % 2], two(gate[:, n % 2, :]), ALU.mult).then_inc(woa.read[n % 2], 1)
                woa.low(dve, n + 3)
                dve.wait_ge(woa.read[n % 2], n // 2 + 1)
                dve.wait_ge(s_p[n % 2], 16 * (n // 2 + 1))
                dve.tensor_tensor(val[:, n % 2, :], val[:, n % 2, :], part[:, n % 2, :], ALU.add).then_inc(s_sum, 1)
                dve.wait_ge(s_hi, n + 1)
                dve.tensor_tensor(mT_lo[:, n, :], val[:, n % 2, :], mT_hi[:, n, :].bitcast(F32), ALU.subtract).then_inc(s_lo, 1)
                if n == KT - 2:
                    rp.low(dve, 0)
                    rp.low(dve, 1)
            for j in range(2):
                for k in range(KT):
                    if j or k >= 2:
                        rp.low(dve, j * KT + k)
                    if j and k == 1:
                        for m in range(ST):
                            add(dve, 0, m)
            for m in range(ST):
                add(dve, 1, m)

        @block.tensor
        def _(pe):
            for n in range(KT):
                woa.product(pe, n)
            for i in range(2):
                pe.wait_ge(woa.read[i], KT // 2)
            rp.products(pe, lambda k: pe.wait_ge(s_lo, k + 1))


def build(nc, w, out):
    gates = nc.dram_tensor("gates", [2 * D, SEQ], F32, kind="Internal").ap()
    partial = nc.dram_tensor("partial", [D, SEQ], F32, kind="Internal").ap()
    kept = nc.dram_tensor("kept", [SEQ, D], F32, kind="Internal").ap()
    latent_rows = nc.dram_tensor("latent_rows", [SEQ, ZW], F32, kind="Internal").ap()
    trig_rows = nc.dram_tensor("trig_rows", [2 * ROPE, SEQ], F32, kind="Internal").ap()
    with ExitStack() as ctx:
        rows_at = -(-nc.sbuf_base // 32) * 32
        rows = ctx.enter_context(nc.sbuf_tensor("rows", [P, ST, D], F32))
        ident = ctx.enter_context(nc.sbuf_tensor("ident", [P, P], F32))
        psum = ctx.enter_context(nc.psum_tensor("psum", [P, 8, HALF], F32))
        make_ident(nc, ident, ctx.enter_context(nc.semaphore("ident_done")))
        ffn_phase(nc, "f1", w["ffn1_norm"][0], w["ffn1_w_gate"][0], w["ffn1_w_up"][0], w["ffn1_w_down"][0], rows, ident, psum, x=w["x"][0])
        with ExitStack() as outer:
            u = outer.enter_context(nc.sbuf_tensor("u", [P, GROUPS, T, SG], F32))
            with ExitStack() as inner:
                C_mat = [inner.enter_context(nc.sbuf_tensor(f"C_mat{c}", [P, GROUPS, T, SG], F32)) for c in range(2)]
                nT_hi, nT_lo = (inner.enter_context(nc.sbuf_tensor(n, [P, KT, SEQ], F32R)) for n in ("nT_hi", "nT_lo"))
                project_phase(nc, w, rows, ident, psum, nT_hi, nT_lo, u, kept, latent_rows, trig_rows)
                ssm_phase(nc, w, rows, rows_at, ident, psum, nT_hi, nT_lo, u, gates, C_mat)
            glu_phase(nc, w, rows, ident, psum, u, gates, partial, kept)
        with ExitStack() as outer:
            aT_hi, aT_lo = (outer.enter_context(nc.sbuf_tensor(n, [P, HEADS // 2, SEQ], F32R)) for n in ("aT_hi", "aT_lo"))
            attention_phase(nc, w, ident, psum, latent_rows, trig_rows, aT_hi, aT_lo)
            merge_phase(nc, w, psum, rows, aT_hi, aT_lo, gates, partial)
        ffn_phase(nc, "f2", w["ffn2_norm"][0], w["ffn2_w_gate"][0], w["ffn2_w_up"][0], w["ffn2_w_down"][0], rows, ident, psum,
                  finish=(w["final_norm"], out[0]))


INPUTS = ["x", "positions", "ffn1_norm", "ffn1_w_gate", "ffn1_w_up", "ffn1_w_down", "mix_norm", "w_in", "q_norm", "w_uq", "kv_norm",
          "w_ukv", "w_o_attn", "ssm_lambda_re", "ssm_lambda_im", "ssm_log_dt", "ssm_b_re", "ssm_b_im", "ssm_c_re", "ssm_c_im",
          "ssm_d", "w_glu", "b_glu", "w_o_ssm", "w_out", "ffn2_norm", "ffn2_w_gate", "ffn2_w_up", "ffn2_w_down", "final_norm"]


def rope_const():
    half, at = ROPE // 2, P - 2 * ROPE
    freq = (np.float32(10000.0) ** (-np.arange(0, ROPE, 2, dtype=np.float32) / np.float32(ROPE))).astype(np.float32)
    const = np.zeros((P, 4), np.float32)
    const[:, 0] = np.tile(freq, P // half)
    const[P - ROPE:P - half, 0] = -freq
    const[:, 1] = 1 / (2 * math.pi)
    const[at:at + ROPE, 2] = 0.25
    const[at:at + ROPE, 3] = math.pi / 2
    return const


def kernel(**inputs):
    import concourse.bacc as bacc
    from concourse.bass_utils import run_bass_kernel_spmd

    nc = bacc.Bacc("TRN2", target_bir_lowering=False, num_devices=1)
    arrays = {name: np.ascontiguousarray(inputs[name]) for name in INPUTS}
    arrays["rope_const"] = rope_const()
    w = {name: nc.dram_tensor(name, a.shape, mybir.dt.from_np(a.dtype), kind="ExternalInput").ap() for name, a in arrays.items()}
    out = nc.dram_tensor("out", (1, SEQ, D), F32, kind="ExternalOutput").ap()
    build(nc, w, out)
    r = run_bass_kernel_spmd(nc, [arrays], core_ids=[0])
    return r.results[0]["out"]
```
